# Optimizing a Trainium2 kernel written in Bass

```python
import jax, jax.numpy as jnp
from jax import lax
import numpy as np

D_MODEL = 1024
BATCH = 1
SEQ = 256
DEPTH = 1

CHUNK = 64
N_MEM = 256
BRANCH_WIDTH = 512
N_BRANCH = 3
HEAD_DIM = 64
FOX_HEADS = BRANCH_WIDTH // HEAD_DIM
CONV_K = 3
CONV_GROUPS = 8
XA_HEADS = 4
XA_HEAD_DIM = BRANCH_WIDTH // XA_HEADS
Q_BLOCK = 128
N_EXPERTS = 32
TOP_K = 4
D_FF = D_MODEL
SWIGLU_ALPHA = 1.702
SWIGLU_LIMIT = 7.0
NORM_EPS = 1e-5
QK_EPS = 1e-6
PROJ_SPLITS = (BRANCH_WIDTH, BRANCH_WIDTH, BRANCH_WIDTH, FOX_HEADS,
               BRANCH_WIDTH, BRANCH_WIDTH, BRANCH_WIDTH, BRANCH_WIDTH, N_BRANCH * D_MODEL)
PROJ_COLS = 7 * BRANCH_WIDTH + FOX_HEADS + N_BRANCH * D_MODEL

kernel_name = 'hybrid_fox_shortconv_memxattn_moe'

def rms_norm(x, g, eps):
    xf = x.astype(jnp.float32)
    y = xf * lax.rsqrt(jnp.mean(xf * xf, axis=-1, keepdims=True) + eps)
    return (y * g.astype(jnp.float32)).astype(x.dtype)

def forgetting_attention(q, k, v, log_f):
    S = q.shape[1]
    Dh = q.shape[-1]
    scale = Dh ** -0.5
    cum = jnp.cumsum(log_f, axis=1).transpose(0, 2, 1)
    outs = []
    for i in range(S // Q_BLOCK):
        q0 = i * Q_BLOCK
        kend = q0 + Q_BLOCK
        qb = q[:, q0:kend]
        kb = k[:, :kend]
        vb = v[:, :kend]
        s = jnp.einsum('bqhd,bkhd->bhqk', qb, kb, preferred_element_type=jnp.float32) * scale
        bias = cum[:, :, q0:kend, None] - cum[:, :, None, :kend]
        t_idx = q0 + jnp.arange(Q_BLOCK)[:, None]
        s_idx = jnp.arange(kend)[None, :]
        s = jnp.where(s_idx <= t_idx, s + bias, -jnp.inf)
        p = jax.nn.softmax(s, axis=-1).astype(vb.dtype)
        outs.append(jnp.einsum('bhqk,bkhd->bqhd', p, vb))
    return jnp.concatenate(outs, axis=1)

def causal_short_conv(u, w):
    S = u.shape[1]
    up = jnp.pad(u, ((0, 0), (CONV_K - 1, 0), (0, 0)))
    y = up[:, 0:S] * w[0]
    for j in range(1, CONV_K):
        y = y + up[:, j:j + S] * w[j]
    return y

def memory_cross_attention(q, mk, mv):
    scale = q.shape[-1] ** -0.5
    s = jnp.einsum('bshd,bmhd->bhsm', q, mk, preferred_element_type=jnp.float32) * scale
    p = jax.nn.softmax(s, axis=-1).astype(mv.dtype)
    return jnp.einsum('bhsm,bmhd->bshd', p, mv)

def clamped_swiglu(h):
    glu, lin = h[..., :D_FF], h[..., D_FF:]
    glu = jnp.minimum(glu, SWIGLU_LIMIT)
    lin = jnp.clip(lin, -SWIGLU_LIMIT, SWIGLU_LIMIT)
    return glu * jax.nn.sigmoid(SWIGLU_ALPHA * glu) * (lin + 1.0)

def moe(x2, w_router, b_router, w_up, b_up, w_down, b_down):
    logits = (x2 @ w_router + b_router).astype(jnp.float32)
    top_vals, top_idx = lax.top_k(logits, TOP_K)
    top_w = jax.nn.softmax(top_vals, axis=-1)
    combine = jnp.einsum('tk,tke->te', top_w,
                         jax.nn.one_hot(top_idx, N_EXPERTS, dtype=jnp.float32)).astype(x2.dtype)
    out = jnp.zeros_like(x2)
    for e in range(N_EXPERTS):
        a = clamped_swiglu(x2 @ w_up[e] + b_up[e])
        out = out + combine[:, e:e + 1] * (a @ w_down[e] + b_down[e])
    return out

def hybrid_layer(x, mem, norm1_g, w_in, b_forget, b_gate, fox_q_g, fox_k_g, conv_w,
                 mem_norm_g, w_mem_kv, xa_q_g, xa_k_g, w_branch, w_out, norm2_g,
                 w_router, b_router, w_up, b_up, w_down, b_down):
    B, S, D = x.shape
    M = mem.shape[1]
    h = rms_norm(x, norm1_g, NORM_EPS)
    p = h @ w_in
    idx = [int(v) for v in np.cumsum(PROJ_SPLITS)[:-1]]
    fq, fk, fv, f_logit, cu, cc, cb, xq, g_logit = jnp.split(p, idx, axis=-1)

    q = rms_norm(fq.reshape(B, S, FOX_HEADS, HEAD_DIM), fox_q_g, QK_EPS)
    k = rms_norm(fk.reshape(B, S, FOX_HEADS, HEAD_DIM), fox_k_g, QK_EPS)
    v = fv.reshape(B, S, FOX_HEADS, HEAD_DIM)
    log_f = jax.nn.log_sigmoid(f_logit.astype(jnp.float32) + b_forget.astype(jnp.float32))
    y_fox = forgetting_attention(q, k, v, log_f).reshape(B, S, BRANCH_WIDTH)

    y_conv = cb * causal_short_conv(cc * cu, conv_w)

    mn = rms_norm(mem, mem_norm_g, NORM_EPS)
    mk, mv = jnp.split(mn @ w_mem_kv, 2, axis=-1)
    mk = rms_norm(mk.reshape(B, M, XA_HEADS, XA_HEAD_DIM), xa_k_g, QK_EPS)
    mv = mv.reshape(B, M, XA_HEADS, XA_HEAD_DIM)
    xq = rms_norm(xq.reshape(B, S, XA_HEADS, XA_HEAD_DIM), xa_q_g, QK_EPS)
    y_mem = memory_cross_attention(xq, mk, mv).reshape(B, S, BRANCH_WIDTH)

    branches = jnp.stack([y_fox, y_conv, y_mem], axis=2)
    proj = jnp.einsum('bsnc,ncd->bsnd', branches, w_branch)
    gates = jax.nn.sigmoid(g_logit.reshape(B, S, N_BRANCH, D) + b_gate)
    merged = jnp.sum(gates * proj, axis=2)
    x1 = x + merged @ w_out

    h2 = rms_norm(x1, norm2_g, NORM_EPS).reshape(B * S, D)
    y = moe(h2, w_router, b_router, w_up, b_up, w_down, b_down).reshape(B, S, D)
    return x1 + y

def setup_inputs(seed: int = 0) -> dict:
    key = jax.random.key(seed)
    ks = jax.random.split(key, 24)
    L = DEPTH
    f32 = jnp.float32

    def nrm(k, shape, scale):
        return jax.random.normal(k, shape, f32) * scale

    return {
        'x': nrm(ks[0], (BATCH, SEQ, D_MODEL), 1.0),
        'mem': nrm(ks[1], (BATCH, N_MEM, D_MODEL), 1.0),
        'norm1_g': 1.0 + nrm(ks[2], (L, D_MODEL), 0.02),
        'w_in': nrm(ks[3], (L, D_MODEL, PROJ_COLS), D_MODEL ** -0.5),
        'b_forget': 3.0 + nrm(ks[4], (L, FOX_HEADS), 0.5),
        'b_gate': nrm(ks[5], (L, N_BRANCH, D_MODEL), 0.1),
        'fox_q_g': 1.0 + nrm(ks[6], (L, HEAD_DIM), 0.02),
        'fox_k_g': 1.0 + nrm(ks[7], (L, HEAD_DIM), 0.02),
        'conv_w': nrm(ks[8], (L, CONV_K, BRANCH_WIDTH), CONV_K ** -0.5),
        'mem_norm_g': 1.0 + nrm(ks[9], (L, D_MODEL), 0.02),
        'w_mem_kv': nrm(ks[10], (L, D_MODEL, 2 * BRANCH_WIDTH), D_MODEL ** -0.5),
        'xa_q_g': 1.0 + nrm(ks[11], (L, XA_HEAD_DIM), 0.02),
        'xa_k_g': 1.0 + nrm(ks[12], (L, XA_HEAD_DIM), 0.02),
        'w_branch': nrm(ks[13], (L, N_BRANCH, BRANCH_WIDTH, D_MODEL), BRANCH_WIDTH ** -0.5),
        'w_out': nrm(ks[14], (L, D_MODEL, D_MODEL), D_MODEL ** -0.5),
        'norm2_g': 1.0 + nrm(ks[15], (L, D_MODEL), 0.02),
        'w_router': nrm(ks[16], (L, D_MODEL, N_EXPERTS), D_MODEL ** -0.5),
        'b_router': nrm(ks[17], (L, N_EXPERTS), 0.01),
        'w_up': nrm(ks[18], (L, N_EXPERTS, D_MODEL, 2 * D_FF), D_MODEL ** -0.5),
        'b_up': nrm(ks[19], (L, N_EXPERTS, 2 * D_FF), 0.01),
        'w_down': nrm(ks[20], (L, N_EXPERTS, D_FF, D_MODEL), D_FF ** -0.5),
        'b_down': nrm(ks[21], (L, N_EXPERTS, D_MODEL), 0.01),
    }

def reference(x, mem, norm1_g, w_in, b_forget, b_gate, fox_q_g, fox_k_g, conv_w,
              mem_norm_g, w_mem_kv, xa_q_g, xa_k_g, w_branch, w_out, norm2_g,
              w_router, b_router, w_up, b_up, w_down, b_down):
    for l in range(DEPTH):
        x = hybrid_layer(x, mem, norm1_g[l], w_in[l], b_forget[l], b_gate[l], fox_q_g[l],
                         fox_k_g[l], conv_w[l], mem_norm_g[l], w_mem_kv[l], xa_q_g[l],
                         xa_k_g[l], w_branch[l], w_out[l], norm2_g[l], w_router[l],
                         b_router[l], w_up[l], b_up[l], w_down[l], b_down[l])
    return x


_drawn_inputs = setup_inputs


def setup_inputs(seed=0):
    import zlib

    import numpy as np

    out = dict(_drawn_inputs(seed))
    spreads = {}
    factors = {'fox_q_g': 3.649,
     'fox_k_g': 14.236,
     'mem_norm_g': 4.431,
     'xa_q_g': 6.778,
     'xa_k_g': 5.674,
     'b_router': 9.037,
     'b_up': 24.32,
     'b_down': 28.024,
     'norm2_g': 3.4}
    for name, (base, spread) in spreads.items():
        noise = np.random.default_rng([zlib.crc32(name.encode()), seed]).standard_normal(out[name].shape)
        drawn = base * np.exp(spread * noise) if base else spread * noise
        out[name] = __import__('jax').numpy.asarray(drawn.astype(out[name].dtype))
    for name, factor in factors.items():
        out[name] = (out[name] * factor).astype(out[name].dtype)
    return out
```

```python
from contextlib import ExitStack

import concourse.bass as bass
from concourse import mybir

F32 = mybir.dt.float32
F32R = mybir.dt.float32r
BF16 = mybir.dt.bfloat16
I32 = mybir.dt.int32
U32 = mybir.dt.uint32
ALU = mybir.AluOpType
ACT = mybir.ActivationFunctionType
AX = mybir.AxisListType.X

P = 128
SEQ = 256
NT = SEQ // P
D = 1024
KD = D // P
W = 512
KB = W // P
FOX_H, FOX_D = 8, 64
MEM_H, MEM_D = 4, 128
NEXP, TOPK, FF = 32, 4, 1024
NORM_EPS, QK_EPS = 1e-5, 1e-6
ALPHA, LIMIT = 1.702, 7.0
SLOTS = 64
EXTRA = (SEQ * TOPK - 1) // SLOTS
EXTRA_COLS = EXTRA + 1
TABLE = NEXP + EXTRA_COLS + 4
NEG = -1.0e30

C_G1, C_GM, C_G2, C_CONV = 0, 8, 16, 24
C_XQ, C_XK, C_FQ, C_FK = 36, 37, 38, 39
NCOLS = 40

R_NEG, R_POS, R_END = 64, 96, 104


def blocks_and_pieces():
    blocks = [("q",), ("k",), ("v",), ("mk",), ("mv",), ("xq",), ("cu",), ("cc",), ("cb",)]
    for branch in (1, 2, 0):
        for half in range(2):
            blocks += [("gate", branch, half), ("proj", branch, half)]
    pieces = []
    for b in blocks:
        pieces += [(b, 0)] if b[0] == "proj" else [(b, 0), (b, 1)]
    blocks += [("out", 0), ("out", 1)]
    pieces += [(("out", 0), 0), (("out", 1), 0), (("out", 0), 1), (("out", 1), 1)]
    return blocks, pieces


BLOCKS, PIECES = blocks_and_pieces()
NP = len(PIECES)
BLOCK_NO = {b: n for n, b in enumerate(BLOCKS)}
LAST_PIECE = {}
for _p, (_b, _h) in enumerate(PIECES):
    LAST_PIECE[_b] = _p


def auxiliary_jobs():
    jobs = [(-1, "hT", g) for g in range(4)]
    jobs += [(0, "logit_f", 0)]
    jobs += [(1, "mT", g) for g in range(4)]
    jobs += [(2, "cum", 0)]
    jobs += [(3, "qT", g) for g in range(4)]
    jobs += [(5, "kT", g) for g in range(4)]
    jobs += [(6 + h, "fox_s", h) for h in range(FOX_H)]
    jobs += [(7 + h, "fox_pT", h) for h in range(FOX_H)]
    jobs += [(8 + h, "fox_y", h) for h in range(FOX_H)]
    jobs += [(9, "mkT", g) for g in range(2)]
    jobs += [(13, "xqT", g) for g in range(2)]
    jobs += [(14 + h, "mem_s", h) for h in range(MEM_H)]
    jobs += [(15 + h, "mem_pT", h) for h in range(MEM_H)]
    jobs += [(16 + h, "mem_y", h) for h in range(MEM_H)]
    jobs += [(33, "zT", g) for g in range(2)]
    jobs += [(36, "zT", g) for g in range(2, 4)]
    return sorted(jobs, key=lambda j: j[0])


JOBS = auxiliary_jobs()
JOB = {(kind, arg): n for n, (_, kind, arg) in enumerate(JOBS)}
SPLIT_JOBS = [n for n, (_, kind, _) in enumerate(JOBS) if kind in ("hT", "mT", "fox_y", "mem_y", "zT")]
SPLIT_NO = {n: i for i, n in enumerate(SPLIT_JOBS)}
SMAX = [("fox", h) for h in range(FOX_H)] + [("mem", h) for h in range(MEM_H)]
SMAX_NO = {x: n for n, x in enumerate(SMAX)}


BYTES = {F32: 4, F32R: 4, BF16: 2, I32: 4, U32: 4}


class Region:

    def __init__(self, nc, start, end):
        self.nc, self.at, self.end = nc, start, end

    def place(self, name, shape, dt):
        size = BYTES[dt]
        for n in shape[1:]:
            size *= n
        tile = self.nc.alloc_sbuf_tensor_at(name, shape, dt, offset=self.at)
        self.at += -(-size // 32) * 32
        assert self.at <= self.end, (name, self.at, self.end)
        return tile


def jobs_at(step):
    return [(n, kind, arg) for n, (s, kind, arg) in enumerate(JOBS) if s == step]


def hybrid_block(nc, x_d, mem_d, w_in, w_kv, w_branch, w_out, w_up, w_down,
                 cols_d, spread_d, wf_d, wr_d, b_gate, b_up, b_down, out):
    ctx = ExitStack()
    with ctx:
        def sb(name, shape, dt, where=None):
            return (where or always).place(name, shape, dt)

        def sem(name):
            return ctx.enter_context(nc.semaphore(name))

        base, top = -(-nc.sbuf_base // 32) * 32, nc.sbuf_base + nc.sbuf_bytes_remaining
        up_bytes = KD * 2 * FF * 4
        raw_bytes = 4 * KB * W * 4
        always = Region(nc, base, top)
        ident = sb("ident", [P, P], F32)
        x1 = sb("x1", [P, NT, D], F32)
        cols = sb("cols", [P, NCOLS], F32)
        qcols = sb("qcols", [P, 2], F32)
        spread = sb("spread", [P, 40], F32)
        iota = sb("iota", [P, SLOTS], F32)
        ss = sb("ss", [P, 7, 16], F32)
        ms = sb("ms", [P, 7, 16], F32)
        rstd = sb("rstd", [P, 7, 16], F32)
        minus_half = sb("minus_half", [P, 16], F32)
        bias_up = sb("bias_up", [96, 2 * FF], BF16)
        bias_down = sb("bias_down", [96, D], BF16)
        ident_rep = sb("ident_rep", [96, NEXP], BF16)
        tri_strict = sb("tri_strict", [P, P], BF16)
        block_tri = sb("block_tri", [96, 96], BF16)
        ones_bf = sb("ones_bf", [P, P], BF16)
        ones_f = sb("ones_f", [32, P], F32)
        iota_e = sb("iota_e", [32, 2], F32)

        start_u = always.at
        u = Region(nc, start_u, start_u + up_bytes)
        mT_hi = sb("mT_hi", [P, KD, SEQ], F32R, u)
        mT_lo = sb("mT_lo", [P, KD, SEQ], F32R, u)
        q_rows = sb("q_rows", [P, FOX_H, SEQ], F32, u)
        k_rows = sb("k_rows", [P, FOX_H, SEQ], F32, u)
        tok = sb("tok", [P, 2, NT, W], F32, u)
        xqT = sb("xqT", [P, MEM_H, SEQ], F32, u)
        mkT = sb("mkT", [P, MEM_H, SEQ], F32, u)
        v_tok = sb("v_tok", [P, NT, W], F32, u)
        mv_tok = sb("mv_tok", [P, NT, W], F32, u)
        score = sb("score", [P, 2, W], F32, u)
        pT = sb("pT", [P, 2, W], F32, u)
        v = Region(nc, start_u, start_u + 2 * KD * SEQ * 4)
        conv_cu = sb("conv_cu", [P, KB, SEQ], F32, v)
        conv_out = sb("conv_out", [P, KB, SEQ], F32, v)
        conv_u = sb("conv_u", [P, KB, SEQ + 2], F32, v)
        u2 = Region(nc, start_u, start_u + up_bytes)
        w_up_ring = sb("w_up_ring", [P, KD, 2 * FF], F32, u2)
        start_d = u2.at
        raw = sb("raw", [P, 4, KB, W], F32, Region(nc, start_d, start_d + raw_bytes))
        w_down_ring = raw[:].rearrange("p a b n -> p (a b n)").rearrange("p (k n) -> p k n", n=D)

        start_r = start_d + raw_bytes
        r = Region(nc, start_r, top)
        w_hi = sb("w_hi", [P, 4, 2, W], F32R, r)
        w_lo = sb("w_lo", [P, 4, 2, W], F32R, r)
        hT_hi = sb("hT_hi", [P, KD, SEQ], F32R, r)
        hT_lo = sb("hT_lo", [P, KD, SEQ], F32R, r)
        start_y = r.at
        y_conv_hi = sb("y_conv_hi", [P, KB, SEQ], F32R, r)
        y_conv_lo = sb("y_conv_lo", [P, KB, SEQ], F32R, r)
        end_y = r.at
        yT_hi = [sb("y_fox_hi", [P, KB, SEQ], F32R, r), y_conv_hi, sb("y_mem_hi", [P, KB, SEQ], F32R, r)]
        yT_lo = [sb("y_fox_lo", [P, KB, SEQ], F32R, r), y_conv_lo, sb("y_mem_lo", [P, KB, SEQ], F32R, r)]
        y = Region(nc, start_y, end_y)
        mask = sb("mask", [P, 3 * P], F32, y)
        tri_ones = sb("tri_ones", [P, SEQ], F32, y)
        head_hot = sb("head_hot", [P, FOX_H], F32, y)
        cum = sb("cum", [P, SEQ], F32, y)
        f_cols = sb("f_cols", [P, NT, R_END], F32, y)
        f_tmp = sb("f_tmp", [P, 4, NT, FOX_H], F32, y)
        wf = sb("wf", [P, KD, FOX_H], F32, y)
        wf_hi = sb("wf_hi", [P, KD, FOX_H], F32R, y)
        wf_lo = sb("wf_lo", [P, KD, FOX_H], F32R, y)
        merged = sb("merged", [P, NT, D], F32, r)
        gate = sb("gate", [P, NT, W], F32, r)
        prob = sb("prob", [P, 2, W], F32, r)
        nmax = sb("nmax", [P, 2, 2], F32, r)
        den = sb("den", [P, 2, 2], F32, r)
        rden = sb("rden", [P, 2, 2], F32, r)
        gate_sel = sb("gate_sel", [96, 3, P], BF16, r)
        bias_gate = sb("bias_gate", [96, D], BF16, r)
        b_raw = sb("b_raw", [96, W], F32, r)
        b_mid = sb("b_mid", [96, W], BF16, r)
        print("left in phase 1:", top - r.at)
        m = Region(nc, start_r, top)
        xs = merged
        m_parts = sb("h_parts", [P, 3, NT, D], BF16, m)
        x1s = sb("x1s", [P, NT, D], F32, m)
        x1r = sb("x1r", [P, NT, D], F32, m)
        h2T = sb("h2T", [P, KD, SEQ], F32, m)
        xgT = sb("xgT", [P, KD, SLOTS], F32, m)
        glu = sb("glu", [P, W], F32, m)
        lin = sb("lin", [P, W], F32, m)
        glin = sb("glin", [P, W], F32, m)
        sig = sb("sig", [P, W], F32, m)
        a_tok = sb("a_tok", [P, W], F32, m)
        aT = sb("aT", [P, KB, P], F32, m)
        y_sb = sb("y_sb", [P, W], F32, m)
        pick = sb("pick", [P, NT, SLOTS], BF16, m)
        pick_w = sb("pick_w", [P, NT, 2, SLOTS], F32, m)
        pick_wT = sb("pick_wT", [P, NT, P], F32, m)
        bias_sel = sb("bias_sel", [96, SLOTS], BF16, m)
        pos_tab = sb("pos_tab", [P, NT, TABLE], F32, m)
        comb_tab = sb("comb_tab", [P, NT, TABLE], F32, m)
        exp_sel = sb("exp_sel", [96, TABLE], F32, m)
        logits = sb("logits", [P, NT, NEXP], F32, m)
        top_v = sb("top_v", [P, NT, 8], F32, m)
        top_i = sb("top_i", [P, NT, 8], U32, m)
        top_f = sb("top_f", [P, NT, 8], F32, m)
        top_e = sb("top_e", [P, NT, TOPK], F32, m)
        top_den = sb("top_den", [P, NT, 2], F32, m)
        ntop = sb("ntop", [P, NT], F32, m)
        hot4 = sb("hot4", [P, NT, TOPK, NEXP], F32, m)
        hot4w = sb("hot4w", [P, NT, TOPK, NEXP], F32, m)
        chosen = sb("chosen", [P, NT, NEXP], F32, m)
        chosen3 = sb("chosen3", [P, NT, 3, NEXP], BF16, m)
        count = sb("count", [96, 4], F32, m)
        extra = sb("extra", [96, 2], F32, m)
        extra_bf = sb("extra_bf", [96, 2], BF16, m)
        first = sb("first", [96, 2], F32, m)
        xt = sb("xt", [96, 3, EXTRA_COLS], F32, m)
        posT = sb("posT", [32, 2, NT, P], F32, m)
        wr = sb("wr", [P, KD, NEXP], F32, m)
        zeros_bf = sb("zeros_bf", [P, W], BF16, m)
        meta = sb("meta", [1, EXTRA_COLS + 1], I32, m)
        print("left in phase 2:", top - m.at)

        acc = [ctx.enter_context(nc.psum_tensor(f"acc{b}", [P, W], F32)) for b in range(4)]
        aux = [ctx.enter_context(nc.psum_tensor(f"aux{b}", [P, W], F32)) for b in range(4)]
        bank_glu, bank_lin, bank_cy, bank_t = aux

        x_loaded = [sem(f"x_loaded{t}") for t in range(NT)]
        mem_loaded = [sem(f"mem_loaded{t}") for t in range(NT)]
        params_loaded = sem("params_loaded")
        brow_loaded = sem("brow_loaded")
        brow_used = sem("brow_used")
        raw_loaded = [sem(f"raw_loaded{s}") for s in range(4)]
        const_built = sem("const_built")
        ss_ready = [sem(f"ss_ready{n}") for n in range(7)]
        rstd_ready = sem("rstd_ready")
        pool_step = sem("pool_step")
        xs_ready = sem("xs_ready")
        hi_done = sem("hi_done")
        lo_done = sem("lo_done")
        half_used = sem("half_used")
        wf_hi_done = sem("wf_hi_done")
        wf_lo_done = sem("wf_lo_done")
        block_free = [sem(f"block_free{s}") for s in range(2)]
        aux_ready = sem("aux_ready")
        aux_free = [sem(f"aux_free{b}") for b in range(4)]
        part_hi = sem("part_hi")
        squares = sem("squares")
        forget_neg = sem("forget_neg")
        forget_log = sem("forget_log")
        forget_ready = sem("forget_ready")
        rows_ready = sem("rows_ready")
        max_ready = sem("max_ready")
        exp_ready = sem("exp_ready")
        prob_ready = sem("prob_ready")
        conv_y = sem("conv_y")
        conv_hi = sem("conv_hi")
        merged_done = sem("merged_done")
        x1_ready = sem("x1_ready")
        act_step = sem("act_step")
        dve_step = sem("dve_step")
        wr_loaded = sem("wr_loaded")
        x1s_ready = sem("x1s_ready")
        x1sT_ready = sem("x1sT_ready")
        h2T_act = sem("h2T_act")
        h2T_dve = sem("h2T_dve")
        logits_ready = sem("logits_ready")
        parts_act = sem("parts_act")
        parts_pool = sem("parts_pool")
        top_ready = sem("top_ready")
        soft_ready = sem("soft_ready")
        chosen_ready = sem("chosen_ready")
        slots_ready = sem("slots_ready")
        extra_ready = sem("extra_ready")
        first_ready = sem("first_ready")
        table_ready = sem("table_ready")
        list_ready = sem("list_ready")
        xtab_ready = sem("xtab_ready")
        meta_ready = sem("meta_ready")
        up_loaded = [sem(f"up_loaded{k}") for k in range(KD)]
        up_used = [sem(f"up_used{k}") for k in range(KD)]
        down_loaded = [sem(f"down_loaded{m}") for m in range(4)]
        down_used = [sem(f"down_used{m}") for m in range(3)]
        pick_ready = sem("pick_ready")
        pick_w_ready = sem("pick_w_ready")
        bias_sel_ready = sem("bias_sel_ready")
        gathered = sem("gathered")
        xg_ready = sem("xg_ready")
        up_done = sem("up_done")
        up_read = sem("up_read")
        glu_ready = sem("glu_ready")
        glin_ready = sem("glin_ready")
        sig_ready = sem("sig_ready")
        a_ready = sem("a_ready")
        pick_wT_done = sem("pick_wT_done")
        pick_wT_ready = sem("pick_wT_ready")
        aT_done = sem("aT_done")
        aT_ready = sem("aT_ready")
        y_done = sem("y_done")
        y_ready = sem("y_ready")
        scattered = sem("scattered")
        out_ready = sem("out_ready")
        stored = sem("stored")

        def block_done(eng, b):
            eng.wait_ge(half_used, 2 * LAST_PIECE[b] + 2)

        def block_read(eng, b):
            eng.wait_ge(block_free[BLOCK_NO[b] % 2], BLOCK_NO[b] // 2 + 1)

        mem_sb = tok[:].rearrange("p a t n -> p (a t n)").rearrange("p (t n) -> p t n", t=NT)

        def piece_source(p):
            block, half = PIECES[p]
            kind = block[0]
            rows = slice(half * KB * P, (half + 1) * KB * P)
            if kind in ("mk", "mv"):
                c = {"mk": 0, "mv": W}[kind]
                src = w_kv[rows, c:c + W]
            elif kind == "gate":
                c = 7 * W + FOX_H + block[1] * D + block[2] * W
                src = w_in[rows, c:c + W]
            elif kind == "proj":
                src = w_branch[block[1], :, block[2] * W:(block[2] + 1) * W]
            elif kind == "out":
                src = w_out[rows, block[1] * W:(block[1] + 1) * W]
            else:
                c = {"q": 0, "k": W, "v": 2 * W, "cu": 3 * W + FOX_H, "cc": 4 * W + FOX_H,
                     "cb": 5 * W + FOX_H, "xq": 6 * W + FOX_H}[kind]
                src = w_in[rows, c:c + W]
            return src.rearrange("(k p) n -> p k n", p=P)

        bias_chunks = [(b_up, bias_up, c) for c in range(4)] + [(b_down, bias_down, c) for c in range(2)]
        bias_chunks = [(b_gate, bias_gate, c) for c in range(2)] + bias_chunks

        block = ctx.enter_context(nc.Block())

        @block.sync
        def _(sp):
            def load_piece(p):
                if p >= 4:
                    sp.wait_ge(lo_done, 2 * (p - 4) + 2)
                sp.dma_start(raw[:, p % 4], piece_source(p)).then_inc(raw_loaded[p % 4], 16)

            for t in range(NT):
                sp.dma_start(x1[:, t], x_d[t * P:(t + 1) * P, :]).then_inc(x_loaded[t], 16)
            load_piece(0)
            for t in range(NT):
                sp.dma_start(mem_sb[:, t], mem_d[t * P:(t + 1) * P, :]).then_inc(mem_loaded[t], 16)
            for p in range(1, NP):
                load_piece(p)
                if 27 <= p < 27 + KD:
                    if p == 27:
                        sp.wait_ge(aux_ready, JOB["mem_y", MEM_H - 1] + 1)
                        block_read(sp, ("cb",))
                        sp.wait_ge(rows_ready, 1)
                    k = p - 27
                    sp.dma_start(w_up_ring[:, k], w_up[0, k * P:(k + 1) * P, :]).then_inc(up_loaded[k], 16)
            sp.wait_ge(lo_done, 2 * NP)
            for m in range(4):
                sp.dma_start(w_down_ring[:, 2 * m:2 * m + 2],
                             w_down[0, 2 * m * P:(2 * m + 2) * P, :].rearrange("(k p) n -> p k n", p=P)
                             ).then_inc(down_loaded[m], 16)

            def load_item(expert, before):
                for k in range(KD):
                    sp.wait_ge(up_used[k], before)
                    sp.dma_start(w_up_ring[:, k],
                                 w_up[bass.ds(expert, 1), k * P:(k + 1) * P, :].rearrange("o p n -> p (o n)")
                                 ).then_inc(up_loaded[k], 16)
                for m in range(4):
                    sp.wait_ge(down_used[m] if m < 3 else y_done, before)
                    sp.dma_start(w_down_ring[:, 2 * m:2 * m + 2],
                                 w_down[bass.ds(expert, 1), 2 * m * P:(2 * m + 2) * P, :]
                                 .rearrange("o (k p) n -> p (o k) n", p=P)).then_inc(down_loaded[m], 16)

            with sp.Fori(2, NEXP + 1) as n:
                before = sp.snap(sp.to_reg(n - 1), min_val=1, max_val=NEXP - 1)
                load_item(before, before)
            sp.wait_ge(meta_ready, 1)
            more = sp.value_load(meta[0:1, EXTRA_COLS:EXTRA_COLS + 1], min_val=0, max_val=EXTRA)
            with sp.If(more > 0):
                with sp.Fori(NEXP + 1, NEXP + 1 + more) as n:
                    expert = sp.value_load(meta[0:1, bass.ds(n - (NEXP + 1), 1)], min_val=0, max_val=NEXP - 1)
                    before = sp.snap(sp.to_reg(n - 1), min_val=NEXP, max_val=NEXP + EXTRA)
                    load_item(expert, before)
            for t in range(NT):
                for h in range(2):
                    sp.wait_ge(out_ready, 2 * t + h + 1)
                    sp.dma_start(out[t * P:(t + 1) * P, h * W:(h + 1) * W],
                                 x1[:, t, h * W:(h + 1) * W]).then_inc(stored, 16)
            sp.wait_ge(stored, 16 * 2 * NT)

        @block.gpsimd
        def _(pool):
            steps = [0]

            def chained(ins):
                steps[0] += 1
                ins.then_inc(pool_step, 1)
                pool.wait_ge(pool_step, steps[0])

            consts = [0]

            def constant(ins):
                consts[0] += 1
                ins.then_inc(const_built, 1)
                pool.wait_ge(const_built, consts[0])

            chained(nc.gpsimd.memset(minus_half[:], -0.5))
            chained(nc.gpsimd.memset(ident[:], 0.0))
            constant(nc.gpsimd.affine_select(out=ident[:], in_=ident[:], compare_op=ALU.not_equal, fill=1.0,
                                             base=0, pattern=[[-1, P]], channel_multiplier=1))

            def rstd_of(n, width, count, eps):
                pool.wait_ge(ss_ready[n], 1)
                chained(nc.gpsimd.tensor_scalar(ms[:, n, 0:count], ss[:, n, 0:count], 1.0 / width, eps,
                                                ALU.mult, ALU.add))
                nc.gpsimd.tensor_tensor(rstd[:, n, 0:count], ms[:, n, 0:count], minus_half[:, 0:count],
                                        ALU.pow).then_inc(rstd_ready, 1)
                pool.wait_ge(rstd_ready, n + 1)

            rstd_of(0, D, 2, NORM_EPS)
            rstd_of(1, D, 2, NORM_EPS)
            chained(nc.gpsimd.memset(tri_ones[:], 1.0))
            constant(nc.gpsimd.affine_select(out=tri_ones[:], in_=tri_ones[:], compare_op=ALU.is_ge, fill=0.0,
                                             base=0, pattern=[[1, SEQ]], channel_multiplier=-1))
            chained(nc.gpsimd.memset(f_cols[:], 0.0))
            pool.wait_ge(params_loaded, 16 * 3)
            constant(nc.gpsimd.tensor_scalar(qcols[:, 0:1], cols[:, C_FQ:C_FQ + 1], FOX_D ** -0.5, None, ALU.mult))
            constant(nc.gpsimd.tensor_scalar(qcols[:, 1:2], cols[:, C_XQ:C_XQ + 1], MEM_D ** -0.5, None, ALU.mult))
            rstd_of(2, FOX_D, 16, QK_EPS)
            chained(nc.gpsimd.memset(q_rows[64:P], 0.0))
            chained(nc.gpsimd.memset(k_rows[64:P], 0.0))
            chained(nc.gpsimd.memset(head_hot[:], 0.0))
            chained(nc.gpsimd.memset(k_rows[R_POS:R_END], 1.0))
            for row in (R_NEG, R_POS):
                hot = head_hot[row:row + FOX_H]
                chained(nc.gpsimd.affine_select(out=hot, in_=hot, compare_op=ALU.not_equal, fill=1.0,
                                                base=0, pattern=[[-1, FOX_H]], channel_multiplier=1))
            chained(nc.gpsimd.tensor_copy(q_rows[R_NEG:R_NEG + FOX_H],
                                          head_hot[R_NEG:R_NEG + FOX_H].unsqueeze(2).to_broadcast([FOX_H, FOX_H, SEQ])))
            pool.wait_ge(aux_free[JOB["cum", 0] % 4], JOB["cum", 0] // 4 + 1)
            chained(nc.gpsimd.tensor_tensor(
                q_rows[R_POS:R_END], cum[R_POS:R_END].unsqueeze(1).to_broadcast([FOX_H, FOX_H, SEQ]),
                head_hot[R_POS:R_END].unsqueeze(2).to_broadcast([FOX_H, FOX_H, SEQ]), ALU.mult))
            nc.gpsimd.tensor_copy(k_rows[R_NEG:R_NEG + FOX_H],
                                  cum[R_NEG:R_NEG + FOX_H].unsqueeze(1).to_broadcast([FOX_H, FOX_H, SEQ])
                                  ).then_inc(rows_ready, 1)
            pool.wait_ge(rows_ready, 1)
            rstd_of(3, FOX_D, 16, QK_EPS)
            chained(nc.gpsimd.memset(mask[:], 0.0))
            for c in (0, 2 * P):
                constant(nc.gpsimd.affine_select(out=mask[:, c:c + P], in_=mask[:, c:c + P], compare_op=ALU.is_ge,
                                                 fill=NEG, base=0, pattern=[[-1, P]], channel_multiplier=1))
            assert consts[0] == 6
            chained(nc.gpsimd.memset(ones_bf[:], 1.0))
            chained(nc.gpsimd.memset(ident_rep[:], 0.0))
            for g in range(3):
                rep = ident_rep[32 * g:32 * g + 32]
                chained(nc.gpsimd.affine_select(out=rep, in_=rep, compare_op=ALU.not_equal, fill=1.0,
                                                base=0, pattern=[[-1, NEXP]], channel_multiplier=1))
            constant(nc.gpsimd.tensor_copy(gate_sel[:], ident_rep[:, 0:3].unsqueeze(2).to_broadcast([96, 3, P])))

            for n, (src, dst, c) in enumerate(bias_chunks):
                if n == 2:
                    rstd_of(4, MEM_D, 8, QK_EPS)
                if n == 4:
                    rstd_of(5, MEM_D, 8, QK_EPS)
                pool.wait_ge(brow_loaded, 16 * 3 * (n + 1))
                part = dst[:, c * W:(c + 1) * W]
                chained(nc.gpsimd.tensor_copy(part, b_raw[:]))
                chained(nc.gpsimd.tensor_tensor(b_raw[:], b_raw[:], part, ALU.subtract))
                chained(nc.gpsimd.tensor_copy(b_mid[:], b_raw[:]))
                chained(nc.gpsimd.tensor_copy(part[32:64], b_mid[32:64]))
                nc.gpsimd.tensor_tensor(part[64:96], b_raw[64:96], b_mid[64:96],
                                        ALU.subtract).then_inc(brow_used, 1)
                pool.wait_ge(brow_used, n + 1)
            chained(nc.gpsimd.memset(tri_strict[:], 1.0))
            chained(nc.gpsimd.memset(block_tri[:], 0.0))
            constant(nc.gpsimd.affine_select(out=tri_strict[:], in_=tri_strict[:], compare_op=ALU.is_ge, fill=0.0,
                                             base=-1, pattern=[[1, P]], channel_multiplier=-1))
            for g in range(3):
                s = slice(32 * g, 32 * g + 32)
                constant(nc.gpsimd.affine_select(out=block_tri[s, s], in_=ones_bf[s, 0:32], compare_op=ALU.is_ge,
                                                 fill=0.0, base=-1, pattern=[[1, 32]], channel_multiplier=-1))
            constant(nc.gpsimd.iota(iota[:], pattern=[[1, SLOTS]], base=0, channel_multiplier=0,
                                    allow_small_or_imprecise_dtypes=True))
            constant(nc.gpsimd.iota(iota_e[:], pattern=[[0, 2]], base=0, channel_multiplier=1,
                                    allow_small_or_imprecise_dtypes=True))
            constant(nc.gpsimd.memset(ones_f[:], 1.0))
            assert consts[0] == 14

            rstd_of(6, D, 2, NORM_EPS)
            chained(nc.gpsimd.memset(zeros_bf[:], 0.0))
            chained(nc.gpsimd.memset(pos_tab[:], -1.0))
            chained(nc.gpsimd.memset(comb_tab[:], 0.0))
            chained(nc.gpsimd.memset(exp_sel[:], 0.0))
            constant(nc.gpsimd.tensor_copy(exp_sel[:, 0:NEXP], ident_rep[:]))
            for t in range(NT):
                pool.wait_ge(parts_act, t + 1)
                nc.gpsimd.tensor_tensor(x1r[:, t], x1s[:, t], m_parts[:, 0, t], ALU.subtract).then_inc(parts_pool, 1)
                pool.wait_ge(parts_pool, t + 1)
            for t in range(NT):
                pool.wait_ge(parts_act, NT + t + 1)
                nc.gpsimd.tensor_tensor(m_parts[:, 2, t], x1r[:, t], m_parts[:, 1, t],
                                        ALU.subtract).then_inc(parts_pool, 1)
                pool.wait_ge(parts_pool, NT + t + 1)
            assert consts[0] == 15

        @block.scalar
        def _(act):
            act.dma_start(cols[:], cols_d).then_inc(params_loaded, 16)
            act.dma_start(spread[:], spread_d).then_inc(params_loaded, 16)
            act.dma_start(wf[:], wf_d).then_inc(params_loaded, 16)

            def bias_rows(n):
                src, _, c = bias_chunks[n]
                rows = src.shape[0]
                if n == 0:
                    act.wait_ge(act_step, 1)
                else:
                    act.wait_ge(brow_used, n)
                for g in range(3):
                    act.dma_start(b_raw[32 * g:32 * g + rows], src[:, c * W:(c + 1) * W]).then_inc(brow_loaded, 16)

            def split_hi(p):
                for h in range(2):
                    s = 2 * p + h
                    if h == 0:
                        act.wait_ge(raw_loaded[p % 4], 16 * (p // 4 + 1))
                    if s >= 4:
                        act.wait_ge(half_used, s - 3)
                    nc.scalar.activation(w_hi[:, s % 4], raw[:, p % 4, 2 * h:2 * h + 2], ACT.Copy).then_inc(hi_done, 1)

            scratch = [tile[:].rearrange("p t n -> p (t n)") for tile in (gate, prob)]
            for t in range(NT):
                act.wait_ge(x_loaded[t], 16)
                ins = nc.scalar.activation(xs[:, t], x1[:, t], ACT.Square, accum_out=ss[:, 0, t:t + 1])
            ins.then_inc(ss_ready[0], 1)
            act.wait_ge(params_loaded, 16 * 3)
            nc.scalar.activation(wf_hi[:], wf[:], ACT.Copy).then_inc(wf_hi_done, 1)
            split_hi(0)

            def finish_job(j, kind, arg):
                bank = aux[j % 4]
                free = aux_free[j % 4]
                if kind in ("hT", "mT"):
                    hi, g = (hT_hi, C_G1) if kind == "hT" else (mT_hi, C_GM)
                    act.wait_ge(aux_ready, j + 1)
                    for i in range(2):
                        k = 2 * arg + i
                        ins = nc.scalar.activation(hi[:, k], bank[:, i * SEQ:(i + 1) * SEQ], ACT.Copy,
                                                   scale=cols[:, g + k:g + k + 1])
                    ins.then_inc(part_hi, 1)
                elif kind in ("qT", "kT"):
                    dst, scale = (q_rows, qcols[0:FOX_D, 0:1]) if kind == "qT" else \
                                 (k_rows, cols[0:FOX_D, C_FK:C_FK + 1])
                    act.wait_ge(const_built, 4)
                    act.wait_ge(aux_ready, j + 1)
                    nc.scalar.activation(dst[0:FOX_D, 2 * arg:2 * arg + 2], bank[0:FOX_D, :].rearrange(
                        "p (h s) -> p h s", h=2), ACT.Copy, scale=scale).then_inc(free, 1)
                elif kind in ("mkT", "xqT"):
                    dst, scale = (mkT, cols[:, C_XK:C_XK + 1]) if kind == "mkT" else (xqT, qcols[:, 1:2])
                    act.wait_ge(aux_ready, j + 1)
                    nc.scalar.activation(dst[:, 2 * arg:2 * arg + 2], bank[:, :].rearrange("p (h s) -> p h s", h=2),
                                         ACT.Copy, scale=scale).then_inc(free, 1)
                elif kind == "logit_f":
                    act.wait_ge(forget_neg, 1)
                    nc.scalar.activation(f_tmp[:, 2], f_tmp[:, 1], ACT.Exp).then_inc(act_step, 1)
                    act.wait_ge(act_step, 2)
                    nc.scalar.activation(f_tmp[:, 3], f_tmp[:, 2], ACT.Ln, bias=1.0).then_inc(forget_log, 1)
                elif kind == "cum":
                    act.wait_ge(aux_ready, j + 1)
                    nc.scalar.activation(cum[64:R_END], bank[64:R_END, 0:SEQ], ACT.Copy).then_inc(free, 1)
                elif kind in ("fox_s", "mem_s"):
                    n = SMAX_NO[kind[:3], arg]
                    act.wait_ge(max_ready, n + 1)
                    if n >= 2:
                        old = SMAX[n - 2]
                        act.wait_ge(aux_ready, JOB[old[0] + "_pT", old[1]] + 1)
                    edges = (0, P, 3 * P) if kind == "fox_s" else (0, SEQ, 2 * SEQ)
                    for t in range(NT):
                        c = slice(edges[t], edges[t + 1])
                        nc.scalar.activation(prob[:, n % 2, c], score[:, n % 2, c], ACT.Exp,
                                             bias=nmax[:, n % 2, t:t + 1],
                                             accum_out=den[:, n % 2, t:t + 1]).then_inc(exp_ready, 1)
                elif kind in ("fox_pT", "mem_pT"):
                    n = SMAX_NO[kind[:3], arg]
                    width = 3 * P if kind == "fox_pT" else W
                    act.wait_ge(aux_ready, j + 1)
                    if n >= 2:
                        old = SMAX[n - 2]
                        act.wait_ge(aux_ready, JOB[old[0] + "_y", old[1]] + 1)
                    nc.scalar.activation(pT[:, n % 2, 0:width], bank[:, 0:width], ACT.Copy).then_inc(free, 1)
                elif kind == "fox_y":
                    act.wait_ge(aux_ready, j + 1)
                    s = slice(64 * (arg % 2), 64 * (arg % 2) + 64)
                    nc.scalar.activation(yT_hi[0][s, arg // 2], bank[s, 0:SEQ], ACT.Copy).then_inc(part_hi, 1)
                elif kind == "mem_y":
                    act.wait_ge(aux_ready, j + 1)
                    nc.scalar.activation(yT_hi[2][:, arg], bank[:, 0:SEQ], ACT.Copy).then_inc(part_hi, 1)
                elif kind == "zT":
                    act.wait_ge(aux_ready, j + 1)
                    nc.scalar.activation(hT_hi[:, 2 * arg:2 * arg + 2], bank[:].rearrange("p (k s) -> p k s", k=2),
                                         ACT.Copy).then_inc(part_hi, 1)

            def finish_block(b):
                n = BLOCK_NO[b]
                banks = acc[2 * (n % 2):2 * (n % 2) + 2]
                kind = b[0]
                if kind in ("q", "k", "mk", "xq"):
                    block_done(act, b)
                    m = {"q": 2, "k": 3, "mk": 4, "xq": 5}[kind]
                    if m > 2:
                        act.wait_ge(ss_ready[m - 1], 1)
                    for t in range(NT):
                        nc.scalar.activation(gate[:, t], banks[t][:], ACT.Square).then_inc(squares, 1)
                elif kind in ("v", "mv"):
                    block_done(act, b)
                    dst = v_tok if kind == "v" else mv_tok
                    for t in range(NT):
                        ins = nc.scalar.activation(dst[:, t], banks[t][:], ACT.Copy)
                    ins.then_inc(block_free[n % 2], 1)
                elif kind == "cu":
                    block_done(act, b)
                    for i in range(2):
                        ins = nc.scalar.activation(conv_cu[:, 2 * i:2 * i + 2],
                                                   banks[i][:].rearrange("p (c s) -> p c s", c=2), ACT.Copy)
                    ins.then_inc(block_free[n % 2], 1)
                elif kind == "cb":
                    act.wait_ge(conv_y, 1)
                    nc.scalar.activation(yT_hi[1][:], conv_out[:], ACT.Copy).then_inc(conv_hi, 1)
                elif kind == "gate":
                    block_done(act, b)
                    g = (n - BLOCK_NO[("gate", 1, 0)]) // 2
                    if g == 0:
                        act.wait_ge(ss_ready[5], 1)
                    elif g <= 2:
                        block_read(act, BLOCKS[n - 1])
                    else:
                        act.wait_ge(merged_done, g - 2)
                    for t in range(NT):
                        ins = nc.scalar.activation(gate[:, t], banks[t][:], ACT.Sigmoid)
                    ins.then_inc(block_free[n % 2], 1)

            bias_steps = [3, 5, 9, 11, 14, 16, 18, 20]
            for step in range(0, NP + 1):
                if step == 0:
                    for j, kind, arg in jobs_at(-1):
                        finish_job(j, kind, arg)
                    for t in range(NT):
                        act.wait_ge(mem_loaded[t], 16)
                        ins = nc.scalar.activation(scratch[t], mem_sb[:, t], ACT.Square, accum_out=ss[:, 1, t:t + 1])
                    ins.then_inc(ss_ready[1], 1)
                    nc.scalar.activation(b_raw[:], ident[0:96, 0:1].to_broadcast([96, W]), ACT.Copy,
                                         scale=0.0).then_inc(act_step, 1)
                if step + 1 < NP:
                    split_hi(step + 1)
                if step > 0:
                    for j, kind, arg in jobs_at(step - 1):
                        finish_job(j, kind, arg)
                for b in BLOCKS:
                    if LAST_PIECE[b] == step - 1:
                        finish_block(b)
                if step in bias_steps:
                    bias_rows(bias_steps.index(step))

            for t in range(NT):
                act.wait_ge(x1_ready, 4 if t else 3)
                ins = nc.scalar.activation(x1r[:, t], x1[:, t], ACT.Square, accum_out=ss[:, 6, t:t + 1])
            ins.then_inc(ss_ready[6], 1)
            act.dma_start(wr[:], wr_d).then_inc(wr_loaded, 16)
            for g in range(4):
                if g < NT:
                    act.wait_ge(x1s_ready, g + 1)
                    nc.scalar.activation(m_parts[:, 0, g], x1s[:, g], ACT.Copy).then_inc(parts_act, 1)
            for g in (0, 2):
                act.wait_ge(x1sT_ready, g + 1)
                for k in (2 * g, 2 * g + 1):
                    ins = nc.scalar.activation(h2T[:, k], aux[g][:, (k % 2) * SEQ:(k % 2 + 1) * SEQ], ACT.Copy,
                                               scale=cols[:, C_G2 + k:C_G2 + k + 1])
                ins.then_inc(h2T_act, 1)
            for t in range(NT):
                act.wait_ge(parts_pool, t + 1)
                nc.scalar.activation(m_parts[:, 1, t], x1r[:, t], ACT.Copy).then_inc(parts_act, 1)
            act.wait_ge(top_ready, 1)
            for t in range(NT):
                nc.scalar.activation(top_e[:, t], top_v[:, t, 0:TOPK], ACT.Exp, bias=ntop[:, t:t + 1],
                                     accum_out=top_den[:, t, 0:1]).then_inc(soft_ready, 1)

            nc.scalar.activation(aT[:, 0], ident[:], ACT.Copy).then_inc(aT_ready, 1)
            nc.scalar.activation(y_sb[:, 0:P], ident[:], ACT.Copy).then_inc(y_ready, 1)

            def item(n):
                act.wait_ge(glu_ready, n)
                nc.scalar.activation(sig[:], glu[:], ACT.Sigmoid, scale=ALPHA).then_inc(sig_ready, 1)
                act.wait_ge(pick_wT_done, n)
                act.wait_ge(scattered, n)
                nc.scalar.activation(pick_wT[:].rearrange("p t s -> p (t s)"), bank_t[:, 0:NT * P],
                                     ACT.Copy).then_inc(pick_wT_ready, 1)
                act.wait_ge(aT_done, n)
                nc.scalar.activation(aT[:].rearrange("p k s -> p (k s)"), bank_t[:], ACT.Copy).then_inc(aT_ready, 1)
                act.wait_ge(y_done, n)
                nc.scalar.activation(y_sb[:], bank_cy[:], ACT.Copy).then_inc(y_ready, 1)

            with act.Fori(1, NEXP + 1) as n:
                item(n)
            act.wait_ge(meta_ready, 1)
            more = act.value_load(meta[0:1, EXTRA_COLS:EXTRA_COLS + 1], min_val=0, max_val=EXTRA)
            with act.If(more > 0):
                with act.Fori(NEXP + 1, NEXP + 1 + more) as n:
                    item(n)

        @block.vector
        def _(dve):
            steps = [0]

            def chained(ins):
                steps[0] += 1
                ins.then_inc(dve_step, 1)
                dve.wait_ge(dve_step, steps[0])

            def plain_f32(ap):
                return ap.bitcast(F32)

            def split_lo(p):
                for h in range(2):
                    s = 2 * p + h
                    dve.wait_ge(hi_done, s + 1)
                    nc.vector.tensor_tensor(w_lo[:, s % 4], raw[:, p % 4, 2 * h:2 * h + 2],
                                            plain_f32(w_hi[:, s % 4]), ALU.subtract).then_inc(lo_done, 1)


            def finish_job(j, kind, arg):
                bank = aux[j % 4]
                free = aux_free[j % 4]
                if kind in ("hT", "mT"):
                    hi, lo, g = (hT_hi, hT_lo, C_G1) if kind == "hT" else (mT_hi, mT_lo, C_GM)
                    dve.wait_ge(part_hi, SPLIT_NO[j] + 1)
                    for i in range(2):
                        k = 2 * arg + i
                        ins = nc.vector.scalar_tensor_tensor(lo[:, k], bank[:, i * SEQ:(i + 1) * SEQ],
                                                             cols[:, g + k:g + k + 1], plain_f32(hi[:, k]),
                                                             ALU.mult, ALU.subtract)
                    ins.then_inc(free, 1)
                elif kind == "logit_f":
                    dve.wait_ge(aux_ready, j + 1)
                    dve.wait_ge(params_loaded, 16 * 3)
                    nc.vector.tensor_tensor(
                        f_tmp[:, 0], bank[:, 0:NT * FOX_H].rearrange("p (t h) -> p t h", t=NT),
                        spread[:, 0:FOX_H].unsqueeze(1).to_broadcast([P, NT, FOX_H]), ALU.add).then_inc(free, 1)
                    dve.wait_ge(free, j // 4 + 1)
                    nc.vector.scalar_tensor_tensor(f_tmp[:, 1], f_tmp[:, 0], -1.0, f_tmp[:, 0],
                                                   ALU.mult, ALU.min).then_inc(forget_neg, 1)
                    dve.wait_ge(forget_log, 1)
                    dve.wait_ge(const_built, 3)
                    nc.vector.scalar_tensor_tensor(f_cols[:, :, R_NEG:R_NEG + FOX_H], f_tmp[:, 0], 0.0, f_tmp[:, 3],
                                                   ALU.min, ALU.subtract).then_inc(dve_step, 1)
                    steps[0] += 1
                    nc.vector.scalar_tensor_tensor(f_cols[:, :, R_POS:R_END], f_tmp[:, 0], 0.0, f_tmp[:, 3],
                                                   ALU.min, ALU.subtract).then_inc(dve_step, 1)
                    steps[0] += 1
                    dve.wait_ge(dve_step, steps[0])
                    nc.vector.tensor_scalar(f_cols[:, :, R_NEG:R_NEG + FOX_H], f_cols[:, :, R_NEG:R_NEG + FOX_H],
                                            -1.0, None, ALU.mult).then_inc(forget_ready, 1)
                elif kind in ("fox_s", "mem_s"):
                    n = SMAX_NO[kind[:3], arg]
                    edges = (0, P, 3 * P) if kind == "fox_s" else (0, SEQ, 2 * SEQ)
                    if n >= 2:
                        dve.wait_ge(exp_ready, 2 * (n - 2) + 2)
                    dve.wait_ge(aux_ready, j + 1)
                    if kind == "fox_s":
                        dve.wait_ge(const_built, 6)
                        nc.vector.tensor_tensor(score[:, n % 2, 0:3 * P], bank[:, 0:3 * P], mask[:],
                                                ALU.add).then_inc(free, 1)
                    else:
                        nc.vector.tensor_copy(score[:, n % 2], bank[:]).then_inc(free, 1)
                    dve.wait_ge(free, j // 4 + 1)
                    for t in range(NT):
                        ins = nc.vector.tensor_reduce(nmax[:, n % 2, t:t + 1], score[:, n % 2, edges[t]:edges[t + 1]],
                                                      AX, ALU.max, negate=True)
                    ins.then_inc(max_ready, 1)
                elif kind in ("fox_y", "mem_y"):
                    dve.wait_ge(part_hi, SPLIT_NO[j] + 1)
                    if kind == "fox_y":
                        s = slice(64 * (arg % 2), 64 * (arg % 2) + 64)
                        b, part = 0, (s, arg // 2)
                    else:
                        s = slice(0, P)
                        b, part = 2, (s, arg)
                    nc.vector.tensor_tensor(yT_lo[b][part], bank[s, 0:SEQ], plain_f32(yT_hi[b][part]),
                                            ALU.subtract).then_inc(free, 1)
                elif kind == "zT":
                    dve.wait_ge(part_hi, SPLIT_NO[j] + 1)
                    k = slice(2 * arg, 2 * arg + 2)
                    nc.vector.tensor_tensor(hT_lo[:, k], bank[:].rearrange("p (k s) -> p k s", k=2),
                                            plain_f32(hT_hi[:, k]), ALU.subtract).then_inc(free, 1)

            def normalise_probs(kind, arg):
                n = SMAX_NO[kind[:3], arg]
                edges = (0, P, 3 * P) if kind == "fox_s" else (0, SEQ, 2 * SEQ)
                dve.wait_ge(exp_ready, 2 * n + 2)
                chained(nc.vector.reciprocal(rden[:, n % 2], den[:, n % 2]))
                for t in range(NT):
                    c = slice(edges[t], edges[t + 1])
                    ins = nc.vector.tensor_scalar(prob[:, n % 2, c], prob[:, n % 2, c], rden[:, n % 2, t:t + 1],
                                                  None, ALU.mult)
                ins.then_inc(prob_ready, 1)

            norm_blocks = {"q": (2, 0), "k": (3, 1), "mk": (4, 0), "xq": (5, 1)}

            def block_squares(b):
                n, _ = norm_blocks[b[0]]
                heads = FOX_H if n < 4 else MEM_H
                for t in range(NT):
                    dve.wait_ge(squares, 2 * (n - 2) + t + 1)
                    ins = nc.vector.tensor_reduce(ss[:, n, t * heads:(t + 1) * heads],
                                                  gate[:, t].rearrange("p (h d) -> p h d", h=heads), AX, ALU.add)
                ins.then_inc(ss_ready[n], 1)

            def block_scale(b):
                n, where = norm_blocks[b[0]]
                no = BLOCK_NO[b]
                banks = acc[2 * (no % 2):2 * (no % 2) + 2]
                heads = FOX_H if n < 4 else MEM_H
                width = W // heads
                dve.wait_ge(rstd_ready, n + 1)
                if n == 2:
                    dve.wait_ge(xs_ready, 4)
                if n >= 4:
                    dve.wait_ge(aux_ready, JOB[{4: "qT", 5: "kT"}[n], 3] + 1)
                for t in range(NT):
                    ins = nc.vector.tensor_tensor(
                        tok[:, where, t].rearrange("p (h d) -> p h d", h=heads),
                        banks[t][:].rearrange("p (h d) -> p h d", h=heads),
                        rstd[:, n, t * heads:(t + 1) * heads].unsqueeze(2).to_broadcast([P, heads, width]), ALU.mult)
                ins.then_inc(block_free[no % 2], 1)

            def finish_block(b):
                n = BLOCK_NO[b]
                banks = acc[2 * (n % 2):2 * (n % 2) + 2]
                kind = b[0]
                if kind == "cc":
                    block_read(dve, ("cu",))
                    nc.vector.memset(conv_u[:, :, 0:2], 0.0).then_inc(dve_step, 1)
                    steps[0] += 1
                    block_done(dve, b)
                    for i in range(2):
                        ins = nc.vector.tensor_tensor(conv_u[:, 2 * i:2 * i + 2, 2:2 + SEQ],
                                                      banks[i][:].rearrange("p (c s) -> p c s", c=2),
                                                      conv_cu[:, 2 * i:2 * i + 2], ALU.mult)
                    ins.then_inc(block_free[n % 2], 1)
                    block_read(dve, b)
                    dve.wait_ge(dve_step, steps[0])
                    for c in range(KB):
                        tap = cols[:, C_CONV + c:C_CONV + c + 1]
                        nc.vector.tensor_scalar(conv_out[:, c], conv_u[:, c, 0:SEQ], tap, None,
                                                ALU.mult).then_inc(dve_step, 1)
                        steps[0] += 1
                    for j in (1, 2):
                        dve.wait_ge(dve_step, steps[0])
                        for c in range(KB):
                            tap = cols[:, C_CONV + j * KB + c:C_CONV + j * KB + c + 1]
                            nc.vector.scalar_tensor_tensor(conv_out[:, c], conv_u[:, c, j:j + SEQ], tap,
                                                           conv_out[:, c], ALU.mult, ALU.add).then_inc(dve_step, 1)
                            steps[0] += 1
                elif kind == "cb":
                    dve.wait_ge(dve_step, steps[0])
                    block_done(dve, b)
                    for i in range(2):
                        s = slice(2 * i, 2 * i + 2)
                        ins = nc.vector.tensor_tensor(conv_out[:, s], banks[i][:].rearrange("p (c s) -> p c s", c=2),
                                                      conv_out[:, s], ALU.mult)
                    ins.then_inc(conv_y, 1)
                    dve.wait_ge(conv_hi, 1)
                    nc.vector.tensor_tensor(yT_lo[1][:], conv_out[:], plain_f32(yT_hi[1][:]),
                                            ALU.subtract).then_inc(block_free[n % 2], 1)
                elif kind == "proj":
                    g = (n - BLOCK_NO[("proj", 1, 0)]) // 2
                    half = slice(b[2] * W, (b[2] + 1) * W)
                    block_read(dve, BLOCKS[n - 1])
                    block_done(dve, b)
                    if g < 2:
                        for t in range(NT):
                            ins = nc.vector.tensor_tensor(merged[:, t, half], banks[t][:], gate[:, t], ALU.mult)
                        ins.then_inc(block_free[n % 2], 1)
                    else:
                        for t in range(NT):
                            ins = nc.vector.tensor_tensor(gate[:, t], banks[t][:], gate[:, t], ALU.mult)
                        ins.then_inc(block_free[n % 2], 1)
                        block_read(dve, b)
                        for t in range(NT):
                            ins = nc.vector.tensor_tensor(merged[:, t, half], merged[:, t, half], gate[:, t], ALU.add)
                        ins.then_inc(merged_done, 1)
                elif kind == "out":
                    half = slice(b[1] * W, (b[1] + 1) * W)
                    block_done(dve, b)
                    for t in range(NT):
                        nc.vector.tensor_tensor(x1[:, t, half], banks[t][:], x1[:, t, half],
                                                ALU.add).then_inc(x1_ready, 1)

            dve.wait_ge(rstd_ready, 1)
            for t in range(NT):
                nc.vector.tensor_scalar(xs[:, t], x1[:, t], rstd[:, 0, t:t + 1], None, ALU.mult).then_inc(xs_ready, 1)
            dve.wait_ge(wf_hi_done, 1)
            nc.vector.tensor_tensor(wf_lo[:], wf[:], plain_f32(wf_hi[:]), ALU.subtract).then_inc(wf_lo_done, 1)
            split_lo(0)
            for step in range(0, NP + 1):
                here = jobs_at(step - 1)
                for j, kind, arg in here:
                    if kind in ("fox_s", "mem_s"):
                        finish_job(j, kind, arg)
                    elif kind == "hT":
                        finish_job(j, kind, arg)
                done = [b for b in BLOCKS if LAST_PIECE[b] == step - 1]
                if step + 1 < NP:
                    split_lo(step + 1)
                for b in done:
                    if b[0] in norm_blocks:
                        block_squares(b)
                for j, kind, arg in here:
                    if kind in ("fox_s", "mem_s"):
                        normalise_probs(kind, arg)
                    elif kind != "hT":
                        finish_job(j, kind, arg)
                for b in done:
                    if b[0] in norm_blocks:
                        block_scale(b)
                    else:
                        finish_block(b)
                if step == 0:
                    dve.wait_ge(rstd_ready, 2)
                    dve.wait_ge(aux_ready, JOB["hT", 3] + 1)
                    for t in range(NT):
                        nc.vector.tensor_scalar(xs[:, t], mem_sb[:, t], rstd[:, 1, t:t + 1], None,
                                                ALU.mult).then_inc(xs_ready, 1)

            dve.wait_ge(rstd_ready, 7)
            for t in range(NT):
                nc.vector.tensor_scalar(x1s[:, t], x1[:, t], rstd[:, 6, t:t + 1], None, ALU.mult).then_inc(x1s_ready, 1)
            for g in (1, 3):
                dve.wait_ge(x1sT_ready, g + 1)
                for k in (2 * g, 2 * g + 1):
                    ins = nc.vector.tensor_scalar(h2T[:, k], aux[g][:, (k % 2) * SEQ:(k % 2 + 1) * SEQ],
                                                  cols[:, C_G2 + k:C_G2 + k + 1], None, ALU.mult)
                ins.then_inc(h2T_dve, 1)
            dve.wait_ge(logits_ready, 1)
            chained(nc.vector.tensor_tensor(logits[:], acc[0][:, 0:NT * NEXP].rearrange("p (t e) -> p t e", t=NT),
                                            spread[:, 8:40].unsqueeze(1).to_broadcast([P, NT, NEXP]), ALU.add))
            for t in range(NT):
                ins = nc.vector.max(top_v[:, t], logits[:, t])
            chained(ins)
            for t in range(NT):
                nc.vector.tensor_scalar(ntop[:, t:t + 1], top_v[:, t, 0:1], -1.0, None, ALU.mult
                                        ).then_inc(top_ready if t == NT - 1 else dve_step, 1)
            steps[0] += 1
            for t in range(NT):
                ins = nc.vector.max_index(top_i[:, t], top_v[:, t], logits[:, t])
            chained(ins)
            chained(nc.vector.tensor_copy(top_f[:], top_i[:]))
            dve.wait_ge(const_built, 14)
            wide4 = [P, NT, TOPK, NEXP]
            chained(nc.vector.tensor_tensor(hot4[:], iota[:, 0:NEXP].unsqueeze(1).unsqueeze(1).to_broadcast(wide4),
                                            top_f[:, :, 0:TOPK].unsqueeze(3).to_broadcast(wide4), ALU.is_equal))
            chained(nc.vector.tensor_reduce(chosen[:], hot4[:].rearrange("p t k e -> p t e k"), AX, ALU.add))
            nc.vector.tensor_copy(chosen3[:], chosen[:].unsqueeze(2).to_broadcast([P, NT, 3, NEXP])
                                  ).then_inc(chosen_ready, 1)
            dve.wait_ge(soft_ready, 2)
            chained(nc.vector.reciprocal(top_den[:, :, 1:2], top_den[:, :, 0:1]))
            chained(nc.vector.tensor_tensor(top_e[:], top_e[:], top_den[:, :, 1:2].to_broadcast([P, NT, TOPK]),
                                            ALU.mult))
            chained(nc.vector.tensor_tensor(hot4w[:], hot4[:], top_e[:].unsqueeze(3).to_broadcast(wide4), ALU.mult))
            dve.wait_ge(const_built, 15)
            chained(nc.vector.tensor_reduce(comb_tab[:, :, 0:NEXP], hot4w[:].rearrange("p t k e -> p t e k"),
                                            AX, ALU.add))
            dve.wait_ge(slots_ready, 1)
            slots = acc[1][:, 0:NT * NEXP].rearrange("p (t e) -> p t e", t=NT)
            chained(nc.vector.scalar_tensor_tensor(pos_tab[:, :, 0:NEXP], slots, 1.0, chosen[:], ALU.add, ALU.mult))
            nc.vector.tensor_scalar(pos_tab[:, :, 0:NEXP], pos_tab[:, :, 0:NEXP], -1.0, None,
                                    ALU.add).then_inc(table_ready, 1)
            dve.wait_ge(table_ready, 1)

            def build_pick(col):
                for t in range(NT):
                    ins = nc.vector.tensor_scalar(pick[:, t], iota[:], pos_tab[:, t, col], None, ALU.is_equal)
                ins.then_inc(pick_ready, 1)

            def build_pick_w(col):
                for t in range(NT):
                    ins = nc.vector.tensor_scalar(pick_w[:, t], iota[:].unsqueeze(1).to_broadcast([P, 2, SLOTS]),
                                                  pos_tab[:, t, col], comb_tab[:, t, col], ALU.is_equal, ALU.mult)
                ins.then_inc(pick_w_ready, 1)

            def build_bias_sel(col):
                nc.vector.tensor_scalar(bias_sel[:], ones_bf[0:96, 0:SLOTS], exp_sel[:, col], None,
                                        ALU.mult).then_inc(bias_sel_ready, 1)

            def move_gathered():
                nc.vector.tensor_tensor(xgT[:], bank_cy[:].rearrange("p (k s) -> p k s", k=KD),
                                        cols[:, C_G2:C_G2 + KD].unsqueeze(2).to_broadcast([P, KD, SLOTS]),
                                        ALU.mult).then_inc(xg_ready, 1)

            build_pick(slice(0, 1))
            build_pick_w(slice(0, 1))
            build_bias_sel(slice(0, 1))
            chained(nc.vector.tensor_copy(count[:, 0:1], acc[1][0:96, 2 * NEXP:2 * NEXP + 1]))
            chained(nc.vector.tensor_scalar(count[:, 1:2], count[:, 0:1], float(SLOTS), None, ALU.is_gt))
            chained(nc.vector.scalar_tensor_tensor(count[:, 2:3], count[:, 0:1], 2.0 * SLOTS, count[:, 1:2],
                                                   ALU.is_gt, ALU.add))
            chained(nc.vector.scalar_tensor_tensor(extra[:, 0:1], count[:, 0:1], 3.0 * SLOTS, count[:, 2:3],
                                                   ALU.is_gt, ALU.add))
            nc.vector.tensor_copy(extra_bf[:], extra[:, 0:1].to_broadcast([96, 2])).then_inc(extra_ready, 1)
            dve.wait_ge(gathered, 1)
            move_gathered()
            build_pick(slice(1, 2))
            dve.wait_ge(first_ready, 1)
            chained(nc.vector.tensor_copy(first[:, 0:1], acc[2][0:96, 0:1]))
            chained(nc.vector.tensor_scalar(xt[:, 0], iota[0:96, 0:EXTRA_COLS], first[:, 0:1], None, ALU.subtract))
            chained(nc.vector.tensor_scalar(xt[:, 1], xt[:, 0], 0.0, None, ALU.is_ge))
            chained(nc.vector.scalar_tensor_tensor(exp_sel[:, NEXP:NEXP + EXTRA_COLS], xt[:, 0], extra[:, 0:1],
                                                   xt[:, 1], ALU.is_lt, ALU.mult))
            chained(nc.vector.scalar_tensor_tensor(xt[:, 2], xt[:, 0], 1.0, exp_sel[:, NEXP:NEXP + EXTRA_COLS],
                                                   ALU.add, ALU.mult))
            chained(nc.vector.tensor_scalar(xt[:, 2], xt[:, 2], -float(SLOTS), None, ALU.mult))
            dve.wait_ge(list_ready, 1)
            nc.vector.tensor_copy(posT[:], bank_glu[0:32, :].rearrange("p (a t s) -> p a t s", a=2, t=NT)
                                  ).then_inc(xtab_ready, 1)
            dve.wait_ge(list_ready, 2)
            nc.vector.tensor_copy(pos_tab[:, :, NEXP:NEXP + EXTRA_COLS],
                                  bank_lin[:, 0:NT * EXTRA_COLS].rearrange("p (t j) -> p t j", t=NT))
            nc.vector.tensor_copy(comb_tab[:, :, NEXP:NEXP + EXTRA_COLS],
                                  bank_lin[:, SEQ:SEQ + NT * EXTRA_COLS].rearrange("p (t j) -> p t j", t=NT))
            nc.vector.tensor_copy(meta[0:1, :], bank_lin[0:1, 128:128 + EXTRA_COLS + 1]).then_inc(meta_ready, 1)
            dve.wait_ge(meta_ready, 1)
            nc.vector.memset(glu[:, 0:1], 0.0).then_inc(up_read, 1)

            def item(n):
                dve.wait_ge(up_done, n)
                nc.vector.tensor_scalar(glu[:], bank_glu[:], LIMIT, None, ALU.min).then_inc(glu_ready, 1)
                nc.vector.tensor_scalar(lin[:], bank_lin[:], LIMIT, -LIMIT, ALU.min, ALU.max).then_inc(up_read, 1)
                dve.wait_ge(glu_ready, n)
                dve.wait_ge(up_read, n + 1)
                nc.vector.scalar_tensor_tensor(glin[:], lin[:], 1.0, glu[:], ALU.add, ALU.mult
                                               ).then_inc(glin_ready, 1)
                dve.wait_ge(glin_ready, n)
                dve.wait_ge(sig_ready, n)
                nc.vector.tensor_tensor(a_tok[:], glin[:], sig[:], ALU.mult).then_inc(a_ready, 1)
                dve.wait_ge(gathered, n + 1)
                move_gathered()
                build_pick(bass.ds(n + 1, 1))
                dve.wait_ge(pick_wT_done, n)
                build_pick_w(bass.ds(n, 1))
                dve.wait_ge(y_done, n)
                build_bias_sel(bass.ds(n, 1))

            with dve.Fori(1, NEXP + 1) as n:
                item(n)
            more = dve.value_load(meta[0:1, EXTRA_COLS:EXTRA_COLS + 1], min_val=0, max_val=EXTRA)
            with dve.If(more > 0):
                with dve.Fori(NEXP + 1, NEXP + 1 + more) as n:
                    item(n)
            dve.wait_ge(scattered, more + NEXP + 1)
            for t in range(NT):
                for h in range(2):
                    s = slice(h * W, (h + 1) * W)
                    nc.vector.tensor_tensor(x1[:, t, s], acc[2 * t + h][:], x1[:, t, s], ALU.add).then_inc(out_ready, 1)

        @block.tensor
        def _(pe):
            def bank_of(j):
                if j >= 4:
                    pe.wait_ge(aux_free[j % 4], j // 4)
                return aux[j % 4]

            def job_read(kind, arg):
                j = JOB[kind, arg]
                pe.wait_ge(aux_free[j % 4], j // 4 + 1)

            def do_job(j, kind, arg):
                if kind in ("hT", "mT"):
                    pe.wait_ge(xs_ready, 2 if kind == "hT" else 4)
                    if kind == "hT":
                        pe.wait_ge(const_built, 1)
                    bank = bank_of(j)
                    for i in range(2):
                        for t in range(NT):
                            k = 2 * arg + i
                            ins = nc.tensor.transpose(bank[:, i * SEQ + t * P:i * SEQ + (t + 1) * P],
                                                      xs[:, t, k * P:(k + 1) * P], ident[:])
                elif kind == "logit_f":
                    bank = bank_of(j)
                    pe.wait_ge(wf_lo_done, 1)
                    for t in range(NT):
                        s = slice(t * P, (t + 1) * P)
                        for k in range(KD):
                            for c, (a, w) in enumerate(((hT_hi, wf_hi), (hT_lo, wf_hi), (hT_hi, wf_lo))):
                                ins = nc.tensor.matmul(bank[:, t * FOX_H:(t + 1) * FOX_H], a[:, k, s], w[:, k],
                                                       start=(k == 0 and c == 0), stop=(k == KD - 1 and c == 2))
                elif kind == "cum":
                    bank = bank_of(j)
                    pe.wait_ge(forget_ready, 1)
                    nc.tensor.matmul(bank[0:R_END, 0:SEQ], f_cols[:, 0], tri_ones[:], start=True, stop=False,
                                     skip_group_check=True)
                    ins = nc.tensor.matmul(bank[0:R_END, P:SEQ], f_cols[:, 1], tri_ones[:, 0:P], start=False,
                                           stop=True, skip_group_check=True)
                elif kind in ("qT", "kT"):
                    bank = bank_of(j)
                    block_read(pe, (kind[0],))
                    for i in range(2):
                        h = 2 * arg + i
                        for t in range(NT):
                            ins = nc.tensor.transpose(bank[0:FOX_D, i * SEQ + t * P:i * SEQ + (t + 1) * P],
                                                      tok[:, 0 if kind == "qT" else 1, t, h * FOX_D:(h + 1) * FOX_D],
                                                      ident[:])
                elif kind in ("mkT", "xqT"):
                    bank = bank_of(j)
                    block_read(pe, (kind[:2],))
                    for i in range(2):
                        h = 2 * arg + i
                        for t in range(NT):
                            ins = nc.tensor.transpose(bank[:, i * SEQ + t * P:i * SEQ + (t + 1) * P],
                                                      tok[:, 0 if kind == "mkT" else 1, t, h * P:(h + 1) * P], ident[:])
                elif kind == "fox_s":
                    bank = bank_of(j)
                    if arg == 0:
                        job_read("qT", 3)
                        pe.wait_ge(rows_ready, 1)
                    if arg % 2 == 0:
                        job_read("kT", arg // 2)
                    nc.tensor.matmul(bank[:, 0:P], q_rows[0:R_END, arg, 0:P], k_rows[0:R_END, arg, 0:P],
                                     start=True, stop=True)
                    ins = nc.tensor.matmul(bank[:, P:3 * P], q_rows[0:R_END, arg, P:SEQ], k_rows[0:R_END, arg],
                                           start=True, stop=True)
                elif kind == "mem_s":
                    bank = bank_of(j)
                    if arg % 2 == 0:
                        job_read("xqT", arg // 2)
                        job_read("mkT", arg // 2)
                    for t in range(NT):
                        ins = nc.tensor.matmul(bank[:, t * SEQ:(t + 1) * SEQ], xqT[:, arg, t * P:(t + 1) * P],
                                               mkT[:, arg], start=True, stop=True)
                elif kind in ("fox_pT", "mem_pT"):
                    bank = bank_of(j)
                    n = SMAX_NO[kind[:3], arg]
                    pe.wait_ge(prob_ready, n + 1)
                    order = [0, 1, 2] if kind == "fox_pT" else [0, 2, 1, 3]
                    for i, c in enumerate(order):
                        ins = nc.tensor.transpose(bank[:, i * P:(i + 1) * P], prob[:, n % 2, c * P:(c + 1) * P],
                                                  ident[:])
                elif kind == "fox_y":
                    bank = bank_of(j)
                    if arg == 0:
                        block_read(pe, ("v",))
                    job_read("fox_pT", arg)
                    n = SMAX_NO["fox", arg]
                    s = slice(64 * (arg % 2), 64 * (arg % 2) + 64)
                    c = slice(arg * FOX_D, (arg + 1) * FOX_D)
                    nc.tensor.matmul(bank[s, 0:SEQ], v_tok[:, 0, c], pT[:, n % 2, 0:SEQ], start=True, stop=False,
                                     skip_group_check=True)
                    ins = nc.tensor.matmul(bank[s, P:SEQ], v_tok[:, 1, c], pT[:, n % 2, SEQ:3 * P], start=False,
                                           stop=True, skip_group_check=True)
                elif kind == "mem_y":
                    bank = bank_of(j)
                    if arg == 0:
                        block_read(pe, ("mv",))
                    job_read("mem_pT", arg)
                    n = SMAX_NO["mem", arg]
                    for t in range(NT):
                        ins = nc.tensor.matmul(bank[:, 0:SEQ], mv_tok[:, t, arg * P:(arg + 1) * P],
                                               pT[:, n % 2, t * SEQ:(t + 1) * SEQ], start=(t == 0), stop=(t == 1))
                elif kind == "zT":
                    bank = bank_of(j)
                    pe.wait_ge(merged_done, 3 if arg < 2 else 4)
                    for i in range(2):
                        for t in range(NT):
                            k = 2 * arg + i
                            ins = nc.tensor.transpose(bank[:, i * SEQ + t * P:i * SEQ + (t + 1) * P],
                                                      merged[:, t, k * P:(k + 1) * P], ident[:])
                ins.then_inc(aux_ready, 1)

            def piece(p):
                b, half = PIECES[p]
                kind = b[0]
                n = BLOCK_NO[b]
                banks = acc[2 * (n % 2):2 * (n % 2) + 2]
                last = p == LAST_PIECE[b]
                if half == 0 and n >= 2:
                    pe.wait_ge(block_free[n % 2], n // 2)
                if p == 0:
                    job_read("hT", 3)
                if b == ("mk",) and half == 0:
                    job_read("mT", 3)
                if kind == "proj" and b[2] == 0:
                    if b[1] == 0:
                        for h in range(FOX_H):
                            job_read("fox_y", h)
                    elif b[1] == 1:
                        block_read(pe, ("cb",))
                    else:
                        for h in range(MEM_H):
                            job_read("mem_y", h)
                if kind == "out" and b[1] == 0:
                    job_read("zT", 2 * half)
                    job_read("zT", 2 * half + 1)
                if kind == "proj":
                    a_hi, a_lo = yT_hi[b[1]], yT_lo[b[1]]
                elif kind in ("mk", "mv"):
                    a_hi, a_lo = mT_hi, mT_lo
                else:
                    a_hi, a_lo = hT_hi, hT_lo
                if kind == "gate" and half == 0:
                    if n == BLOCK_NO[("gate", 1, 0)]:
                        pe.wait_ge(const_built, 7)
                        pe.wait_ge(brow_used, 2)
                    for t in range(NT):
                        nc.tensor.matmul(banks[t][:], gate_sel[:, b[1]], bias_gate[:, b[2] * W:(b[2] + 1) * W],
                                         start=True, stop=False)
                for h in range(2):
                    s = 2 * p + h
                    pe.wait_ge(lo_done, s + 1)
                    for i in range(2):
                        k = half * KB + 2 * h + i
                        opening = half == 0 and h == 0 and i == 0
                        closing = last and h == 1 and i == 1
                        wh, wl = w_hi[:, s % 4, i], w_lo[:, s % 4, i]
                        if kind in ("cu", "cc", "cb"):
                            for c in range(KB):
                                dst = banks[c // 2][:, (c % 2) * SEQ:(c % 2 + 1) * SEQ]
                                cs = slice(c * P, (c + 1) * P)
                                for m, (w_, a_) in enumerate(((wh, a_hi), (wh, a_lo), (wl, a_hi))):
                                    ins = nc.tensor.matmul(dst, w_[:, cs], a_[:, k],
                                                           start=opening and m == 0 and c % 2 == 0,
                                                           stop=closing and m == 2, skip_group_check=True)
                        else:
                            for t in range(NT):
                                ts = slice(t * P, (t + 1) * P)
                                for m, (a_, w_) in enumerate(((a_hi, wh), (a_hi, wl), (a_lo, wh))):
                                    ins = nc.tensor.matmul(banks[t][:], a_[:, k, ts], w_,
                                                           start=opening and m == 0 and kind != "gate",
                                                           stop=closing and m == 2)
                    ins.then_inc(half_used, 1)

            for j, kind, arg in jobs_at(-1):
                do_job(j, kind, arg)
            for p in range(NP):
                piece(p)
                for j, kind, arg in jobs_at(p):
                    do_job(j, kind, arg)

            for g in range(4):
                pe.wait_ge(x1s_ready, NT)
                if g == 0:
                    for b in range(4):
                        js = [j for j in range(len(JOBS)) if j % 4 == b]
                        pe.wait_ge(aux_free[b], len(js))
                for i in range(2):
                    for t in range(NT):
                        k = 2 * g + i
                        ins = nc.tensor.transpose(aux[g][:, i * SEQ + t * P:i * SEQ + (t + 1) * P],
                                                  x1s[:, t, k * P:(k + 1) * P], ident[:])
                ins.then_inc(x1sT_ready, 1)
            pe.wait_ge(x1_ready, 4)
            pe.wait_ge(h2T_act, 2)
            pe.wait_ge(h2T_dve, 2)
            pe.wait_ge(wr_loaded, 16)
            for t in range(NT):
                for k in range(KD):
                    ins = nc.tensor.matmul(acc[0][:, t * NEXP:(t + 1) * NEXP], h2T[:, k, t * P:(t + 1) * P], wr[:, k],
                                           start=(k == 0), stop=(k == KD - 1))
            ins.then_inc(logits_ready, 1)
            pe.wait_ge(chosen_ready, 1)
            pe.wait_ge(const_built, 14)
            hot = [chosen3[:, t, 0] for t in range(NT)]
            nc.tensor.matmul(acc[1][:, 0:NEXP], tri_strict[:], hot[0], start=True, stop=True)
            nc.tensor.matmul(acc[1][:, NEXP:2 * NEXP], ones_bf[:], hot[0], start=True, stop=False)
            nc.tensor.matmul(acc[1][:, NEXP:2 * NEXP], tri_strict[:], hot[1], start=False, stop=True)
            for t in range(NT):
                ins = nc.tensor.matmul(acc[1][0:96, 2 * NEXP:2 * NEXP + 2],
                                       chosen3[:, t].rearrange("p a e -> p (a e)"), ones_bf[:, 0:2],
                                       start=(t == 0), stop=(t == 1))
            ins.then_inc(slots_ready, 1)

            def gather():
                for k in range(KD):
                    for t in range(NT):
                        for m in range(3):
                            ins = nc.tensor.matmul(bank_cy[:, k * SLOTS:(k + 1) * SLOTS],
                                                   m_parts[:, m, t, k * P:(k + 1) * P], pick[:, t],
                                                   start=(t == 0 and m == 0), stop=(t == NT - 1 and m == 2))
                ins.then_inc(gathered, 1)

            pe.wait_ge(parts_pool, 2 * NT)
            pe.wait_ge(parts_act, 2 * NT)
            pe.wait_ge(pick_ready, 1)
            gather()
            pe.wait_ge(extra_ready, 1)
            nc.tensor.matmul(acc[2][0:96, 0:2], block_tri[:], extra_bf[:], start=True, stop=True
                             ).then_inc(first_ready, 1)
            pe.wait_ge(table_ready, 1)
            for a, tab in enumerate((pos_tab, comb_tab)):
                for t in range(NT):
                    c = (a * NT + t) * P
                    ins = nc.tensor.transpose(bank_glu[0:32, c:c + P], tab[:, t, 0:NEXP], ident[:])
            ins.then_inc(list_ready, 1)
            pe.wait_ge(xtab_ready, 1)
            hot_x = exp_sel[0:32, NEXP:NEXP + EXTRA_COLS]
            for t in range(NT):
                c = t * EXTRA_COLS
                nc.tensor.matmul(bank_lin[:, c:c + EXTRA_COLS], posT[:, 0, t], hot_x, start=True, stop=False)
                nc.tensor.matmul(bank_lin[:, c:c + EXTRA_COLS], ones_f[:], xt[0:32, 2], start=False, stop=True)
                nc.tensor.matmul(bank_lin[:, SEQ + c:SEQ + c + EXTRA_COLS], posT[:, 1, t], hot_x, start=True, stop=True)
            nc.tensor.matmul(bank_lin[0:1, 128:128 + EXTRA_COLS], iota_e[:, 0:1], hot_x, start=True, stop=True)
            nc.tensor.matmul(bank_lin[0:1, 128 + EXTRA_COLS:128 + EXTRA_COLS + 1], ones_f[:, 0:1],
                             extra[0:32, 0:1], start=True, stop=True
                             ).then_inc(list_ready, 1)
            pe.wait_ge(meta_ready, 1)
            pe.wait_ge(const_built, 15)
            for b in range(4):
                ins = nc.tensor.matmul(acc[b][:], zeros_bf[:, 0:P], zeros_bf[:], start=True, stop=True)
            ins.then_inc(scattered, 1)

            def item(n):
                pe.wait_ge(xg_ready, n)
                pe.wait_ge(up_read, n)
                for k in range(KD):
                    pe.wait_ge(up_loaded[k], 16 * n)
                    for bank, c0 in ((bank_glu, 0), (bank_lin, FF)):
                        for half in range(2):
                            ins = nc.tensor.matmul(bank[64 * half:64 * half + 64, :], xgT[:, k],
                                                   w_up_ring[:, k, c0 + half * W:c0 + (half + 1) * W],
                                                   start=(k == 0), stop=False, skip_group_check=True)
                    ins.then_inc(up_used[k], 1)
                pe.wait_ge(bias_sel_ready, n)
                for bank, c0 in ((bank_glu, 0), (bank_lin, FF)):
                    for half in range(2):
                        ins = nc.tensor.matmul(bank[64 * half:64 * half + 64, :], bias_sel[:],
                                               bias_up[:, c0 + half * W:c0 + (half + 1) * W],
                                               start=False, stop=True, skip_group_check=True)
                ins.then_inc(up_done, 1)
                pe.wait_ge(pick_w_ready, n)
                pe.wait_ge(aT_ready, n)
                for t in range(NT):
                    ins = nc.tensor.transpose(bank_t[:, t * P:(t + 1) * P],
                                              pick_w[:, t].rearrange("p a s -> p (a s)"), ident[:])
                ins.then_inc(pick_wT_done, 1)
                pe.wait_ge(pick_ready, n + 1)
                pe.wait_ge(y_ready, n)
                gather()
                pe.wait_ge(a_ready, n)
                pe.wait_ge(pick_wT_ready, n)
                for j in range(KB):
                    ins = nc.tensor.transpose(bank_t[:, j * P:(j + 1) * P], a_tok[:, j * P:(j + 1) * P], ident[:])
                ins.then_inc(aT_done, 1)
                pe.wait_ge(aT_ready, n + 1)
                pe.wait_ge(xg_ready, n + 1)
                for half in range(2):
                    nc.tensor.matmul(bank_cy[64 * half:64 * half + 64, :], bias_sel[:],
                                     bias_down[:, half * W:(half + 1) * W], start=True, stop=False,
                                     skip_group_check=True)
                for m in range(KD):
                    if m % 2 == 0:
                        pe.wait_ge(down_loaded[m // 2], 16 * n)
                    j, ff_half = m % KB, m // KB
                    for half in range(2):
                        ins = nc.tensor.matmul(bank_cy[64 * half:64 * half + 64, :],
                                               aT[:, j, 64 * ff_half:64 * ff_half + 64],
                                               w_down_ring[:, m, half * W:(half + 1) * W],
                                               start=False, stop=(m == KD - 1), skip_group_check=True)
                    if m % 2:
                        ins.then_inc(down_used[m // 2] if m < KD - 1 else y_done, 1)
                pe.wait_ge(y_ready, n + 1)
                for t in range(NT):
                    for half in range(2):
                        s = slice(64 * half, 64 * half + 64)
                        ins = nc.tensor.matmul(acc[2 * t + half][:], pick_wT[s, t], y_sb[s, :],
                                               start=False, stop=True, skip_group_check=True)
                ins.then_inc(scattered, 1)

            with pe.Fori(1, NEXP + 1) as n:
                item(n)
            more = pe.value_load(meta[0:1, EXTRA_COLS:EXTRA_COLS + 1], min_val=0, max_val=EXTRA)
            with pe.If(more > 0):
                with pe.Fori(NEXP + 1, NEXP + 1 + more) as n:
                    item(n)


def kernel(**inputs):
    import numpy as np
    import concourse.bacc as bacc
    from concourse.bass_utils import run_bass_kernel_spmd

    a = {name: np.ascontiguousarray(value) for name, value in inputs.items()}
    cols = np.zeros((P, NCOLS), np.float32)
    for c, name in ((C_G1, "norm1_g"), (C_GM, "mem_norm_g"), (C_G2, "norm2_g")):
        cols[:, c:c + KD] = a[name][0].reshape(KD, P).T
    for j in range(3):
        cols[:, C_CONV + j * KB:C_CONV + (j + 1) * KB] = a["conv_w"][0, j].reshape(KB, P).T
    cols[:, C_XQ], cols[:, C_XK] = a["xa_q_g"][0], a["xa_k_g"][0]
    cols[:FOX_D, C_FQ], cols[:FOX_D, C_FK] = a["fox_q_g"][0], a["fox_k_g"][0]
    spread = np.ascontiguousarray(np.broadcast_to(
        np.concatenate([a["b_forget"][0], a["b_router"][0]])[None, :], (P, FOX_H + NEXP)))

    def by_row(w):
        return np.ascontiguousarray(w.reshape(KD, P, -1).transpose(1, 0, 2))

    arrays = {
        "x": a["x"][0], "mem": a["mem"][0], "w_in": a["w_in"][0], "w_kv": a["w_mem_kv"][0],
        "w_branch": a["w_branch"][0], "w_out": a["w_out"][0], "w_up": a["w_up"][0], "w_down": a["w_down"][0],
        "cols": cols, "spread": spread, "wf": by_row(a["w_in"][0][:, 3 * W:3 * W + FOX_H]),
        "wr": by_row(a["w_router"][0]), "b_gate": a["b_gate"][0], "b_up": a["b_up"][0], "b_down": a["b_down"][0],
    }
    nc = bacc.Bacc("TRN2", target_bir_lowering=False, num_devices=1)
    args = [nc.dram_tensor(f"{name}_dram", v.shape, mybir.dt.from_np(v.dtype), kind="ExternalInput").ap()
            for name, v in arrays.items()]
    args.append(nc.dram_tensor("out_dram", (SEQ, D), F32, kind="ExternalOutput").ap())
    hybrid_block(nc, *args)
    got = run_bass_kernel_spmd(nc, [{f"{name}_dram": v for name, v in arrays.items()}], core_ids=[0])
    return got.results[0]["out_dram"].reshape(1, SEQ, D)
```

```python
from contextlib import ExitStack

import concourse.bass as bass
from concourse import mybir

F32 = mybir.dt.float32
F32R = mybir.dt.float32r
BF16 = mybir.dt.bfloat16
I32 = mybir.dt.int32
U32 = mybir.dt.uint32
ALU = mybir.AluOpType
ACT = mybir.ActivationFunctionType
AX = mybir.AxisListType.X

P = 128
SEQ = 256
NT = SEQ // P
D = 1024
KD = D // P
W = 512
KB = W // P
FOX_H, FOX_D = 8, 64
MEM_H, MEM_D = 4, 128
NEXP, TOPK, FF = 32, 4, 1024
NORM_EPS, QK_EPS = 1e-5, 1e-6
ALPHA, LIMIT = 1.702, 7.0
SLOTS = 64
EXTRA = (SEQ * TOPK - 1) // SLOTS
EXTRA_COLS = EXTRA + 1
TABLE = NEXP + EXTRA_COLS + 4
NEG = -1.0e30

C_G1, C_GM, C_G2, C_CONV = 0, 8, 16, 24
C_XQ, C_XK, C_FQ, C_FK = 36, 37, 38, 39
NCOLS = 40

R_NEG, R_POS, R_END = 64, 96, 104


def blocks_and_pieces():
    blocks = [("q",), ("k",), ("v",), ("mk",), ("mv",), ("xq",), ("cu",), ("cc",), ("cb",)]
    for branch in (1, 2, 0):
        for half in range(2):
            blocks += [("gate", branch, half), ("proj", branch, half)]
    pieces = []
    for b in blocks:
        pieces += [(b, 0)] if b[0] == "proj" else [(b, 0), (b, 1)]
    blocks += [("out", 0), ("out", 1)]
    pieces += [(("out", 0), 0), (("out", 1), 0), (("out", 0), 1), (("out", 1), 1)]
    return blocks, pieces


BLOCKS, PIECES = blocks_and_pieces()
NP = len(PIECES)
BLOCK_NO = {b: n for n, b in enumerate(BLOCKS)}
LAST_PIECE = {}
for _p, (_b, _h) in enumerate(PIECES):
    LAST_PIECE[_b] = _p


def auxiliary_jobs():
    jobs = [(-1, "hT", g) for g in range(4)]
    jobs += [(0, "logit_f", 0)]
    jobs += [(1, "mT", g) for g in range(4)]
    jobs += [(2, "cum", 0)]
    jobs += [(3, "qT", g) for g in range(4)]
    jobs += [(5, "kT", g) for g in range(4)]
    jobs += [(6 + h, "fox_s", h) for h in range(FOX_H)]
    jobs += [(7 + h, "fox_pT", h) for h in range(FOX_H)]
    jobs += [(8 + h, "fox_y", h) for h in range(FOX_H)]
    jobs += [(9, "mkT", g) for g in range(2)]
    jobs += [(13, "xqT", g) for g in range(2)]
    jobs += [(14 + h, "mem_s", h) for h in range(MEM_H)]
    jobs += [(15 + h, "mem_pT", h) for h in range(MEM_H)]
    jobs += [(16 + h, "mem_y", h) for h in range(MEM_H)]
    jobs += [(33, "zT", g) for g in range(2)]
    jobs += [(36, "zT", g) for g in range(2, 4)]
    return sorted(jobs, key=lambda j: j[0])


JOBS = auxiliary_jobs()
JOB = {(kind, arg): n for n, (_, kind, arg) in enumerate(JOBS)}
SPLIT_JOBS = [n for n, (_, kind, _) in enumerate(JOBS) if kind in ("hT", "mT", "fox_y", "mem_y", "zT")]
SPLIT_NO = {n: i for i, n in enumerate(SPLIT_JOBS)}
SMAX = [("fox", h) for h in range(FOX_H)] + [("mem", h) for h in range(MEM_H)]
SMAX_NO = {x: n for n, x in enumerate(SMAX)}


CONSTANTS = ["ident", "q_clear", "k_clear", "k_ones", "f_cols", "fox_gain", "xa_gain", "q_hot", "mask0", "mask1",
             "gate_sel", "tri_strict", "block_tri0", "block_tri1", "block_tri2", "iota", "iota_e", "ones_f",
             "tables"]


def built(name):
    return CONSTANTS.index(name) + 1


BYTES = {F32: 4, F32R: 4, BF16: 2, I32: 4, U32: 4}


class Region:

    def __init__(self, nc, start, end):
        self.nc, self.at, self.end = nc, start, end

    def place(self, name, shape, dt):
        size = BYTES[dt]
        for n in shape[1:]:
            size *= n
        tile = self.nc.alloc_sbuf_tensor_at(name, shape, dt, offset=self.at)
        self.at += -(-size // 32) * 32
        assert self.at <= self.end, (name, self.at, self.end)
        return tile


def jobs_at(step):
    return [(n, kind, arg) for n, (s, kind, arg) in enumerate(JOBS) if s == step]


def hybrid_block(nc, x_d, mem_d, w_in, w_kv, w_branch, w_out, w_up, w_down,
                 cols_d, spread_d, wf_d, wr_d, b_gate, b_up, b_down, out):
    ctx = ExitStack()
    with ctx:
        def sb(name, shape, dt, where=None):
            return (where or always).place(name, shape, dt)

        def sem(name):
            return ctx.enter_context(nc.semaphore(name))

        base, top = -(-nc.sbuf_base // 32) * 32, nc.sbuf_base + nc.sbuf_bytes_remaining
        up_bytes = KD * 2 * FF * 4
        raw_bytes = 4 * KB * W * 4
        always = Region(nc, base, top)
        ident = sb("ident", [P, P], F32)
        x1 = sb("x1", [P, NT, D], F32)
        cols = sb("cols", [P, NCOLS], F32)
        qcols = sb("qcols", [P, 2], F32)
        spread = sb("spread", [P, 40], F32)
        iota = sb("iota", [P, SLOTS], F32)
        ss = sb("ss", [P, 7, 16], F32)
        ms = sb("ms", [P, 7, 16], F32)
        rstd = sb("rstd", [P, 7, 16], F32)
        minus_half = sb("minus_half", [P, 16], F32)
        bias_up = sb("bias_up", [96, 2 * FF], BF16)
        bias_down = sb("bias_down", [96, D], BF16)
        ident_rep = sb("ident_rep", [96, NEXP], BF16)
        tri_strict = sb("tri_strict", [P, P], BF16)
        block_tri = sb("block_tri", [96, 96], BF16)
        ones_bf = sb("ones_bf", [P, P], BF16)
        ones_f = sb("ones_f", [32, P], F32)
        iota_e = sb("iota_e", [32, 2], F32)

        start_u = always.at
        u = Region(nc, start_u, start_u + up_bytes)
        mT_hi = sb("mT_hi", [P, KD, SEQ], F32R, u)
        mT_lo = sb("mT_lo", [P, KD, SEQ], F32R, u)
        q_rows = sb("q_rows", [P, FOX_H, SEQ], F32, u)
        k_rows = sb("k_rows", [P, FOX_H, SEQ], F32, u)
        tok = sb("tok", [P, 2, NT, W], F32, u)
        xqT = sb("xqT", [P, MEM_H, SEQ], F32, u)
        mkT = sb("mkT", [P, MEM_H, SEQ], F32, u)
        v_tok = sb("v_tok", [P, NT, W], F32, u)
        mv_tok = sb("mv_tok", [P, NT, W], F32, u)
        score = sb("score", [P, 2, W], F32, u)
        pT = sb("pT", [P, 2, W], F32, u)
        v = Region(nc, start_u, start_u + 2 * KD * SEQ * 4)
        conv_cu = sb("conv_cu", [P, KB, SEQ], F32, v)
        conv_out = sb("conv_out", [P, KB, SEQ], F32, v)
        conv_u = sb("conv_u", [P, KB, SEQ + 2], F32, v)
        u2 = Region(nc, start_u, start_u + up_bytes)
        w_up_ring = sb("w_up_ring", [P, KD, 2 * FF], F32, u2)
        start_d = u2.at
        raw = sb("raw", [P, 4, KB, W], F32, Region(nc, start_d, start_d + raw_bytes))
        w_down_ring = raw[:].rearrange("p a b n -> p (a b n)").rearrange("p (k n) -> p k n", n=D)

        start_r = start_d + raw_bytes
        r = Region(nc, start_r, top)
        w_hi = sb("w_hi", [P, 4, 2, W], F32R, r)
        w_lo = sb("w_lo", [P, 4, 2, W], F32R, r)
        hT_hi = sb("hT_hi", [P, KD, SEQ], F32R, r)
        hT_lo = sb("hT_lo", [P, KD, SEQ], F32R, r)
        start_y = r.at
        y_conv_hi = sb("y_conv_hi", [P, KB, SEQ], F32R, r)
        y_conv_lo = sb("y_conv_lo", [P, KB, SEQ], F32R, r)
        end_y = r.at
        yT_hi = [sb("y_fox_hi", [P, KB, SEQ], F32R, r), y_conv_hi, sb("y_mem_hi", [P, KB, SEQ], F32R, r)]
        yT_lo = [sb("y_fox_lo", [P, KB, SEQ], F32R, r), y_conv_lo, sb("y_mem_lo", [P, KB, SEQ], F32R, r)]
        y = Region(nc, start_y, end_y)
        mask = sb("mask", [P, 3 * P], F32, y)
        tri_ones = sb("tri_ones", [P, SEQ], F32, y)
        head_hot = sb("head_hot", [P, FOX_H], F32, y)
        f_cols = sb("f_cols", [P, NT, R_END], F32, y)
        f_tmp = sb("f_tmp", [P, 4, NT, FOX_H], F32, y)
        wf = sb("wf", [P, KD, FOX_H], F32, y)
        wf_hi = sb("wf_hi", [P, KD, FOX_H], F32R, y)
        wf_lo = sb("wf_lo", [P, KD, FOX_H], F32R, y)
        merged = sb("merged", [P, NT, D], F32, r)
        end_merged = r.at
        gate = sb("gate", [P, NT, W], F32, r)
        prob = sb("prob", [P, 2, W], F32, r)
        nmax = sb("nmax", [P, 2, 2], F32, r)
        den = sb("den", [P, 2, 2], F32, r)
        rden = sb("rden", [P, 2, 2], F32, r)
        gate_sel = sb("gate_sel", [96, 3, P], BF16, r)
        bias_gate = sb("bias_gate", [96, D], BF16, r)
        b_raw = sb("b_raw", [96, W], F32, r)
        b_mid = sb("b_mid", [96, W], BF16, r)
        xs = merged
        w_up_next = sb("w_up_next", [P, KD // 2, 2 * FF], F32, Region(nc, start_y, end_merged))
        g = Region(nc, end_merged, top)
        h2T = sb("h2T", [P, KD, SEQ], F32, g)
        wr = sb("wr", [P, KD, NEXP], F32, g)
        zeros_bf = sb("zeros_bf", [P, W], BF16, g)
        pos_tab = sb("pos_tab", [P, NT, TABLE], F32, g)
        comb_tab = sb("comb_tab", [P, NT, TABLE], F32, g)
        exp_sel = sb("exp_sel", [96, TABLE], F32, g)
        m = Region(nc, start_r, start_y)
        m_parts = sb("m_parts", [P, 3, NT, D], BF16, m)
        x1s = sb("x1s", [P, NT, D], F32, m)
        xgT = sb("xgT", [P, KD, SLOTS], F32, m)
        glu = sb("glu", [P, W], F32, m)
        lin = sb("lin", [P, W], F32, m)
        glin = sb("glin", [P, W], F32, m)
        sig = sb("sig", [P, W], F32, m)
        a_tok = sb("a_tok", [P, W], F32, m)
        aT = sb("aT", [P, KB, P], F32, m)
        y_sb = sb("y_sb", [P, W], F32, m)
        pick = sb("pick", [P, NT, SLOTS], BF16, m)
        pick_w = sb("pick_w", [P, NT, 2, SLOTS], F32, m)
        pick_wT = sb("pick_wT", [P, NT, P], F32, m)
        bias_sel = sb("bias_sel", [96, SLOTS], BF16, m)
        logits = sb("logits", [P, NT, NEXP], F32, m)
        top_v = sb("top_v", [P, NT, 8], F32, m)
        top_i = sb("top_i", [P, NT, 8], U32, m)
        top_f = sb("top_f", [P, NT, 8], F32, m)
        top_e = sb("top_e", [P, NT, TOPK], F32, m)
        top_den = sb("top_den", [P, NT, 2], F32, m)
        ntop = sb("ntop", [P, NT], F32, m)
        hot4 = sb("hot4", [P, NT, TOPK, NEXP], F32, m)
        hot4w = sb("hot4w", [P, NT, TOPK, NEXP], F32, m)
        chosen = sb("chosen", [P, NT, NEXP], F32, m)
        chosen3 = sb("chosen3", [P, NT, 3, NEXP], BF16, m)
        count = sb("count", [96, 4], F32, m)
        extra = sb("extra", [96, 2], F32, m)
        extra_bf = sb("extra_bf", [96, 2], BF16, m)
        first = sb("first", [96, 2], F32, m)
        xt = sb("xt", [96, 3, EXTRA_COLS], F32, m)
        posT = sb("posT", [32, 2, NT, P], F32, m)
        meta = sb("meta", [1, EXTRA_COLS + 1], I32, m)

        acc = [ctx.enter_context(nc.psum_tensor(f"acc{b}", [P, W], F32)) for b in range(4)]
        aux = [ctx.enter_context(nc.psum_tensor(f"aux{b}", [P, W], F32)) for b in range(4)]
        bank_glu, bank_lin, bank_cy, bank_t = aux

        x_loaded = [sem(f"x_loaded{t}") for t in range(NT)]
        mem_loaded = [sem(f"mem_loaded{t}") for t in range(NT)]
        params_loaded = sem("params_loaded")
        brow_loaded = sem("brow_loaded")
        brow_used = sem("brow_used")
        raw_loaded = [sem(f"raw_loaded{s}") for s in range(4)]
        const_built = sem("const_built")
        ss_ready = [sem(f"ss_ready{n}") for n in range(6)]
        rstd_ready = sem("rstd_ready")
        pool_step = sem("pool_step")
        xs_ready = sem("xs_ready")
        hi_done = sem("hi_done")
        lo_done = sem("lo_done")
        half_used = sem("half_used")
        wf_hi_done = sem("wf_hi_done")
        wf_lo_done = sem("wf_lo_done")
        block_free = [sem(f"block_free{s}") for s in range(2)]
        aux_ready = sem("aux_ready")
        aux_free = [sem(f"aux_free{b}") for b in range(4)]
        part_hi = sem("part_hi")
        squares = sem("squares")
        forget_neg = sem("forget_neg")
        forget_log = sem("forget_log")
        forget_ready = sem("forget_ready")
        k_cum_ready = sem("k_cum_ready")
        max_ready = sem("max_ready")
        exp_ready = sem("exp_ready")
        prob_ready = sem("prob_ready")
        conv_y = sem("conv_y")
        conv_hi = sem("conv_hi")
        merged_done = sem("merged_done")
        last_tile0 = sem("last_tile0")
        x1_ready = sem("x1_ready")
        x1_squared = sem("x1_squared")
        act_step = sem("act_step")
        dve_step = sem("dve_step")
        wr_loaded = sem("wr_loaded")
        x1s_ready = sem("x1s_ready")
        x1T_ready = sem("x1T_ready")
        h2T_act = sem("h2T_act")
        h2T_dve = sem("h2T_dve")
        logits_ready = sem("logits_ready")
        parts_act = sem("parts_act")
        parts_pool = sem("parts_pool")
        parts_dve = sem("parts_dve")
        top_ready = sem("top_ready")
        soft_ready = sem("soft_ready")
        chosen_ready = sem("chosen_ready")
        slots_ready = sem("slots_ready")
        extra_ready = sem("extra_ready")
        first_ready = sem("first_ready")
        table_ready = sem("table_ready")
        list_ready = sem("list_ready")
        xtab_ready = sem("xtab_ready")
        meta_ready = sem("meta_ready")
        up_loaded = [sem(f"up_loaded{k}") for k in range(KD)]
        up_used = [sem(f"up_used{k}") for k in range(KD - 1)]
        down_loaded = [sem(f"down_loaded{m}") for m in range(4)]
        down_used = [sem(f"down_used{m}") for m in range(3)]
        pick_ready = sem("pick_ready")
        pick_w_ready = sem("pick_w_ready")
        bias_sel_ready = sem("bias_sel_ready")
        gathered = sem("gathered")
        xg_ready = sem("xg_ready")
        up_done = sem("up_done")
        up_read = sem("up_read")
        glu_ready = sem("glu_ready")
        glin_ready = sem("glin_ready")
        sig_ready = sem("sig_ready")
        a_ready = sem("a_ready")
        pick_wT_done = sem("pick_wT_done")
        pick_wT_ready = sem("pick_wT_ready")
        aT_done = sem("aT_done")
        aT_ready = sem("aT_ready")
        y_done = sem("y_done")
        y_ready = sem("y_ready")
        scattered = sem("scattered")
        out_ready = sem("out_ready")
        stored = sem("stored")

        def block_done(eng, b):
            eng.wait_ge(half_used, 2 * LAST_PIECE[b] + 2)

        def block_read(eng, b):
            eng.wait_ge(block_free[BLOCK_NO[b] % 2], BLOCK_NO[b] // 2 + 1)

        mem_sb = tok[:].rearrange("p a t n -> p (a t n)").rearrange("p (t n) -> p t n", t=NT)

        def piece_source(p):
            block, half = PIECES[p]
            kind = block[0]
            rows = slice(half * KB * P, (half + 1) * KB * P)
            if kind in ("mk", "mv"):
                c = {"mk": 0, "mv": W}[kind]
                src = w_kv[rows, c:c + W]
            elif kind == "gate":
                c = 7 * W + FOX_H + block[1] * D + block[2] * W
                src = w_in[rows, c:c + W]
            elif kind == "proj":
                src = w_branch[block[1], :, block[2] * W:(block[2] + 1) * W]
            elif kind == "out":
                src = w_out[rows, block[1] * W:(block[1] + 1) * W]
            else:
                c = {"q": 0, "k": W, "v": 2 * W, "cu": 3 * W + FOX_H, "cc": 4 * W + FOX_H,
                     "cb": 5 * W + FOX_H, "xq": 6 * W + FOX_H}[kind]
                src = w_in[rows, c:c + W]
            return src.rearrange("(k p) n -> p k n", p=P)

        bias_chunks = [(b_up, bias_up, c) for c in range(4)] + [(b_down, bias_down, c) for c in range(2)]
        bias_chunks = [(b_gate, bias_gate, c) for c in range(2)] + bias_chunks

        block = ctx.enter_context(nc.Block())

        @block.sync
        def _(sp):
            def load_piece(p):
                if p >= 4:
                    sp.wait_ge(lo_done, 2 * (p - 4) + 2)
                sp.dma_start(raw[:, p % 4], piece_source(p)).then_inc(raw_loaded[p % 4], 16)

            for t in range(NT):
                sp.dma_start(x1[:, t], x_d[t * P:(t + 1) * P, :]).then_inc(x_loaded[t], 16)
            load_piece(0)
            for t in range(NT):
                sp.dma_start(mem_sb[:, t], mem_d[t * P:(t + 1) * P, :]).then_inc(mem_loaded[t], 16)
            for p in range(1, NP):
                load_piece(p)
                if 27 <= p < 27 + KD:
                    if p == 27:
                        sp.wait_ge(aux_ready, JOB["mem_y", MEM_H - 1] + 1)
                        block_read(sp, ("cb",))
                    k = p - 27
                    sp.dma_start(w_up_ring[:, k], w_up[0, k * P:(k + 1) * P, :]).then_inc(up_loaded[k], 16)
            def load_up(k, expert, buffer):
                sp.dma_start(buffer, w_up[bass.ds(expert, 1), k * P:(k + 1) * P, :].rearrange("o p n -> p (o n)")
                             ).then_inc(up_loaded[k], 16)

            def load_down(m, expert):
                sp.dma_start(w_down_ring[:, 2 * m:2 * m + 2],
                             w_down[bass.ds(expert, 1), 2 * m * P:(2 * m + 2) * P, :]
                             .rearrange("o (k p) n -> p (o k) n", p=P)).then_inc(down_loaded[m], 16)

            def up_slot_free(k, items):
                sp.wait_ge(up_used[k] if k < KD - 1 else up_done, items)

            def down_slot_free(m, items):
                sp.wait_ge(down_used[m] if m < 3 else y_done, items)

            sp.wait_ge(aux_ready, JOB["zT", 3] + 1)
            for k in range(KD // 2, KD):
                sp.wait_ge(up_loaded[k], 16)
                load_up(k, 1, w_up_next[:, k - KD // 2])
            for m in range(4):
                last = max(p for p in range(NP) if p % 4 == m)
                sp.wait_ge(lo_done, 2 * last + 2)
                load_down(m, 0)
            for k in range(KD // 2):
                up_slot_free(k, 1)
                load_up(k, 1, w_up_ring[:, k])
            for k in range(KD // 2, KD):
                sp.wait_ge(up_loaded[k], 2 * 16)
                up_slot_free(k, 1)
                load_up(k, 2, w_up_ring[:, k])
            for m in range(4):
                down_slot_free(m, 1)
                load_down(m, 1)
            for k in range(KD // 2):
                up_slot_free(k, 2)
                load_up(k, 2, w_up_ring[:, k])
            for m in range(4):
                down_slot_free(m, 2)
                load_down(m, 2)

            def load_item(expert, before):
                for k in range(KD):
                    up_slot_free(k, before)
                    load_up(k, expert, w_up_ring[:, k])
                for m in range(4):
                    down_slot_free(m, before)
                    load_down(m, expert)

            with sp.Fori(4, NEXP + 1) as n:
                before = sp.snap(sp.to_reg(n - 1), min_val=3, max_val=NEXP - 1)
                load_item(before, before)
            sp.wait_ge(meta_ready, 1)
            more = sp.value_load(meta[0:1, EXTRA_COLS:EXTRA_COLS + 1], min_val=0, max_val=EXTRA)
            with sp.If(more > 0):
                with sp.Fori(NEXP + 1, NEXP + 1 + more) as n:
                    expert = sp.value_load(meta[0:1, bass.ds(n - (NEXP + 1), 1)], min_val=0, max_val=NEXP - 1)
                    before = sp.snap(sp.to_reg(n - 1), min_val=NEXP, max_val=NEXP + EXTRA)
                    load_item(expert, before)
            for t in range(NT):
                for h in range(2):
                    sp.wait_ge(out_ready, 2 * t + h + 1)
                    sp.dma_start(out[t * P:(t + 1) * P, h * W:(h + 1) * W],
                                 x1[:, t, h * W:(h + 1) * W]).then_inc(stored, 16)
            sp.wait_ge(stored, 16 * 2 * NT)

        @block.gpsimd
        def _(pool):
            steps = [0]

            def chained(ins):
                steps[0] += 1
                ins.then_inc(pool_step, 1)
                pool.wait_ge(pool_step, steps[0])

            order = iter(CONSTANTS)

            def constant(name, ins):
                assert next(order) == name
                ins.then_inc(const_built, 1)
                pool.wait_ge(const_built, built(name))

            chained(nc.gpsimd.memset(minus_half[:], -0.5))
            chained(nc.gpsimd.memset(ident[:], 0.0))
            constant("ident", nc.gpsimd.affine_select(out=ident[:], in_=ident[:], compare_op=ALU.not_equal, fill=1.0,
                                                      base=0, pattern=[[-1, P]], channel_multiplier=1))
            constant("q_clear", nc.gpsimd.memset(q_rows[64:P], 0.0))
            constant("k_clear", nc.gpsimd.memset(k_rows[64:P], 0.0))

            def rstd_of(n, width, count, eps):
                pool.wait_ge(ss_ready[n], 1)
                chained(nc.gpsimd.tensor_scalar(ms[:, n, 0:count], ss[:, n, 0:count], 1.0 / width, eps,
                                                ALU.mult, ALU.add))
                nc.gpsimd.tensor_tensor(rstd[:, n, 0:count], ms[:, n, 0:count], minus_half[:, 0:count],
                                        ALU.pow).then_inc(rstd_ready, 1)
                pool.wait_ge(rstd_ready, n + 1)

            rstd_of(0, D, 2, NORM_EPS)
            chained(nc.gpsimd.memset(head_hot[:], 0.0))
            for row in (R_NEG, R_POS):
                hot = head_hot[row:row + FOX_H]
                chained(nc.gpsimd.affine_select(out=hot, in_=hot, compare_op=ALU.not_equal, fill=1.0,
                                                base=0, pattern=[[-1, FOX_H]], channel_multiplier=1))
            constant("k_ones", nc.gpsimd.memset(k_rows[R_POS:R_END], 1.0))
            chained(nc.gpsimd.memset(tri_ones[:], 1.0))
            chained(nc.gpsimd.affine_select(out=tri_ones[:], in_=tri_ones[:], compare_op=ALU.is_ge, fill=0.0,
                                            base=0, pattern=[[1, SEQ]], channel_multiplier=-1))
            constant("f_cols", nc.gpsimd.memset(f_cols[:], 0.0))
            pool.wait_ge(params_loaded, 16 * 3)
            constant("fox_gain", nc.gpsimd.tensor_scalar(qcols[:, 0:1], cols[:, C_FQ:C_FQ + 1], FOX_D ** -0.5, None,
                                                         ALU.mult))
            constant("xa_gain", nc.gpsimd.tensor_scalar(qcols[:, 1:2], cols[:, C_XQ:C_XQ + 1], MEM_D ** -0.5, None,
                                                        ALU.mult))
            rstd_of(1, D, 2, NORM_EPS)
            constant("q_hot", nc.gpsimd.tensor_copy(
                q_rows[R_NEG:R_NEG + FOX_H],
                head_hot[R_NEG:R_NEG + FOX_H].unsqueeze(2).to_broadcast([FOX_H, FOX_H, SEQ])))
            chained(nc.gpsimd.memset(mask[:], 0.0))
            for name, c in (("mask0", 0), ("mask1", 2 * P)):
                constant(name, nc.gpsimd.affine_select(out=mask[:, c:c + P], in_=mask[:, c:c + P],
                                                       compare_op=ALU.is_ge, fill=NEG, base=0, pattern=[[-1, P]],
                                                       channel_multiplier=1))
            chained(nc.gpsimd.memset(ones_bf[:], 1.0))
            chained(nc.gpsimd.memset(ident_rep[:], 0.0))
            for g in range(3):
                rep = ident_rep[32 * g:32 * g + 32]
                chained(nc.gpsimd.affine_select(out=rep, in_=rep, compare_op=ALU.not_equal, fill=1.0,
                                                base=0, pattern=[[-1, NEXP]], channel_multiplier=1))
            constant("gate_sel", nc.gpsimd.tensor_copy(gate_sel[:],
                                                       ident_rep[:, 0:3].unsqueeze(2).to_broadcast([96, 3, P])))
            rstd_of(2, FOX_D, 16, QK_EPS)
            rstd_of(3, FOX_D, 16, QK_EPS)

            for n, (src, dst, c) in enumerate(bias_chunks):
                if n == 2:
                    rstd_of(4, MEM_D, 8, QK_EPS)
                if n == 4:
                    rstd_of(5, MEM_D, 8, QK_EPS)
                pool.wait_ge(brow_loaded, 16 * 3 * (n + 1))
                part = dst[:, c * W:(c + 1) * W]
                chained(nc.gpsimd.tensor_copy(part, b_raw[:]))
                chained(nc.gpsimd.tensor_tensor(b_raw[:], b_raw[:], part, ALU.subtract))
                chained(nc.gpsimd.tensor_copy(b_mid[:], b_raw[:]))
                chained(nc.gpsimd.tensor_copy(part[32:64], b_mid[32:64]))
                nc.gpsimd.tensor_tensor(part[64:96], b_raw[64:96], b_mid[64:96],
                                        ALU.subtract).then_inc(brow_used, 1)
                pool.wait_ge(brow_used, n + 1)
            chained(nc.gpsimd.memset(tri_strict[:], 1.0))
            chained(nc.gpsimd.memset(block_tri[:], 0.0))
            constant("tri_strict", nc.gpsimd.affine_select(out=tri_strict[:], in_=tri_strict[:], compare_op=ALU.is_ge, fill=0.0,
                                             base=-1, pattern=[[1, P]], channel_multiplier=-1))
            for g in range(3):
                s = slice(32 * g, 32 * g + 32)
                constant(f"block_tri{g}", nc.gpsimd.affine_select(out=block_tri[s, s], in_=ones_bf[s, 0:32], compare_op=ALU.is_ge,
                                                 fill=0.0, base=-1, pattern=[[1, 32]], channel_multiplier=-1))
            constant("iota", nc.gpsimd.iota(iota[:], pattern=[[1, SLOTS]], base=0, channel_multiplier=0,
                                    allow_small_or_imprecise_dtypes=True))
            constant("iota_e", nc.gpsimd.iota(iota_e[:], pattern=[[0, 2]], base=0, channel_multiplier=1,
                                    allow_small_or_imprecise_dtypes=True))
            constant("ones_f", nc.gpsimd.memset(ones_f[:], 1.0))

            pool.wait_ge(merged_done, 4)
            chained(nc.gpsimd.memset(zeros_bf[:], 0.0))
            chained(nc.gpsimd.memset(pos_tab[:], -1.0))
            chained(nc.gpsimd.memset(comb_tab[:], 0.0))
            chained(nc.gpsimd.memset(exp_sel[:], 0.0))
            constant("tables", nc.gpsimd.tensor_copy(exp_sel[:, 0:NEXP], ident_rep[:]))
            pool.wait_ge(x1_squared, 4)
            halves = ss[:, 6, 0:2 * NT].rearrange("p (t h) -> p t h", h=2)
            chained(nc.gpsimd.tensor_tensor(ms[:, 6, 0:NT], halves[:, :, 0], halves[:, :, 1], ALU.add))
            chained(nc.gpsimd.tensor_scalar(ms[:, 6, 0:NT], ms[:, 6, 0:NT], 1.0 / D, NORM_EPS, ALU.mult, ALU.add))
            nc.gpsimd.tensor_tensor(rstd[:, 6, 0:NT], ms[:, 6, 0:NT], minus_half[:, 0:NT], ALU.pow
                                    ).then_inc(rstd_ready, 1)
            pool.wait_ge(parts_act, 1)
            nc.gpsimd.tensor_tensor(x1s[:, 0], x1s[:, 0], m_parts[:, 0, 0], ALU.subtract).then_inc(parts_pool, 1)
            pool.wait_ge(parts_pool, 1)
            for t in range(NT):
                pool.wait_ge(parts_act, NT + t + 1)
                nc.gpsimd.tensor_tensor(m_parts[:, 2, t], x1s[:, t], m_parts[:, 1, t],
                                        ALU.subtract).then_inc(parts_pool, 1)
                pool.wait_ge(parts_pool, t + 2)

        @block.scalar
        def _(act):
            act.dma_start(cols[:], cols_d).then_inc(params_loaded, 16)
            act.dma_start(spread[:], spread_d).then_inc(params_loaded, 16)
            act.dma_start(wf[:], wf_d).then_inc(params_loaded, 16)

            def bias_rows(n):
                src, _, c = bias_chunks[n]
                rows = src.shape[0]
                if n == 0:
                    act.wait_ge(act_step, 1)
                else:
                    act.wait_ge(brow_used, n)
                for g in range(3):
                    act.dma_start(b_raw[32 * g:32 * g + rows], src[:, c * W:(c + 1) * W]).then_inc(brow_loaded, 16)

            def split_hi(p, halves=(0, 1)):
                for h in halves:
                    s = 2 * p + h
                    if h == 0:
                        act.wait_ge(raw_loaded[p % 4], 16 * (p // 4 + 1))
                    if s >= 4:
                        act.wait_ge(half_used, s - 3)
                    nc.scalar.activation(w_hi[:, s % 4], raw[:, p % 4, 2 * h:2 * h + 2], ACT.Copy).then_inc(hi_done, 1)

            scratch = [tile[:].rearrange("p t n -> p (t n)") for tile in (gate, prob)]
            for t in range(NT):
                act.wait_ge(x_loaded[t], 16)
                ins = nc.scalar.activation(xs[:, t], x1[:, t], ACT.Square, accum_out=ss[:, 0, t:t + 1])
            ins.then_inc(ss_ready[0], 1)
            act.wait_ge(params_loaded, 16 * 3)
            nc.scalar.activation(wf_hi[:], wf[:], ACT.Copy).then_inc(wf_hi_done, 1)

            def finish_job(j, kind, arg):
                bank = aux[j % 4]
                free = aux_free[j % 4]
                if kind in ("hT", "mT"):
                    hi, g = (hT_hi, C_G1) if kind == "hT" else (mT_hi, C_GM)
                    act.wait_ge(aux_ready, j + 1)
                    for i in range(2):
                        k = 2 * arg + i
                        ins = nc.scalar.activation(hi[:, k], bank[:, i * SEQ:(i + 1) * SEQ], ACT.Copy,
                                                   scale=cols[:, g + k:g + k + 1])
                    ins.then_inc(part_hi, 1)
                elif kind in ("qT", "kT"):
                    dst, scale = (q_rows, qcols[0:FOX_D, 0:1]) if kind == "qT" else \
                                 (k_rows, cols[0:FOX_D, C_FK:C_FK + 1])
                    act.wait_ge(const_built, built("xa_gain"))
                    act.wait_ge(aux_ready, j + 1)
                    nc.scalar.activation(dst[0:FOX_D, 2 * arg:2 * arg + 2], bank[0:FOX_D, :].rearrange(
                        "p (h s) -> p h s", h=2), ACT.Copy, scale=scale).then_inc(free, 1)
                elif kind in ("mkT", "xqT"):
                    dst, scale = (mkT, cols[:, C_XK:C_XK + 1]) if kind == "mkT" else (xqT, qcols[:, 1:2])
                    act.wait_ge(aux_ready, j + 1)
                    nc.scalar.activation(dst[:, 2 * arg:2 * arg + 2], bank[:, :].rearrange("p (h s) -> p h s", h=2),
                                         ACT.Copy, scale=scale).then_inc(free, 1)
                elif kind == "logit_f":
                    act.wait_ge(forget_neg, 1)
                    nc.scalar.activation(f_tmp[:, 2], f_tmp[:, 1], ACT.Exp).then_inc(act_step, 1)
                    act.wait_ge(act_step, 2)
                    nc.scalar.activation(f_tmp[:, 3], f_tmp[:, 2], ACT.Ln, bias=1.0).then_inc(forget_log, 1)
                elif kind == "cum":
                    act.wait_ge(const_built, built("k_ones"))
                    act.wait_ge(aux_ready, j + 1)
                    s = slice(R_NEG, R_NEG + FOX_H)
                    nc.scalar.activation(k_rows[s], bank[s, 0:SEQ].unsqueeze(1).to_broadcast([FOX_H, FOX_H, SEQ]),
                                         ACT.Copy).then_inc(k_cum_ready, 1)
                elif kind in ("fox_s", "mem_s"):
                    n = SMAX_NO[kind[:3], arg]
                    act.wait_ge(max_ready, n + 1)
                    if n >= 2:
                        old = SMAX[n - 2]
                        act.wait_ge(aux_ready, JOB[old[0] + "_pT", old[1]] + 1)
                    edges = (0, P, 3 * P) if kind == "fox_s" else (0, SEQ, 2 * SEQ)
                    for t in range(NT):
                        c = slice(edges[t], edges[t + 1])
                        nc.scalar.activation(prob[:, n % 2, c], score[:, n % 2, c], ACT.Exp,
                                             bias=nmax[:, n % 2, t:t + 1],
                                             accum_out=den[:, n % 2, t:t + 1]).then_inc(exp_ready, 1)
                elif kind in ("fox_pT", "mem_pT"):
                    n = SMAX_NO[kind[:3], arg]
                    width = 3 * P if kind == "fox_pT" else W
                    act.wait_ge(aux_ready, j + 1)
                    if n >= 2:
                        old = SMAX[n - 2]
                        act.wait_ge(aux_ready, JOB[old[0] + "_y", old[1]] + 1)
                    nc.scalar.activation(pT[:, n % 2, 0:width], bank[:, 0:width], ACT.Copy).then_inc(free, 1)
                elif kind == "fox_y":
                    act.wait_ge(aux_ready, j + 1)
                    s = slice(64 * (arg % 2), 64 * (arg % 2) + 64)
                    nc.scalar.activation(yT_hi[0][s, arg // 2], bank[s, 0:SEQ], ACT.Copy).then_inc(part_hi, 1)
                elif kind == "mem_y":
                    act.wait_ge(aux_ready, j + 1)
                    nc.scalar.activation(yT_hi[2][:, arg], bank[:, 0:SEQ], ACT.Copy).then_inc(part_hi, 1)
                elif kind == "zT":
                    act.wait_ge(aux_ready, j + 1)
                    nc.scalar.activation(hT_hi[:, 2 * arg:2 * arg + 2], bank[:].rearrange("p (k s) -> p k s", k=2),
                                         ACT.Copy).then_inc(part_hi, 1)

            def finish_block(b):
                n = BLOCK_NO[b]
                banks = acc[2 * (n % 2):2 * (n % 2) + 2]
                kind = b[0]
                if kind in ("q", "k", "mk", "xq"):
                    block_done(act, b)
                    m = {"q": 2, "k": 3, "mk": 4, "xq": 5}[kind]
                    if m > 2:
                        act.wait_ge(ss_ready[m - 1], 1)
                    for t in range(NT):
                        nc.scalar.activation(gate[:, t], banks[t][:], ACT.Square).then_inc(squares, 1)
                elif kind in ("v", "mv"):
                    block_done(act, b)
                    dst = v_tok if kind == "v" else mv_tok
                    for t in range(NT):
                        ins = nc.scalar.activation(dst[:, t], banks[t][:], ACT.Copy)
                    ins.then_inc(block_free[n % 2], 1)
                elif kind == "cu":
                    block_done(act, b)
                    for i in range(2):
                        ins = nc.scalar.activation(conv_cu[:, 2 * i:2 * i + 2],
                                                   banks[i][:].rearrange("p (c s) -> p c s", c=2), ACT.Copy)
                    ins.then_inc(block_free[n % 2], 1)
                elif kind == "cb":
                    act.wait_ge(conv_y, 1)
                    nc.scalar.activation(yT_hi[1][:], conv_out[:], ACT.Copy).then_inc(conv_hi, 1)
                elif kind == "gate":
                    block_done(act, b)
                    g = (n - BLOCK_NO[("gate", 1, 0)]) // 2
                    if g == 0:
                        act.wait_ge(ss_ready[5], 1)
                    elif g <= 2:
                        block_read(act, BLOCKS[n - 1])
                    else:
                        act.wait_ge(merged_done, g - 2)
                    for t in range(NT):
                        ins = nc.scalar.activation(gate[:, t], banks[t][:], ACT.Sigmoid)
                    ins.then_inc(block_free[n % 2], 1)

            bias_steps = [3, 5, 9, 11, 14, 16, 18, 20]
            for step in range(0, NP):
                if step == 0:
                    for h in range(2):
                        split_hi(0, (h,))
                        for j, kind, arg in jobs_at(-1)[2 * h:2 * h + 2]:
                            finish_job(j, kind, arg)
                    for t in range(NT):
                        act.wait_ge(mem_loaded[t], 16)
                        ins = nc.scalar.activation(scratch[t], mem_sb[:, t], ACT.Square, accum_out=ss[:, 1, t:t + 1])
                    ins.then_inc(ss_ready[1], 1)
                    nc.scalar.activation(b_raw[:], ident[0:96, 0:1].to_broadcast([96, W]), ACT.Copy,
                                         scale=0.0).then_inc(act_step, 1)
                if step + 1 < NP:
                    split_hi(step + 1)
                if step > 0:
                    for j, kind, arg in jobs_at(step - 1):
                        finish_job(j, kind, arg)
                for b in BLOCKS:
                    if LAST_PIECE[b] == step - 1:
                        finish_block(b)
                if step in bias_steps:
                    bias_rows(bias_steps.index(step))

            act.wait_ge(merged_done, 4)
            act.wait_ge(brow_used, len(bias_chunks))
            act.dma_start(wr[:], wr_d).then_inc(wr_loaded, 16)
            for h in range(2):
                for t in range(NT):
                    act.wait_ge(x1_ready, 2 * h + t + 1)
                    nc.scalar.activation(acc[2 * (1 - h) + t][:], x1[:, t, h * W:(h + 1) * W], ACT.Square,
                                         accum_out=ss[:, 6, 2 * t + h:2 * t + h + 1]).then_inc(x1_squared, 1)
                g = 2 * h
                act.wait_ge(x1T_ready, g + 1)
                for k in (2 * g, 2 * g + 1):
                    ins = nc.scalar.activation(h2T[:, k], aux[g][:, (k % 2) * SEQ:(k % 2 + 1) * SEQ], ACT.Copy,
                                               scale=cols[:, C_G2 + k:C_G2 + k + 1])
                ins.then_inc(h2T_act, 1)
            for t in range(NT):
                act.wait_ge(x1s_ready, t + 1)
                nc.scalar.activation(m_parts[:, 0, t], x1s[:, t], ACT.Copy).then_inc(parts_act, 1)
            for t in range(NT):
                if t == 0:
                    act.wait_ge(parts_pool, 1)
                else:
                    act.wait_ge(parts_dve, 1)
                nc.scalar.activation(m_parts[:, 1, t], x1s[:, t], ACT.Copy).then_inc(parts_act, 1)
            act.wait_ge(top_ready, 1)
            for t in range(NT):
                nc.scalar.activation(top_e[:, t], top_v[:, t, 0:TOPK], ACT.Exp, bias=ntop[:, t:t + 1],
                                     accum_out=top_den[:, t, 0:1]).then_inc(soft_ready, 1)

            nc.scalar.activation(aT[:, 0], ident[:], ACT.Copy).then_inc(aT_ready, 1)
            nc.scalar.activation(y_sb[:, 0:P], ident[:], ACT.Copy).then_inc(y_ready, 1)

            def item(n):
                act.wait_ge(glu_ready, n)
                nc.scalar.activation(sig[:], glu[:], ACT.Sigmoid, scale=ALPHA).then_inc(sig_ready, 1)
                act.wait_ge(aT_done, n)
                nc.scalar.activation(aT[:].rearrange("p k s -> p (k s)"), bank_t[:], ACT.Copy).then_inc(aT_ready, 1)
                act.wait_ge(pick_wT_done, n)
                act.wait_ge(scattered, 4 * n)
                nc.scalar.activation(pick_wT[:].rearrange("p t s -> p (t s)"), bank_t[:, 0:NT * P],
                                     ACT.Copy).then_inc(pick_wT_ready, 1)
                act.wait_ge(y_done, n)
                nc.scalar.activation(y_sb[:], bank_cy[:], ACT.Copy).then_inc(y_ready, 1)

            with act.Fori(1, NEXP + 1) as n:
                item(n)
            act.wait_ge(meta_ready, 1)
            more = act.value_load(meta[0:1, EXTRA_COLS:EXTRA_COLS + 1], min_val=0, max_val=EXTRA)
            with act.If(more > 0):
                with act.Fori(NEXP + 1, NEXP + 1 + more) as n:
                    item(n)

        @block.vector
        def _(dve):
            steps = [0]

            def chained(ins):
                steps[0] += 1
                ins.then_inc(dve_step, 1)
                dve.wait_ge(dve_step, steps[0])

            def plain_f32(ap):
                return ap.bitcast(F32)

            def split_lo(p, halves=(0, 1)):
                for h in halves:
                    s = 2 * p + h
                    dve.wait_ge(hi_done, s + 1)
                    nc.vector.tensor_tensor(w_lo[:, s % 4], raw[:, p % 4, 2 * h:2 * h + 2],
                                            plain_f32(w_hi[:, s % 4]), ALU.subtract).then_inc(lo_done, 1)


            def finish_job(j, kind, arg):
                bank = aux[j % 4]
                free = aux_free[j % 4]
                if kind in ("hT", "mT"):
                    hi, lo, g = (hT_hi, hT_lo, C_G1) if kind == "hT" else (mT_hi, mT_lo, C_GM)
                    dve.wait_ge(part_hi, SPLIT_NO[j] + 1)
                    for i in range(2):
                        k = 2 * arg + i
                        ins = nc.vector.scalar_tensor_tensor(lo[:, k], bank[:, i * SEQ:(i + 1) * SEQ],
                                                             cols[:, g + k:g + k + 1], plain_f32(hi[:, k]),
                                                             ALU.mult, ALU.subtract)
                    ins.then_inc(free, 1)
                elif kind == "logit_f":
                    dve.wait_ge(aux_ready, j + 1)
                    dve.wait_ge(params_loaded, 16 * 3)
                    nc.vector.tensor_tensor(
                        f_tmp[:, 0], bank[:, 0:NT * FOX_H].rearrange("p (t h) -> p t h", t=NT),
                        spread[:, 0:FOX_H].unsqueeze(1).to_broadcast([P, NT, FOX_H]), ALU.add).then_inc(free, 1)
                    dve.wait_ge(free, j // 4 + 1)
                    nc.vector.scalar_tensor_tensor(f_tmp[:, 1], f_tmp[:, 0], -1.0, f_tmp[:, 0],
                                                   ALU.mult, ALU.min).then_inc(forget_neg, 1)
                    dve.wait_ge(forget_log, 1)
                    dve.wait_ge(const_built, built("f_cols"))
                    nc.vector.scalar_tensor_tensor(f_cols[:, :, R_NEG:R_NEG + FOX_H], f_tmp[:, 0], 0.0, f_tmp[:, 3],
                                                   ALU.min, ALU.subtract).then_inc(dve_step, 1)
                    steps[0] += 1
                    nc.vector.scalar_tensor_tensor(f_cols[:, :, R_POS:R_END], f_tmp[:, 0], 0.0, f_tmp[:, 3],
                                                   ALU.min, ALU.subtract).then_inc(dve_step, 1)
                    steps[0] += 1
                    dve.wait_ge(dve_step, steps[0])
                    nc.vector.tensor_scalar(f_cols[:, :, R_NEG:R_NEG + FOX_H], f_cols[:, :, R_NEG:R_NEG + FOX_H],
                                            -1.0, None, ALU.mult).then_inc(forget_ready, 1)
                elif kind == "cum":
                    dve.wait_ge(const_built, built("q_hot"))
                    dve.wait_ge(k_cum_ready, 1)
                    s = slice(R_POS, R_END)
                    nc.vector.tensor_tensor(
                        q_rows[s], bank[s, 0:SEQ].unsqueeze(1).to_broadcast([FOX_H, FOX_H, SEQ]),
                        head_hot[s].unsqueeze(2).to_broadcast([FOX_H, FOX_H, SEQ]), ALU.mult).then_inc(free, 1)
                elif kind in ("fox_s", "mem_s"):
                    n = SMAX_NO[kind[:3], arg]
                    edges = (0, P, 3 * P) if kind == "fox_s" else (0, SEQ, 2 * SEQ)
                    if n >= 2:
                        dve.wait_ge(exp_ready, 2 * (n - 2) + 2)
                    dve.wait_ge(aux_ready, j + 1)
                    if kind == "fox_s":
                        dve.wait_ge(const_built, built("mask1"))
                        nc.vector.tensor_tensor(score[:, n % 2, 0:3 * P], bank[:, 0:3 * P], mask[:],
                                                ALU.add).then_inc(free, 1)
                    else:
                        nc.vector.tensor_copy(score[:, n % 2], bank[:]).then_inc(free, 1)
                    dve.wait_ge(free, j // 4 + 1)
                    for t in range(NT):
                        ins = nc.vector.tensor_reduce(nmax[:, n % 2, t:t + 1], score[:, n % 2, edges[t]:edges[t + 1]],
                                                      AX, ALU.max, negate=True)
                    ins.then_inc(max_ready, 1)
                elif kind in ("fox_y", "mem_y"):
                    dve.wait_ge(part_hi, SPLIT_NO[j] + 1)
                    if kind == "fox_y":
                        s = slice(64 * (arg % 2), 64 * (arg % 2) + 64)
                        b, part = 0, (s, arg // 2)
                    else:
                        s = slice(0, P)
                        b, part = 2, (s, arg)
                    nc.vector.tensor_tensor(yT_lo[b][part], bank[s, 0:SEQ], plain_f32(yT_hi[b][part]),
                                            ALU.subtract).then_inc(free, 1)
                elif kind == "zT":
                    dve.wait_ge(part_hi, SPLIT_NO[j] + 1)
                    k = slice(2 * arg, 2 * arg + 2)
                    nc.vector.tensor_tensor(hT_lo[:, k], bank[:].rearrange("p (k s) -> p k s", k=2),
                                            plain_f32(hT_hi[:, k]), ALU.subtract).then_inc(free, 1)

            def normalise_probs(kind, arg):
                n = SMAX_NO[kind[:3], arg]
                edges = (0, P, 3 * P) if kind == "fox_s" else (0, SEQ, 2 * SEQ)
                dve.wait_ge(exp_ready, 2 * n + 2)
                chained(nc.vector.reciprocal(rden[:, n % 2], den[:, n % 2]))
                for t in range(NT):
                    c = slice(edges[t], edges[t + 1])
                    ins = nc.vector.tensor_scalar(prob[:, n % 2, c], prob[:, n % 2, c], rden[:, n % 2, t:t + 1],
                                                  None, ALU.mult)
                ins.then_inc(prob_ready, 1)

            norm_blocks = {"q": (2, 0), "k": (3, 1), "mk": (4, 0), "xq": (5, 1)}

            def block_squares(b):
                n, _ = norm_blocks[b[0]]
                heads = FOX_H if n < 4 else MEM_H
                for t in range(NT):
                    dve.wait_ge(squares, 2 * (n - 2) + t + 1)
                    ins = nc.vector.tensor_reduce(ss[:, n, t * heads:(t + 1) * heads],
                                                  gate[:, t].rearrange("p (h d) -> p h d", h=heads), AX, ALU.add)
                ins.then_inc(ss_ready[n], 1)

            def block_scale(b):
                n, where = norm_blocks[b[0]]
                no = BLOCK_NO[b]
                banks = acc[2 * (no % 2):2 * (no % 2) + 2]
                heads = FOX_H if n < 4 else MEM_H
                width = W // heads
                dve.wait_ge(rstd_ready, n + 1)
                if n == 2:
                    dve.wait_ge(xs_ready, 4)
                if n >= 4:
                    dve.wait_ge(aux_ready, JOB[{4: "qT", 5: "kT"}[n], 3] + 1)
                for t in range(NT):
                    ins = nc.vector.tensor_tensor(
                        tok[:, where, t].rearrange("p (h d) -> p h d", h=heads),
                        banks[t][:].rearrange("p (h d) -> p h d", h=heads),
                        rstd[:, n, t * heads:(t + 1) * heads].unsqueeze(2).to_broadcast([P, heads, width]), ALU.mult)
                ins.then_inc(block_free[no % 2], 1)

            def finish_block(b):
                n = BLOCK_NO[b]
                banks = acc[2 * (n % 2):2 * (n % 2) + 2]
                kind = b[0]
                if kind == "cc":
                    block_read(dve, ("cu",))
                    nc.vector.memset(conv_u[:, :, 0:2], 0.0).then_inc(dve_step, 1)
                    steps[0] += 1
                    block_done(dve, b)
                    for i in range(2):
                        ins = nc.vector.tensor_tensor(conv_u[:, 2 * i:2 * i + 2, 2:2 + SEQ],
                                                      banks[i][:].rearrange("p (c s) -> p c s", c=2),
                                                      conv_cu[:, 2 * i:2 * i + 2], ALU.mult)
                    ins.then_inc(block_free[n % 2], 1)
                    block_read(dve, b)
                    dve.wait_ge(dve_step, steps[0])
                    for c in range(KB):
                        tap = cols[:, C_CONV + c:C_CONV + c + 1]
                        nc.vector.tensor_scalar(conv_out[:, c], conv_u[:, c, 0:SEQ], tap, None,
                                                ALU.mult).then_inc(dve_step, 1)
                        steps[0] += 1
                    for j in (1, 2):
                        dve.wait_ge(dve_step, steps[0])
                        for c in range(KB):
                            tap = cols[:, C_CONV + j * KB + c:C_CONV + j * KB + c + 1]
                            nc.vector.scalar_tensor_tensor(conv_out[:, c], conv_u[:, c, j:j + SEQ], tap,
                                                           conv_out[:, c], ALU.mult, ALU.add).then_inc(dve_step, 1)
                            steps[0] += 1
                elif kind == "cb":
                    dve.wait_ge(dve_step, steps[0])
                    block_done(dve, b)
                    for i in range(2):
                        s = slice(2 * i, 2 * i + 2)
                        ins = nc.vector.tensor_tensor(conv_out[:, s], banks[i][:].rearrange("p (c s) -> p c s", c=2),
                                                      conv_out[:, s], ALU.mult)
                    ins.then_inc(conv_y, 1)
                    dve.wait_ge(conv_hi, 1)
                    nc.vector.tensor_tensor(yT_lo[1][:], conv_out[:], plain_f32(yT_hi[1][:]),
                                            ALU.subtract).then_inc(block_free[n % 2], 1)
                elif kind == "proj":
                    g = (n - BLOCK_NO[("proj", 1, 0)]) // 2
                    half = slice(b[2] * W, (b[2] + 1) * W)
                    block_read(dve, BLOCKS[n - 1])
                    block_done(dve, b)
                    if g < 2:
                        for t in range(NT):
                            ins = nc.vector.tensor_tensor(merged[:, t, half], banks[t][:], gate[:, t], ALU.mult)
                        ins.then_inc(block_free[n % 2], 1)
                    else:
                        for t in range(NT):
                            ins = nc.vector.tensor_tensor(gate[:, t], banks[t][:], gate[:, t], ALU.mult)
                        ins.then_inc(block_free[n % 2], 1)
                        block_read(dve, b)
                        for t in range(NT):
                            ins = nc.vector.tensor_tensor(merged[:, t, half], merged[:, t, half], gate[:, t], ALU.add)
                        ins.then_inc(merged_done, 1)
                elif kind == "out":
                    half = slice(b[1] * W, (b[1] + 1) * W)
                    for t in range(NT):
                        if b[1] == 1 and t == 0:
                            dve.wait_ge(last_tile0, 1)
                        else:
                            block_done(dve, b)
                        nc.vector.tensor_tensor(x1[:, t, half], banks[t][:], x1[:, t, half],
                                                ALU.add).then_inc(x1_ready, 1)

            dve.wait_ge(rstd_ready, 1)
            for t in range(NT):
                nc.vector.tensor_scalar(xs[:, t], x1[:, t], rstd[:, 0, t:t + 1], None, ALU.mult).then_inc(xs_ready, 1)
            dve.wait_ge(wf_hi_done, 1)
            nc.vector.tensor_tensor(wf_lo[:], wf[:], plain_f32(wf_hi[:]), ALU.subtract).then_inc(wf_lo_done, 1)
            for h in range(2):
                split_lo(0, (h,))
                for j, kind, arg in jobs_at(-1)[2 * h:2 * h + 2]:
                    finish_job(j, kind, arg)
            for step in range(0, NP):
                here = jobs_at(step - 1)
                for j, kind, arg in here:
                    if kind in ("fox_s", "mem_s"):
                        finish_job(j, kind, arg)
                done = [b for b in BLOCKS if LAST_PIECE[b] == step - 1]
                if step + 1 < NP:
                    split_lo(step + 1)
                for b in done:
                    if b[0] in norm_blocks:
                        block_squares(b)
                for j, kind, arg in here:
                    if kind in ("fox_s", "mem_s"):
                        normalise_probs(kind, arg)
                    elif kind != "hT":
                        finish_job(j, kind, arg)
                for b in done:
                    if b[0] in norm_blocks:
                        block_scale(b)
                    else:
                        finish_block(b)
                if step == 0:
                    dve.wait_ge(rstd_ready, 2)
                    dve.wait_ge(aux_ready, JOB["hT", 3] + 1)
                    for t in range(NT):
                        nc.vector.tensor_scalar(xs[:, t], mem_sb[:, t], rstd[:, 1, t:t + 1], None,
                                                ALU.mult).then_inc(xs_ready, 1)

            def move_x1T(g):
                dve.wait_ge(x1T_ready, g + 1)
                for k in (2 * g, 2 * g + 1):
                    ins = nc.vector.tensor_scalar(h2T[:, k], aux[g][:, (k % 2) * SEQ:(k % 2 + 1) * SEQ],
                                                  cols[:, C_G2 + k:C_G2 + k + 1], None, ALU.mult)
                ins.then_inc(h2T_dve, 1)

            def scale_x1(t):
                nc.vector.tensor_scalar(x1s[:, t], x1[:, t], rstd[:, 6, t:t + 1], None, ALU.mult).then_inc(x1s_ready, 1)

            move_x1T(1)
            finish_block(("out", 1))
            dve.wait_ge(rstd_ready, 7)
            scale_x1(0)
            move_x1T(3)
            scale_x1(1)
            dve.wait_ge(parts_act, 2)
            nc.vector.tensor_tensor(x1s[:, 1], x1s[:, 1], m_parts[:, 0, 1], ALU.subtract).then_inc(parts_dve, 1)
            dve.wait_ge(logits_ready, 1)
            for t in range(NT):
                ins = nc.vector.scalar_tensor_tensor(logits[:, t], acc[2][:, t * NEXP:(t + 1) * NEXP],
                                                     rstd[:, 6, t:t + 1], spread[:, 8:40], ALU.mult, ALU.add)
            chained(ins)
            for t in range(NT):
                ins = nc.vector.max(top_v[:, t], logits[:, t])
            chained(ins)
            for t in range(NT):
                ins = nc.vector.max_index(top_i[:, t], top_v[:, t], logits[:, t])
            chained(ins)
            chained(nc.vector.tensor_copy(top_f[:], top_i[:]))
            dve.wait_ge(const_built, built("ones_f"))
            wide4 = [P, NT, TOPK, NEXP]
            chained(nc.vector.tensor_tensor(hot4[:], iota[:, 0:NEXP].unsqueeze(1).unsqueeze(1).to_broadcast(wide4),
                                            top_f[:, :, 0:TOPK].unsqueeze(3).to_broadcast(wide4), ALU.is_equal))
            chained(nc.vector.tensor_reduce(chosen[:], hot4[:].rearrange("p t k e -> p t e k"), AX, ALU.add))
            for c in (slice(0, 1), slice(1, 3)):
                nc.vector.tensor_copy(chosen3[:, :, c], chosen[:].unsqueeze(2).to_broadcast(
                    [P, NT, c.stop - c.start, NEXP])).then_inc(chosen_ready, 1)
            nc.vector.tensor_scalar(ntop[:], top_v[:, :, 0], -1.0, None, ALU.mult).then_inc(top_ready, 1)
            dve.wait_ge(const_built, built("tables"))
            dve.wait_ge(slots_ready, 1)
            slots = acc[3][:, 0:NT * NEXP].rearrange("p (t e) -> p t e", t=NT)
            chained(nc.vector.scalar_tensor_tensor(pos_tab[:, :, 0:NEXP], slots, 1.0, chosen[:], ALU.add, ALU.mult))
            nc.vector.tensor_scalar(pos_tab[:, :, 0:NEXP], pos_tab[:, :, 0:NEXP], -1.0, None,
                                    ALU.add).then_inc(table_ready, 1)
            dve.wait_ge(table_ready, 1)

            def build_pick(col):
                for t in range(NT):
                    ins = nc.vector.tensor_scalar(pick[:, t], iota[:], pos_tab[:, t, col], None, ALU.is_equal)
                ins.then_inc(pick_ready, 1)

            def build_pick_w(col):
                for t in range(NT):
                    ins = nc.vector.tensor_scalar(pick_w[:, t], iota[:].unsqueeze(1).to_broadcast([P, 2, SLOTS]),
                                                  pos_tab[:, t, col], comb_tab[:, t, col], ALU.is_equal, ALU.mult)
                ins.then_inc(pick_w_ready, 1)

            def build_bias_sel(col):
                nc.vector.tensor_scalar(bias_sel[:], ones_bf[0:96, 0:SLOTS], exp_sel[:, col], None,
                                        ALU.mult).then_inc(bias_sel_ready, 1)

            def move_gathered():
                nc.vector.tensor_tensor(xgT[:], bank_cy[:].rearrange("p (k s) -> p k s", k=KD),
                                        cols[:, C_G2:C_G2 + KD].unsqueeze(2).to_broadcast([P, KD, SLOTS]),
                                        ALU.mult).then_inc(xg_ready, 1)

            build_pick(slice(0, 1))
            build_bias_sel(slice(0, 1))
            dve.wait_ge(slots_ready, 2)
            nc.vector.tensor_copy(count[:, 0:1], bank_glu[0:96, 0:1]).then_inc(extra_ready, 1)
            dve.wait_ge(soft_ready, 2)
            chained(nc.vector.reciprocal(top_den[:, :, 1:2], top_den[:, :, 0:1]))
            chained(nc.vector.tensor_tensor(top_e[:], top_e[:], top_den[:, :, 1:2].to_broadcast([P, NT, TOPK]),
                                            ALU.mult))
            chained(nc.vector.tensor_tensor(hot4w[:], hot4[:], top_e[:].unsqueeze(3).to_broadcast(wide4), ALU.mult))
            nc.vector.tensor_reduce(comb_tab[:, :, 0:NEXP], hot4w[:].rearrange("p t k e -> p t e k"),
                                    AX, ALU.add).then_inc(table_ready, 1)
            nc.vector.memset(glu[:, 0:1], 0.0).then_inc(up_read, 1)
            dve.wait_ge(gathered, 1)
            move_gathered()
            build_pick(slice(1, 2))
            dve.wait_ge(table_ready, 2)
            build_pick_w(slice(0, 1))
            dve.wait_ge(extra_ready, 1)
            chained(nc.vector.tensor_scalar(count[:, 1:2], count[:, 0:1], float(SLOTS), None, ALU.is_gt))
            chained(nc.vector.scalar_tensor_tensor(count[:, 2:3], count[:, 0:1], 2.0 * SLOTS, count[:, 1:2],
                                                   ALU.is_gt, ALU.add))
            chained(nc.vector.scalar_tensor_tensor(extra[:, 0:1], count[:, 0:1], 3.0 * SLOTS, count[:, 2:3],
                                                   ALU.is_gt, ALU.add))
            nc.vector.tensor_copy(extra_bf[:], extra[:, 0:1].to_broadcast([96, 2])).then_inc(extra_ready, 1)

            def column(c):
                return slice(c, c + 1) if isinstance(c, int) else bass.ds(c, 1)

            def item(n):
                dve.wait_ge(up_done, n)
                nc.vector.tensor_scalar(glu[:], bank_glu[:], LIMIT, None, ALU.min).then_inc(glu_ready, 1)
                nc.vector.tensor_scalar(lin[:], bank_lin[:], LIMIT, -LIMIT, ALU.min, ALU.max).then_inc(up_read, 1)
                dve.wait_ge(glu_ready, n)
                dve.wait_ge(up_read, n + 1)
                nc.vector.scalar_tensor_tensor(glin[:], lin[:], 1.0, glu[:], ALU.add, ALU.mult
                                               ).then_inc(glin_ready, 1)
                dve.wait_ge(glin_ready, n)
                dve.wait_ge(sig_ready, n)
                nc.vector.tensor_tensor(a_tok[:], glin[:], sig[:], ALU.mult).then_inc(a_ready, 1)
                dve.wait_ge(gathered, n + 1)
                move_gathered()
                build_pick(column(n + 1))
                dve.wait_ge(pick_wT_done, n)
                build_pick_w(column(n))
                dve.wait_ge(y_done, n)
                build_bias_sel(column(n))

            item(1)
            dve.wait_ge(first_ready, 1)
            chained(nc.vector.tensor_copy(first[:, 0:1], bank_t[0:96, 0:1]))
            chained(nc.vector.tensor_scalar(xt[:, 0], iota[0:96, 0:EXTRA_COLS], first[:, 0:1], None, ALU.subtract))
            chained(nc.vector.tensor_scalar(xt[:, 1], xt[:, 0], 0.0, None, ALU.is_ge))
            chained(nc.vector.scalar_tensor_tensor(exp_sel[:, NEXP:NEXP + EXTRA_COLS], xt[:, 0], extra[:, 0:1],
                                                   xt[:, 1], ALU.is_lt, ALU.mult))
            chained(nc.vector.scalar_tensor_tensor(xt[:, 2], xt[:, 0], 1.0, exp_sel[:, NEXP:NEXP + EXTRA_COLS],
                                                   ALU.add, ALU.mult))
            chained(nc.vector.tensor_scalar(xt[:, 2], xt[:, 2], -float(SLOTS), None, ALU.mult))
            dve.wait_ge(list_ready, 1)
            nc.vector.tensor_copy(posT[:], bank_glu[0:32, :].rearrange("p (a t s) -> p a t s", a=2, t=NT)
                                  ).then_inc(xtab_ready, 1)
            dve.wait_ge(list_ready, 2)
            nc.vector.tensor_copy(pos_tab[:, :, NEXP:NEXP + EXTRA_COLS],
                                  bank_lin[:, 0:NT * EXTRA_COLS].rearrange("p (t j) -> p t j", t=NT))
            nc.vector.tensor_copy(comb_tab[:, :, NEXP:NEXP + EXTRA_COLS],
                                  bank_lin[:, SEQ:SEQ + NT * EXTRA_COLS].rearrange("p (t j) -> p t j", t=NT))
            nc.vector.tensor_copy(meta[0:1, :], bank_lin[0:1, 128:128 + EXTRA_COLS + 1]).then_inc(meta_ready, 1)
            dve.wait_ge(meta_ready, 1)

            with dve.Fori(2, NEXP + 1) as n:
                item(n)
            more = dve.value_load(meta[0:1, EXTRA_COLS:EXTRA_COLS + 1], min_val=0, max_val=EXTRA)
            with dve.If(more > 0):
                with dve.Fori(NEXP + 1, NEXP + 1 + more) as n:
                    item(n)
            for t in range(NT):
                for h in range(2):
                    dve.wait_ge(scattered, 4 * more + (4 * NEXP + 2 * t + h + 1))
                    s = slice(h * W, (h + 1) * W)
                    nc.vector.tensor_tensor(x1[:, t, s], acc[2 * t + h][:], x1[:, t, s], ALU.add).then_inc(out_ready, 1)

        @block.tensor
        def _(pe):
            def bank_of(j):
                if j >= 4:
                    pe.wait_ge(aux_free[j % 4], j // 4)
                return aux[j % 4]

            def job_read(kind, arg):
                j = JOB[kind, arg]
                pe.wait_ge(aux_free[j % 4], j // 4 + 1)

            def do_job(j, kind, arg):
                if kind in ("hT", "mT"):
                    pe.wait_ge(xs_ready, 2 if kind == "hT" else 4)
                    if kind == "hT":
                        pe.wait_ge(const_built, built("ident"))
                    bank = bank_of(j)
                    for i in range(2):
                        for t in range(NT):
                            k = 2 * arg + i
                            ins = nc.tensor.transpose(bank[:, i * SEQ + t * P:i * SEQ + (t + 1) * P],
                                                      xs[:, t, k * P:(k + 1) * P], ident[:])
                elif kind == "logit_f":
                    bank = bank_of(j)
                    pe.wait_ge(wf_lo_done, 1)
                    for g in range(4):
                        job_read("hT", g)
                    for t in range(NT):
                        s = slice(t * P, (t + 1) * P)
                        for k in range(KD):
                            for c, (a, w) in enumerate(((hT_hi, wf_hi), (hT_lo, wf_hi), (hT_hi, wf_lo))):
                                ins = nc.tensor.matmul(bank[:, t * FOX_H:(t + 1) * FOX_H], a[:, k, s], w[:, k],
                                                       start=(k == 0 and c == 0), stop=(k == KD - 1 and c == 2))
                elif kind == "cum":
                    bank = bank_of(j)
                    pe.wait_ge(forget_ready, 1)
                    nc.tensor.matmul(bank[0:R_END, 0:SEQ], f_cols[:, 0], tri_ones[:], start=True, stop=False,
                                     skip_group_check=True)
                    ins = nc.tensor.matmul(bank[0:R_END, P:SEQ], f_cols[:, 1], tri_ones[:, 0:P], start=False,
                                           stop=True, skip_group_check=True)
                elif kind in ("qT", "kT"):
                    bank = bank_of(j)
                    block_read(pe, (kind[0],))
                    for i in range(2):
                        h = 2 * arg + i
                        for t in range(NT):
                            ins = nc.tensor.transpose(bank[0:FOX_D, i * SEQ + t * P:i * SEQ + (t + 1) * P],
                                                      tok[:, 0 if kind == "qT" else 1, t, h * FOX_D:(h + 1) * FOX_D],
                                                      ident[:])
                elif kind in ("mkT", "xqT"):
                    bank = bank_of(j)
                    block_read(pe, (kind[:2],))
                    for i in range(2):
                        h = 2 * arg + i
                        for t in range(NT):
                            ins = nc.tensor.transpose(bank[:, i * SEQ + t * P:i * SEQ + (t + 1) * P],
                                                      tok[:, 0 if kind == "mkT" else 1, t, h * P:(h + 1) * P], ident[:])
                elif kind == "fox_s":
                    bank = bank_of(j)
                    if arg == 0:
                        job_read("qT", 3)
                        pe.wait_ge(const_built, built("q_hot"))
                        job_read("cum", 0)
                    if arg % 2 == 0:
                        job_read("kT", arg // 2)
                    nc.tensor.matmul(bank[:, 0:P], q_rows[0:R_END, arg, 0:P], k_rows[0:R_END, arg, 0:P],
                                     start=True, stop=True)
                    ins = nc.tensor.matmul(bank[:, P:3 * P], q_rows[0:R_END, arg, P:SEQ], k_rows[0:R_END, arg],
                                           start=True, stop=True)
                elif kind == "mem_s":
                    bank = bank_of(j)
                    if arg % 2 == 0:
                        job_read("xqT", arg // 2)
                        job_read("mkT", arg // 2)
                    for t in range(NT):
                        ins = nc.tensor.matmul(bank[:, t * SEQ:(t + 1) * SEQ], xqT[:, arg, t * P:(t + 1) * P],
                                               mkT[:, arg], start=True, stop=True)
                elif kind in ("fox_pT", "mem_pT"):
                    bank = bank_of(j)
                    n = SMAX_NO[kind[:3], arg]
                    pe.wait_ge(prob_ready, n + 1)
                    order = [0, 1, 2] if kind == "fox_pT" else [0, 2, 1, 3]
                    for i, c in enumerate(order):
                        ins = nc.tensor.transpose(bank[:, i * P:(i + 1) * P], prob[:, n % 2, c * P:(c + 1) * P],
                                                  ident[:])
                elif kind == "fox_y":
                    bank = bank_of(j)
                    if arg == 0:
                        block_read(pe, ("v",))
                    job_read("fox_pT", arg)
                    n = SMAX_NO["fox", arg]
                    s = slice(64 * (arg % 2), 64 * (arg % 2) + 64)
                    c = slice(arg * FOX_D, (arg + 1) * FOX_D)
                    nc.tensor.matmul(bank[s, 0:SEQ], v_tok[:, 0, c], pT[:, n % 2, 0:SEQ], start=True, stop=False,
                                     skip_group_check=True)
                    ins = nc.tensor.matmul(bank[s, P:SEQ], v_tok[:, 1, c], pT[:, n % 2, SEQ:3 * P], start=False,
                                           stop=True, skip_group_check=True)
                elif kind == "mem_y":
                    bank = bank_of(j)
                    if arg == 0:
                        block_read(pe, ("mv",))
                    job_read("mem_pT", arg)
                    n = SMAX_NO["mem", arg]
                    for t in range(NT):
                        ins = nc.tensor.matmul(bank[:, 0:SEQ], mv_tok[:, t, arg * P:(arg + 1) * P],
                                               pT[:, n % 2, t * SEQ:(t + 1) * SEQ], start=(t == 0), stop=(t == 1))
                elif kind == "zT":
                    bank = bank_of(j)
                    pe.wait_ge(merged_done, 3 if arg < 2 else 4)
                    for i in range(2):
                        for t in range(NT):
                            k = 2 * arg + i
                            ins = nc.tensor.transpose(bank[:, i * SEQ + t * P:i * SEQ + (t + 1) * P],
                                                      merged[:, t, k * P:(k + 1) * P], ident[:])
                ins.then_inc(aux_ready, 1)

            def piece(p):
                b, half = PIECES[p]
                kind = b[0]
                n = BLOCK_NO[b]
                banks = acc[2 * (n % 2):2 * (n % 2) + 2]
                last = p == LAST_PIECE[b]
                if half == 0 and n >= 2:
                    pe.wait_ge(block_free[n % 2], n // 2)
                if b == ("mk",) and half == 0:
                    job_read("mT", 3)
                if kind == "proj" and b[2] == 0:
                    if b[1] == 0:
                        for h in range(FOX_H):
                            job_read("fox_y", h)
                    elif b[1] == 1:
                        block_read(pe, ("cb",))
                    else:
                        for h in range(MEM_H):
                            job_read("mem_y", h)
                if kind == "out" and b[1] == 0:
                    job_read("zT", 2 * half)
                    job_read("zT", 2 * half + 1)
                if kind == "proj":
                    a_hi, a_lo = yT_hi[b[1]], yT_lo[b[1]]
                elif kind in ("mk", "mv"):
                    a_hi, a_lo = mT_hi, mT_lo
                else:
                    a_hi, a_lo = hT_hi, hT_lo
                if kind == "gate" and half == 0:
                    if n == BLOCK_NO[("gate", 1, 0)]:
                        pe.wait_ge(const_built, built("gate_sel"))
                        pe.wait_ge(brow_used, 2)
                    for t in range(NT):
                        nc.tensor.matmul(banks[t][:], gate_sel[:, b[1]], bias_gate[:, b[2] * W:(b[2] + 1) * W],
                                         start=True, stop=False)
                for h in range(2):
                    s = 2 * p + h
                    pe.wait_ge(lo_done, s + 1)
                    if p < 2:
                        job_read("hT", s)
                    if p == NP - 1 and h == 1:
                        for t in range(NT):
                            ts = slice(t * P, (t + 1) * P)
                            for i in range(2):
                                k = half * KB + 2 * h + i
                                wh, wl = w_hi[:, s % 4, i], w_lo[:, s % 4, i]
                                for m, (a_, w_) in enumerate(((hT_hi, wh), (hT_hi, wl), (hT_lo, wh))):
                                    ins = nc.tensor.matmul(banks[t][:], a_[:, k, ts], w_, start=False,
                                                           stop=i == 1 and m == 2)
                            ins.then_inc(half_used if t else last_tile0, 1)
                        continue
                    for i in range(2):
                        k = half * KB + 2 * h + i
                        opening = half == 0 and h == 0 and i == 0
                        closing = last and h == 1 and i == 1
                        wh, wl = w_hi[:, s % 4, i], w_lo[:, s % 4, i]
                        if kind in ("cu", "cc", "cb"):
                            for c in range(KB):
                                dst = banks[c // 2][:, (c % 2) * SEQ:(c % 2 + 1) * SEQ]
                                cs = slice(c * P, (c + 1) * P)
                                for m, (w_, a_) in enumerate(((wh, a_hi), (wh, a_lo), (wl, a_hi))):
                                    ins = nc.tensor.matmul(dst, w_[:, cs], a_[:, k],
                                                           start=opening and m == 0 and c % 2 == 0,
                                                           stop=closing and m == 2, skip_group_check=True)
                        else:
                            for t in range(NT):
                                ts = slice(t * P, (t + 1) * P)
                                for m, (a_, w_) in enumerate(((a_hi, wh), (a_hi, wl), (a_lo, wh))):
                                    ins = nc.tensor.matmul(banks[t][:], a_[:, k, ts], w_,
                                                           start=opening and m == 0 and kind != "gate",
                                                           stop=closing and m == 2)
                    ins.then_inc(half_used, 1)
                    if p == NP - 1:
                        transpose_x1(0)

            def transpose_x1(h):
                pe.wait_ge(x1_ready, 2 * h + 2)
                for g in (2 * h, 2 * h + 1):
                    pe.wait_ge(aux_free[g], len([j for j in range(len(JOBS)) if j % 4 == g]))
                    for i in range(2):
                        for t in range(NT):
                            k = 2 * g + i
                            ins = nc.tensor.transpose(aux[g][:, i * SEQ + t * P:i * SEQ + (t + 1) * P],
                                                      x1[:, t, k * P:(k + 1) * P], ident[:])
                    ins.then_inc(x1T_ready, 1)

            for j, kind, arg in jobs_at(-1):
                do_job(j, kind, arg)
            for p in range(NP):
                piece(p)
                for j, kind, arg in jobs_at(p):
                    do_job(j, kind, arg)

            def logit_products(t, h):
                for k in range(4 * h, 4 * h + 4):
                    ins = nc.tensor.matmul(acc[2][:, t * NEXP:(t + 1) * NEXP], h2T[:, k, t * P:(t + 1) * P], wr[:, k],
                                           start=(k == 0 and t == 0), stop=(k == KD - 1), skip_group_check=True)
                return ins

            pe.wait_ge(x1_squared, 2)
            pe.wait_ge(h2T_act, 1)
            pe.wait_ge(h2T_dve, 1)
            pe.wait_ge(wr_loaded, 16)
            logit_products(0, 0)
            transpose_x1(1)
            logit_products(1, 0)
            pe.wait_ge(h2T_act, 2)
            pe.wait_ge(h2T_dve, 2)
            for t in range(NT):
                ins = logit_products(t, 1)
            ins.then_inc(logits_ready, 1)
            pe.wait_ge(x1_squared, 4)
            pe.wait_ge(const_built, built("tables"))
            for b in range(2):
                nc.tensor.matmul(acc[b][:], zeros_bf[:, 0:P], zeros_bf[:], start=True, stop=True).then_inc(scattered, 1)
            pe.wait_ge(chosen_ready, 1)
            hot = [chosen3[:, t, 0] for t in range(NT)]
            nc.tensor.matmul(acc[3][:, 0:NEXP], tri_strict[:], hot[0], start=True, stop=True)
            nc.tensor.matmul(acc[3][:, NEXP:2 * NEXP], ones_bf[:], hot[0], start=True, stop=False)
            nc.tensor.matmul(acc[3][:, NEXP:2 * NEXP], tri_strict[:], hot[1], start=False, stop=True
                             ).then_inc(slots_ready, 1)
            pe.wait_ge(chosen_ready, 2)
            for t in range(NT):
                ins = nc.tensor.matmul(bank_glu[0:96, 0:2],
                                       chosen3[:, t].rearrange("p a e -> p (a e)"), ones_bf[:, 0:2],
                                       start=(t == 0), stop=(t == 1))
            ins.then_inc(slots_ready, 1)
            nc.tensor.matmul(acc[2][:], zeros_bf[:, 0:P], zeros_bf[:], start=True, stop=True).then_inc(scattered, 1)

            def gather():
                for k in range(KD):
                    for t in range(NT):
                        for m in range(3):
                            ins = nc.tensor.matmul(bank_cy[:, k * SLOTS:(k + 1) * SLOTS],
                                                   m_parts[:, m, t, k * P:(k + 1) * P], pick[:, t],
                                                   start=(t == 0 and m == 0), stop=(t == NT - 1 and m == 2))
                ins.then_inc(gathered, 1)

            pe.wait_ge(parts_pool, NT + 1)
            pe.wait_ge(pick_ready, 1)
            gather()
            pe.wait_ge(table_ready, 1)
            pe.wait_ge(extra_ready, 1)
            nc.tensor.matmul(acc[3][:], zeros_bf[:, 0:P], zeros_bf[:], start=True, stop=True).then_inc(scattered, 1)

            def scatter(items, banks):
                pe.wait_ge(y_ready, items)
                pe.wait_ge(pick_wT_ready, items - 1)
                for b in banks:
                    t, half = b // 2, b % 2
                    s = slice(64 * half, 64 * half + 64)
                    nc.tensor.matmul(acc[b][:], pick_wT[s, t], y_sb[s, :],
                                     start=False, stop=True, skip_group_check=True).then_inc(scattered, 1)

            def item(n, last_rows, first_item=False):
                pe.wait_ge(xg_ready, n)
                pe.wait_ge(up_read, n)
                for k in range(KD):
                    pe.wait_ge(up_loaded[k], 16 * n)
                    rows = (w_up_ring if k < KD // 2 else last_rows)[:, k if last_rows is w_up_ring else k % (KD // 2)]
                    for bank, c0 in ((bank_glu, 0), (bank_lin, FF)):
                        for half in range(2):
                            ins = nc.tensor.matmul(bank[64 * half:64 * half + 64, :], xgT[:, k],
                                                   rows[:, c0 + half * W:c0 + (half + 1) * W],
                                                   start=(k == 0), stop=(k == KD - 1), skip_group_check=True)
                    ins.then_inc(up_used[k] if k < KD - 1 else up_done, 1)
                    if k == 0:
                        pe.wait_ge(bias_sel_ready, n)
                        for bank, c0 in ((bank_glu, 0), (bank_lin, FF)):
                            for half in range(2):
                                nc.tensor.matmul(bank[64 * half:64 * half + 64, :], bias_sel[:],
                                                 bias_up[:, c0 + half * W:c0 + (half + 1) * W],
                                                 start=False, stop=False, skip_group_check=True)
                    if k == KD - 2:
                        pe.wait_ge(pick_ready, n + 1)
                        pe.wait_ge(y_ready, n)
                        gather()
                if not first_item:
                    scatter(n, range(3))
                pe.wait_ge(a_ready, n)
                if not first_item:
                    pe.wait_ge(pick_wT_ready, n - 1)
                for j in range(KB):
                    ins = nc.tensor.transpose(bank_t[:, j * P:(j + 1) * P], a_tok[:, j * P:(j + 1) * P], ident[:])
                ins.then_inc(aT_done, 1)
                if not first_item:
                    scatter(n, (3,))
                pe.wait_ge(pick_w_ready, n)
                pe.wait_ge(aT_ready, n + 1)
                for t in range(NT):
                    ins = nc.tensor.transpose(bank_t[:, t * P:(t + 1) * P],
                                              pick_w[:, t].rearrange("p a s -> p (a s)"), ident[:])
                ins.then_inc(pick_wT_done, 1)
                pe.wait_ge(xg_ready, n + 1)
                for half in range(2):
                    nc.tensor.matmul(bank_cy[64 * half:64 * half + 64, :], bias_sel[:],
                                     bias_down[:, half * W:(half + 1) * W], start=True, stop=False,
                                     skip_group_check=True)
                for m in range(KD):
                    if m % 2 == 0:
                        pe.wait_ge(down_loaded[m // 2], 16 * n)
                    j, ff_half = m % KB, m // KB
                    for half in range(2):
                        ins = nc.tensor.matmul(bank_cy[64 * half:64 * half + 64, :],
                                               aT[:, j, 64 * ff_half:64 * ff_half + 64],
                                               w_down_ring[:, m, half * W:(half + 1) * W],
                                               start=False, stop=(m == KD - 1), skip_group_check=True)
                    if m % 2:
                        ins.then_inc(down_used[m // 2] if m < KD - 1 else y_done, 1)
            item(1, w_up_ring, first_item=True)

            pe.wait_ge(extra_ready, 2)
            pe.wait_ge(pick_wT_ready, 1)
            nc.tensor.matmul(bank_t[0:96, 0:2], block_tri[:], extra_bf[:], start=True, stop=True
                             ).then_inc(first_ready, 1)
            pe.wait_ge(table_ready, 2)
            pe.wait_ge(up_read, 2)
            for a, tab in enumerate((pos_tab, comb_tab)):
                for t in range(NT):
                    c = (a * NT + t) * P
                    ins = nc.tensor.transpose(bank_glu[0:32, c:c + P], tab[:, t, 0:NEXP], ident[:])
            ins.then_inc(list_ready, 1)
            pe.wait_ge(xtab_ready, 1)
            hot_x = exp_sel[0:32, NEXP:NEXP + EXTRA_COLS]
            for t in range(NT):
                c = t * EXTRA_COLS
                nc.tensor.matmul(bank_lin[:, c:c + EXTRA_COLS], posT[:, 0, t], hot_x, start=True, stop=False)
                nc.tensor.matmul(bank_lin[:, c:c + EXTRA_COLS], ones_f[:], xt[0:32, 2], start=False, stop=True)
                nc.tensor.matmul(bank_lin[:, SEQ + c:SEQ + c + EXTRA_COLS], posT[:, 1, t], hot_x, start=True, stop=True)
            nc.tensor.matmul(bank_lin[0:1, 128:128 + EXTRA_COLS], iota_e[:, 0:1], hot_x, start=True, stop=True)
            nc.tensor.matmul(bank_lin[0:1, 128 + EXTRA_COLS:128 + EXTRA_COLS + 1], ones_f[:, 0:1],
                             extra[0:32, 0:1], start=True, stop=True
                             ).then_inc(list_ready, 1)
            pe.wait_ge(meta_ready, 1)

            item(2, w_up_next)
            with pe.Fori(3, NEXP + 1) as n:
                item(n, w_up_ring)
            more = pe.value_load(meta[0:1, EXTRA_COLS:EXTRA_COLS + 1], min_val=0, max_val=EXTRA)
            with pe.If(more > 0):
                with pe.Fori(NEXP + 1, NEXP + 1 + more) as n:
                    item(n, w_up_ring)
            scatter(more + (NEXP + 1), range(4))


def kernel(**inputs):
    import numpy as np
    import concourse.bacc as bacc
    from concourse.bass_utils import run_bass_kernel_spmd

    a = {name: np.ascontiguousarray(value) for name, value in inputs.items()}
    cols = np.zeros((P, NCOLS), np.float32)
    for c, name in ((C_G1, "norm1_g"), (C_GM, "mem_norm_g"), (C_G2, "norm2_g")):
        cols[:, c:c + KD] = a[name][0].reshape(KD, P).T
    for j in range(3):
        cols[:, C_CONV + j * KB:C_CONV + (j + 1) * KB] = a["conv_w"][0, j].reshape(KB, P).T
    cols[:, C_XQ], cols[:, C_XK] = a["xa_q_g"][0], a["xa_k_g"][0]
    cols[:FOX_D, C_FQ], cols[:FOX_D, C_FK] = a["fox_q_g"][0], a["fox_k_g"][0]
    spread = np.ascontiguousarray(np.broadcast_to(
        np.concatenate([a["b_forget"][0], a["b_router"][0]])[None, :], (P, FOX_H + NEXP)))

    def by_row(w):
        return np.ascontiguousarray(w.reshape(KD, P, -1).transpose(1, 0, 2))

    arrays = {
        "x": a["x"][0], "mem": a["mem"][0], "w_in": a["w_in"][0], "w_kv": a["w_mem_kv"][0],
        "w_branch": a["w_branch"][0], "w_out": a["w_out"][0], "w_up": a["w_up"][0], "w_down": a["w_down"][0],
        "cols": cols, "spread": spread, "wf": by_row(a["w_in"][0][:, 3 * W:3 * W + FOX_H]),
        "wr": by_row(a["w_router"][0]), "b_gate": a["b_gate"][0], "b_up": a["b_up"][0], "b_down": a["b_down"][0],
    }
    nc = bacc.Bacc("TRN2", target_bir_lowering=False, num_devices=1)
    args = [nc.dram_tensor(f"{name}_dram", v.shape, mybir.dt.from_np(v.dtype), kind="ExternalInput").ap()
            for name, v in arrays.items()]
    args.append(nc.dram_tensor("out_dram", (SEQ, D), F32, kind="ExternalOutput").ap())
    hybrid_block(nc, *args)
    got = run_bass_kernel_spmd(nc, [{f"{name}_dram": v for name, v in arrays.items()}], core_ids=[0])
    return got.results[0]["out_dram"].reshape(1, SEQ, D)
```

```python
from contextlib import ExitStack

import concourse.bass as bass
from concourse import mybir

F32 = mybir.dt.float32
F32R = mybir.dt.float32r
BF16 = mybir.dt.bfloat16
I32 = mybir.dt.int32
U32 = mybir.dt.uint32
ALU = mybir.AluOpType
ACT = mybir.ActivationFunctionType
AX = mybir.AxisListType.X

P = 128
SEQ = 256
NT = SEQ // P
D = 1024
KD = D // P
W = 512
KB = W // P
FOX_H, FOX_D = 8, 64
MEM_H, MEM_D = 4, 128
NEXP, TOPK, FF = 32, 4, 1024
NORM_EPS, QK_EPS = 1e-5, 1e-6
ALPHA, LIMIT = 1.702, 7.0
SLOTS = 64
EXTRA = (SEQ * TOPK - 1) // SLOTS
EXTRA_COLS = EXTRA + 1
TABLE = NEXP + EXTRA_COLS + 4
AHEAD = 6
KEPT = 3
DOWN = [(0, 2), (2, 4), (4, 6), (6, 7), (7, 8)]
WARM_UP, KEEP_UP = 14, 8
NEG = -1.0e30

C_G1, C_GM, C_G2, C_CONV = 0, 8, 16, 24
C_XQ, C_XK, C_FQ, C_FK, C_BF = 36, 37, 38, 39, 40
NCOLS = 41

R_NEG, R_POS, R_END = 64, 96, 104


def blocks_and_pieces():
    blocks = [("q",), ("k",), ("v",), ("mk",), ("mv",), ("xq",), ("cu",), ("cc",), ("cb",)]
    for branch in (1, 2, 0):
        for half in range(2):
            blocks += [("gate", branch, half), ("proj", branch, half)]
    pieces = []
    for b in blocks:
        pieces += [(b, 0)] if b[0] == "proj" else [(b, 0), (b, 1)]
    blocks += [("out", 0), ("out", 1)]
    pieces += [(("out", 0), 0), (("out", 1), 0), (("out", 0), 1), (("out", 1), 1)]
    return blocks, pieces


BLOCKS, PIECES = blocks_and_pieces()
NP = len(PIECES)
BLOCK_NO = {b: n for n, b in enumerate(BLOCKS)}
LAST_PIECE = {}
for _p, (_b, _h) in enumerate(PIECES):
    LAST_PIECE[_b] = _p


def auxiliary_jobs():
    jobs = [(-1, "hT", g) for g in range(4)]
    jobs += [(0, "logit_f", 0)]
    jobs += [(1 + g // 2, "mT", g) for g in range(4)]
    jobs += [(2, "forgetT", 0)]
    jobs += [(3, "qT", g) for g in range(4)]
    jobs += [(4, "cum", 0)]
    jobs += [(5, "kT", g) for g in range(4)]
    jobs += [(6 + h, "fox_s", h) for h in range(FOX_H)]
    jobs += [(7 + h, "fox_pT", h) for h in range(FOX_H)]
    jobs += [(9 + 2 * pair, "fox_y", pair) for pair in range(FOX_H // 2)]
    jobs += [(9, "mkT", g) for g in range(2)]
    jobs += [(13, "xqT", g) for g in range(2)]
    jobs += [(16 + h, "mem_s", h) for h in range(MEM_H)]
    jobs += [(17 + h, "mem_pT", h) for h in range(MEM_H)]
    jobs += [(18 + h, "mem_y", h) for h in range(MEM_H)]
    jobs += [(33, "zT", g) for g in range(2)]
    jobs += [(36, "zT", g) for g in range(2, 4)]
    return sorted(jobs, key=lambda j: j[0])


JOBS = auxiliary_jobs()
JOB = {(kind, arg): n for n, (_, kind, arg) in enumerate(JOBS)}
SPLIT_JOBS = [n for n, (_, kind, _) in enumerate(JOBS) if kind in ("hT", "mT", "fox_y", "mem_y", "zT")]
SPLIT_NO = {n: i for i, n in enumerate(SPLIT_JOBS)}
SMAX = [("fox", h) for h in range(FOX_H)] + [("mem", h) for h in range(MEM_H)]
SMAX_NO = {x: n for n, x in enumerate(SMAX)}


CONSTANTS = ["ident", "q_clear", "k_clear", "k_ones", "f_cols", "fox_gain", "xa_gain", "q_hot", "mask0", "mask1",
             "gate_sel", "tri_strict", "block_tri0", "block_tri1", "block_tri2", "iota", "iota_e", "ones_f",
             "tables"]


def built(name):
    return CONSTANTS.index(name) + 1


BYTES = {F32: 4, F32R: 4, BF16: 2, I32: 4, U32: 4}


class Region:

    def __init__(self, nc, start, end):
        self.nc, self.at, self.end = nc, start, end

    def place(self, name, shape, dt):
        size = BYTES[dt]
        for n in shape[1:]:
            size *= n
        tile = self.nc.alloc_sbuf_tensor_at(name, shape, dt, offset=self.at)
        self.at += -(-size // 32) * 32
        assert self.at <= self.end, (name, self.at, self.end)
        return tile


def jobs_at(step):
    return [(n, kind, arg) for n, (s, kind, arg) in enumerate(JOBS) if s == step]


def hybrid_block(nc, x_d, mem_d, w_in, w_kv, w_branch, w_out, w_up, w_down,
                 cols_d, spread_d, wf_d, wr_d, b_gate, b_up, b_down, out):
    ctx = ExitStack()
    with ctx:
        def sb(name, shape, dt, where=None):
            return (where or always).place(name, shape, dt)

        def sem(name):
            return ctx.enter_context(nc.semaphore(name))

        base, top = -(-nc.sbuf_base // 32) * 32, nc.sbuf_base + nc.sbuf_bytes_remaining
        up_bytes = KD * 2 * FF * 4
        raw_bytes = 4 * KB * W * 4
        always = Region(nc, base, top)
        ident = sb("ident", [P, P], F32)
        x1 = sb("x1", [P, NT, D], F32)
        cols = sb("cols", [P, NCOLS], F32)
        qcols = sb("qcols", [P, 2], F32)
        spread = sb("spread", [P, NEXP], F32)
        iota = sb("iota", [P, SLOTS], F32)
        ss = sb("ss", [P, 7, 16], F32)
        ms = sb("ms", [P, 7, 16], F32)
        rstd = sb("rstd", [P, 7, 16], F32)
        minus_half = sb("minus_half", [P, 16], F32)
        bias_up = sb("bias_up", [96, 2 * FF], BF16)
        bias_down = sb("bias_down", [96, D], BF16)
        ident_rep = sb("ident_rep", [96, NEXP], BF16)
        tri_strict = sb("tri_strict", [P, P], BF16)
        block_tri = sb("block_tri", [96, 96], BF16)
        ones_bf = sb("ones_bf", [P, P], BF16)
        ones_f = sb("ones_f", [32, P], F32)
        iota_e = sb("iota_e", [32, 2], F32)

        start_u = always.at
        u = Region(nc, start_u, start_u + up_bytes)
        mT_hi = sb("mT_hi", [P, KD, SEQ], F32R, u)
        mT_lo = sb("mT_lo", [P, KD, SEQ], F32R, u)
        q_rows = sb("q_rows", [P, FOX_H, SEQ], F32, u)
        k_rows = sb("k_rows", [P, FOX_H, SEQ], F32, u)
        tok = sb("tok", [P, 2, NT, W], F32, u)
        xqT = sb("xqT", [P, MEM_H, SEQ], F32, u)
        mkT = sb("mkT", [P, MEM_H, SEQ], F32, u)
        v_tok = sb("v_tok", [P, NT, W], F32, u)
        mv_tok = sb("mv_tok", [P, NT, W], F32, u)
        score = sb("score", [P, 2, W], F32, u)
        pT = sb("pT", [P, 2, W], F32, u)
        v = Region(nc, start_u, start_u + 2 * KD * SEQ * 4)
        conv_cu = sb("conv_cu", [P, KB, SEQ], F32, v)
        conv_out = sb("conv_out", [P, KB, SEQ], F32, v)
        conv_u = sb("conv_u", [P, KB, SEQ + 2], F32, v)
        u2 = Region(nc, start_u, start_u + up_bytes)
        w_up_tile = sb("w_up_tile", [P, KD, 2 * FF], F32, u2)
        start_d = u2.at
        raw = sb("raw", [P, 4, KB, W], F32, Region(nc, start_d, start_d + raw_bytes))
        w_down_ring = raw[:].rearrange("p a b n -> p (a b n)").rearrange("p (k n) -> p k n", n=D)

        start_r = start_d + raw_bytes
        r = Region(nc, start_r, top)
        w_hi = sb("w_hi", [P, 4, 2, W], F32R, r)
        w_lo = sb("w_lo", [P, 4, 2, W], F32R, r)
        hT_hi = sb("hT_hi", [P, KD, SEQ], F32R, r)
        hT_lo = sb("hT_lo", [P, KD, SEQ], F32R, r)
        start_y = r.at
        y_conv_hi = sb("y_conv_hi", [P, KB, SEQ], F32R, r)
        y_conv_lo = sb("y_conv_lo", [P, KB, SEQ], F32R, r)
        end_y = r.at
        yT_hi = [sb("y_fox_hi", [P, KB, SEQ], F32R, r), y_conv_hi, sb("y_mem_hi", [P, KB, SEQ], F32R, r)]
        yT_lo = [sb("y_fox_lo", [P, KB, SEQ], F32R, r), y_conv_lo, sb("y_mem_lo", [P, KB, SEQ], F32R, r)]
        y = Region(nc, start_y, end_y)
        mask = sb("mask", [P, 3 * P], F32, y)
        tri_ones = sb("tri_ones", [P, SEQ], F32, y)
        head_hot = sb("head_hot", [P, FOX_H], F32, y)
        f_cols = sb("f_cols", [P, NT, R_END], F32, y)
        f_tmp = sb("f_tmp", [FOX_H, 3, SEQ], F32, y)
        wf = sb("wf", [P, KD, FOX_H], F32, y)
        wf_hi = sb("wf_hi", [P, KD, FOX_H], F32R, y)
        wf_lo = sb("wf_lo", [P, KD, FOX_H], F32R, y)
        merged = sb("merged", [P, NT, D], F32, r)
        end_merged = r.at
        gate = sb("gate", [P, NT, W], F32, r)
        prob = sb("prob", [P, 2, W], F32, r)
        nmax = sb("nmax", [P, 2, 2], F32, r)
        den = sb("den", [P, 2, 2], F32, r)
        rden = sb("rden", [P, 2, 2], F32, r)
        gate_sel = sb("gate_sel", [96, 3, P], BF16, r)
        bias_gate = sb("bias_gate", [96, D], BF16, r)
        start_b = r.at
        b_raw = sb("b_raw", [96, W], F32, r)
        b_mid = sb("b_mid", [96, W], BF16, r)
        xs = merged
        w_up_last = sb("w_up_last", [P, KD // 2, 2 * FF], F32, Region(nc, start_y, end_merged))
        g = Region(nc, end_merged, start_b)
        h2T = sb("h2T", [P, KD, SEQ], F32, g)
        pos_tab = sb("pos_tab", [P, NT, TABLE], F32, g)
        comb_tab = sb("comb_tab", [P, NT, TABLE], F32, g)
        exp_sel = sb("exp_sel", [96, TABLE], F32, g)
        g = Region(nc, start_b, top)
        wr = sb("wr", [P, KD, NEXP], F32, g)
        zeros_bf = sb("zeros_bf", [P, W], BF16, g)
        m = Region(nc, start_r, start_y)
        m_parts = sb("m_parts", [P, 3, NT, D], BF16, m)
        x1s = sb("x1s", [P, NT, D], F32, m)
        xgT = sb("xgT", [P, KD, SLOTS], F32, m)
        glu = sb("glu", [P, W], F32, m)
        aT = sb("aT", [P, KB, P], F32, m)
        y_sb = sb("y_sb", [P, W], F32, m)
        pick = sb("pick", [P, NT, SLOTS], BF16, m)
        pick_w = sb("pick_w", [P, NT, 2, SLOTS], F32, m)
        pick_wT = sb("pick_wT", [P, NT, P], F32, m)
        bias_sel = sb("bias_sel", [96, SLOTS], BF16, m)
        meta = sb("meta", [1, EXTRA_COLS + 1], I32, m)
        start_t = m.at
        lin = sb("lin", [P, W], F32, m)
        glin = sb("glin", [P, W], F32, m)
        sig = sb("sig", [P, W], F32, m)
        a_tok = sb("a_tok", [P, W], F32, m)
        w_up_first = sb("w_up_first", [P, 2 * FF], F32, m)
        t = Region(nc, start_t, m.at)
        logits = sb("logits", [P, NT, NEXP], F32, t)
        top_v = sb("top_v", [P, NT, 8], F32, t)
        top_i = sb("top_i", [P, NT, 8], U32, t)
        top_f = sb("top_f", [P, NT, 8], F32, t)
        top_e = sb("top_e", [P, NT, TOPK], F32, t)
        top_den = sb("top_den", [P, NT, 2], F32, t)
        ntop = sb("ntop", [P, NT], F32, t)
        hot4 = sb("hot4", [P, NT, TOPK, NEXP], F32, t)
        hot4w = sb("hot4w", [P, NT, TOPK, NEXP], F32, t)
        chosen = sb("chosen", [P, NT, NEXP], F32, t)
        chosen3 = sb("chosen3", [P, NT, 3, NEXP], BF16, t)
        count = sb("count", [96, 4], F32, t)
        extra = sb("extra", [96, 2], F32, t)
        extra_bf = sb("extra_bf", [96, 2], BF16, t)
        first = sb("first", [96, 2], F32, t)
        xt = sb("xt", [96, 3, EXTRA_COLS], F32, t)
        posT = sb("posT", [32, 2, NT, P], F32, t)
        w_up_ring = [w_up_tile[:, k] for k in range(KD)]
        w_up_next = [w_up_first[:], h2T[:].rearrange("p k s -> p (k s)"), x1s[:].rearrange("p t n -> p (t n)"),
                     w_up_ring[KEPT], *(w_up_last[:, k] for k in range(KD // 2))]

        acc = [ctx.enter_context(nc.psum_tensor(f"acc{b}", [P, W], F32)) for b in range(4)]
        aux = [ctx.enter_context(nc.psum_tensor(f"aux{b}", [P, W], F32)) for b in range(4)]
        bank_glu, bank_lin, bank_cy, bank_t = aux

        x_loaded = [sem(f"x_loaded{t}") for t in range(NT)]
        mem_loaded = [sem(f"mem_loaded{t}") for t in range(NT)]
        params_loaded = sem("params_loaded")
        brow_loaded = sem("brow_loaded")
        brow_used = sem("brow_used")
        raw_half_loaded = sem("raw_half_loaded")
        raw_loaded = [sem(f"raw_loaded{s}") for s in range(4)]
        const_built = sem("const_built")
        ss_ready = [sem(f"ss_ready{n}") for n in range(6)]
        rstd_tile0 = sem("rstd_tile0")
        rstd_ready = sem("rstd_ready")
        pool_step = sem("pool_step")
        xs_ready = sem("xs_ready")
        hi_done = sem("hi_done")
        lo_done = sem("lo_done")
        half_used = sem("half_used")
        wf_hi_done = sem("wf_hi_done")
        wf_lo_done = sem("wf_lo_done")
        block_free = [sem(f"block_free{s}") for s in range(2)]
        aux_ready = sem("aux_ready")
        aux_free = [sem(f"aux_free{b}") for b in range(4)]
        part_hi = sem("part_hi")
        squares = sem("squares")
        forget_neg = sem("forget_neg")
        forget_log = sem("forget_log")
        forget_ready = sem("forget_ready")
        k_cum_ready = sem("k_cum_ready")
        max_ready = sem("max_ready")
        exp_ready = sem("exp_ready")
        prob_ready = sem("prob_ready")
        conv_y = sem("conv_y")
        conv_hi = sem("conv_hi")
        merged_done = sem("merged_done")
        last_tile0 = sem("last_tile0")
        x1_ready = sem("x1_ready")
        x1_squared = sem("x1_squared")
        act_step = sem("act_step")
        dve_step = sem("dve_step")
        wr_loaded = sem("wr_loaded")
        x1s_ready = sem("x1s_ready")
        x1T_ready = sem("x1T_ready")
        h2T_act = sem("h2T_act")
        h2T_dve = sem("h2T_dve")
        logits_ready = sem("logits_ready")
        parts_act = sem("parts_act")
        parts_pool = sem("parts_pool")
        parts_dve = sem("parts_dve")
        top_ready = sem("top_ready")
        soft_ready = sem("soft_ready")
        chosen_ready = sem("chosen_ready")
        slots_ready = sem("slots_ready")
        extra_ready = sem("extra_ready")
        first_ready = sem("first_ready")
        table_ready = sem("table_ready")
        list_ready = sem("list_ready")
        list_read = sem("list_read")
        xtab_ready = sem("xtab_ready")
        meta_ready = sem("meta_ready")
        up_loaded = [sem(f"up_loaded{k}") for k in range(KD)]
        up_used = [sem(f"up_used{k}") for k in range(KD - 1)]
        down_loaded = [sem(f"down_loaded{m}") for m in range(len(DOWN))]
        down_used = [sem(f"down_used{m}") for m in range(len(DOWN) - 1)]
        pick_ready = sem("pick_ready")
        pick_w_ready = sem("pick_w_ready")
        bias_sel_ready = sem("bias_sel_ready")
        gathered = sem("gathered")
        xg_ready = sem("xg_ready")
        up_done = sem("up_done")
        up_read = sem("up_read")
        glu_ready = sem("glu_ready")
        glin_ready = sem("glin_ready")
        sig_ready = sem("sig_ready")
        a_ready = sem("a_ready")
        pick_wT_done = sem("pick_wT_done")
        pick_wT_ready = sem("pick_wT_ready")
        aT_done = sem("aT_done")
        aT_ready = sem("aT_ready")
        y_done = sem("y_done")
        y_ready = sem("y_ready")
        scattered = sem("scattered")
        out_ready = sem("out_ready")
        stored = sem("stored")

        def block_done(eng, b):
            eng.wait_ge(half_used, 2 * LAST_PIECE[b] + 2)

        def block_read(eng, b):
            eng.wait_ge(block_free[BLOCK_NO[b] % 2], BLOCK_NO[b] // 2 + 1)

        mem_sb = tok[:].rearrange("p a t n -> p (a t n)").rearrange("p (t n) -> p t n", t=NT)

        def piece_source(p):
            block, half = PIECES[p]
            kind = block[0]
            rows = slice(half * KB * P, (half + 1) * KB * P)
            if kind in ("mk", "mv"):
                c = {"mk": 0, "mv": W}[kind]
                src = w_kv[rows, c:c + W]
            elif kind == "gate":
                c = 7 * W + FOX_H + block[1] * D + block[2] * W
                src = w_in[rows, c:c + W]
            elif kind == "proj":
                src = w_branch[block[1], :, block[2] * W:(block[2] + 1) * W]
            elif kind == "out":
                src = w_out[rows, block[1] * W:(block[1] + 1) * W]
            else:
                c = {"q": 0, "k": W, "v": 2 * W, "cu": 3 * W + FOX_H, "cc": 4 * W + FOX_H,
                     "cb": 5 * W + FOX_H, "xq": 6 * W + FOX_H}[kind]
                src = w_in[rows, c:c + W]
            return src.rearrange("(k p) n -> p k n", p=P)

        bias_chunks = [(b_up, bias_up, c) for c in range(4)] + [(b_down, bias_down, c) for c in range(2)]
        bias_chunks = [(b_gate, bias_gate, c) for c in range(2)] + bias_chunks

        block = ctx.enter_context(nc.Block())

        @block.sync
        def _(sp):
            def load_piece(p):
                if p >= 4:
                    sp.wait_ge(lo_done, 2 * (p - 4) + 2)
                sp.dma_start(raw[:, p % 4], piece_source(p)).then_inc(raw_loaded[p % 4], 16)

            for t in range(NT):
                sp.dma_start(x1[:, t], x_d[t * P:(t + 1) * P, :]).then_inc(x_loaded[t], 16)
            for h, loaded in ((0, raw_half_loaded), (1, raw_loaded[0])):
                sp.dma_start(raw[:, 0, 2 * h:2 * h + 2], piece_source(0)[:, 2 * h:2 * h + 2]).then_inc(loaded, 16)
            for t in range(NT):
                sp.dma_start(mem_sb[:, t], mem_d[t * P:(t + 1) * P, :]).then_inc(mem_loaded[t], 16)
            for p in range(1, NP):
                load_piece(p)
                if 27 <= p < 27 + KD:
                    if p == 27:
                        sp.wait_ge(aux_ready, JOB["mem_y", MEM_H - 1] + 1)
                        block_read(sp, ("cb",))
                    k = p - 27
                    sp.dma_start(w_up_ring[k], w_up[0, k * P:(k + 1) * P, :]).then_inc(up_loaded[k], 16)
            def load_up(k, expert, buffer):
                sp.dma_start(buffer, w_up[bass.ds(expert, 1), k * P:(k + 1) * P, :].rearrange("o p n -> p (o n)")
                             ).then_inc(up_loaded[k], 16)

            def load_down(m, expert):
                start, end = DOWN[m]
                sp.dma_start(w_down_ring[:, start:end], w_down[bass.ds(expert, 1), start * P:end * P, :]
                             .rearrange("o (k p) n -> p (o k) n", p=P)).then_inc(down_loaded[m], 16)

            def up_slot_free(k, items):
                sp.wait_ge(up_used[k] if k < KD - 1 else up_done, items)

            def down_slot_free(m, items):
                sp.wait_ge(down_used[m] if m < len(DOWN) - 1 else y_done, items)

            for k in range(KD // 2, KD):
                if k == KD // 2:
                    sp.wait_ge(half_used, 2 * LAST_PIECE[("proj", 0, 1)] + 2)
                elif k == KD - 1:
                    sp.wait_ge(aux_ready, JOB["zT", 3] + 1)
                sp.wait_ge(up_loaded[k], 16)
                load_up(k, 1, w_up_next[k])
            for m in range(len(DOWN)):
                last = max(p for p in range(NP) if p % 4 == DOWN[m][0] // 2)
                sp.wait_ge(lo_done, 2 * last + 2)
                load_down(m, 0)
            for k in range(KEPT):
                if k == 0:
                    sp.wait_ge(half_used, 2 * NP)
                elif k == 1:
                    sp.wait_ge(logits_ready, 1)
                else:
                    sp.wait_ge(parts_pool, 2)
                    sp.wait_ge(parts_dve, 2)
                sp.wait_ge(up_loaded[k], 16)
                load_up(k, 1, w_up_next[k])

            def load_item(n, before, loads, places):
                for k in range(KD):
                    if k == KEPT:
                        up_slot_free(k, before)
                        load_up(k, before, places[k])
                    else:
                        sp.wait_ge(up_loaded[k], loads)
                        up_slot_free(k, before)
                        load_up(k, n, places[k])
                for m in range(len(DOWN)):
                    down_slot_free(m, before)
                    load_down(m, before)

            with sp.Fori(2, AHEAD, 2) as i:
                before, even, odd = [sp.snap(sp.to_reg(i + c), min_val=2 + c, max_val=AHEAD + c) for c in (-1, 0, 1)]
                loads = [sp.snap(sp.to_reg(16 * i + 16 * c), min_val=32 + 16 * c, max_val=16 * (AHEAD + c))
                         for c in (0, 1)]
                load_item(even, before, loads[0], w_up_ring)
                load_item(odd, even, loads[1], w_up_next)
            up_slot_free(KEPT, AHEAD - 1)
            load_up(KEPT, AHEAD - 1, w_up_ring[KEPT])
            for m in range(len(DOWN)):
                down_slot_free(m, AHEAD - 1)
                load_down(m, AHEAD - 1)

            def load_in_order(expert, before):
                for k in range(KD):
                    up_slot_free(k, before)
                    load_up(k, expert, w_up_ring[k])
                for m in range(len(DOWN)):
                    down_slot_free(m, before)
                    load_down(m, expert)

            with sp.Fori(AHEAD + 1, NEXP + 1) as n:
                before = sp.snap(sp.to_reg(n - 1), min_val=AHEAD, max_val=NEXP - 1)
                load_in_order(before, before)
            sp.wait_ge(meta_ready, 1)
            more = sp.value_load(meta[0:1, EXTRA_COLS:EXTRA_COLS + 1], min_val=0, max_val=EXTRA)
            with sp.If(more > 0):
                with sp.Fori(NEXP + 1, NEXP + 1 + more) as n:
                    expert = sp.value_load(meta[0:1, bass.ds(n - (NEXP + 1), 1)], min_val=0, max_val=NEXP - 1)
                    before = sp.snap(sp.to_reg(n - 1), min_val=NEXP, max_val=NEXP + EXTRA)
                    load_in_order(expert, before)
            for t in range(NT):
                for h in range(2):
                    sp.wait_ge(out_ready, 2 * t + h + 1)
                    sp.dma_start(out[t * P:(t + 1) * P, h * W:(h + 1) * W],
                                 x1[:, t, h * W:(h + 1) * W]).then_inc(stored, 16)
            sp.wait_ge(stored, 16 * 2 * NT)

        @block.gpsimd
        def _(pool):
            steps = [0]

            def chained(ins):
                steps[0] += 1
                ins.then_inc(pool_step, 1)
                pool.wait_ge(pool_step, steps[0])

            order = iter(CONSTANTS)

            def constant(name, ins):
                assert next(order) == name
                ins.then_inc(const_built, 1)
                pool.wait_ge(const_built, built(name))

            chained(nc.gpsimd.memset(minus_half[:], -0.5))
            chained(nc.gpsimd.memset(ident[:], 0.0))
            constant("ident", nc.gpsimd.affine_select(out=ident[:], in_=ident[:], compare_op=ALU.not_equal, fill=1.0,
                                                      base=0, pattern=[[-1, P]], channel_multiplier=1))
            constant("q_clear", nc.gpsimd.memset(q_rows[64:P], 0.0))
            constant("k_clear", nc.gpsimd.memset(k_rows[64:P], 0.0))

            def rstd_of(n, width, count, eps):
                pool.wait_ge(ss_ready[n], 1)
                chained(nc.gpsimd.tensor_scalar(ms[:, n, 0:count], ss[:, n, 0:count], 1.0 / width, eps,
                                                ALU.mult, ALU.add))
                nc.gpsimd.tensor_tensor(rstd[:, n, 0:count], ms[:, n, 0:count], minus_half[:, 0:count],
                                        ALU.pow).then_inc(rstd_ready, 1)
                pool.wait_ge(rstd_ready, n + 1)

            for t in range(NT):
                pool.wait_ge(ss_ready[0], t + 1)
                chained(nc.gpsimd.tensor_scalar(ms[:, 0, t:t + 1], ss[:, 0, t:t + 1], 1.0 / D, NORM_EPS,
                                                ALU.mult, ALU.add))
                ready = rstd_ready if t else rstd_tile0
                nc.gpsimd.tensor_tensor(rstd[:, 0, t:t + 1], ms[:, 0, t:t + 1], minus_half[:, 0:1],
                                        ALU.pow).then_inc(ready, 1)
                pool.wait_ge(ready, 1)
            chained(nc.gpsimd.memset(head_hot[:], 0.0))
            for row in (R_NEG, R_POS):
                hot = head_hot[row:row + FOX_H]
                chained(nc.gpsimd.affine_select(out=hot, in_=hot, compare_op=ALU.not_equal, fill=1.0,
                                                base=0, pattern=[[-1, FOX_H]], channel_multiplier=1))
            constant("k_ones", nc.gpsimd.memset(k_rows[R_POS:R_END], 1.0))
            chained(nc.gpsimd.memset(tri_ones[:], 1.0))
            chained(nc.gpsimd.affine_select(out=tri_ones[:], in_=tri_ones[:], compare_op=ALU.is_ge, fill=0.0,
                                            base=0, pattern=[[1, SEQ]], channel_multiplier=-1))
            constant("f_cols", nc.gpsimd.memset(f_cols[:], 0.0))
            pool.wait_ge(params_loaded, 16 * 3)
            constant("fox_gain", nc.gpsimd.tensor_scalar(qcols[:, 0:1], cols[:, C_FQ:C_FQ + 1], FOX_D ** -0.5, None,
                                                         ALU.mult))
            constant("xa_gain", nc.gpsimd.tensor_scalar(qcols[:, 1:2], cols[:, C_XQ:C_XQ + 1], MEM_D ** -0.5, None,
                                                        ALU.mult))
            rstd_of(1, D, 2, NORM_EPS)
            constant("q_hot", nc.gpsimd.tensor_copy(
                q_rows[R_NEG:R_NEG + FOX_H],
                head_hot[R_NEG:R_NEG + FOX_H].unsqueeze(2).to_broadcast([FOX_H, FOX_H, SEQ])))
            chained(nc.gpsimd.memset(mask[:], 0.0))
            for name, c in (("mask0", 0), ("mask1", 2 * P)):
                constant(name, nc.gpsimd.affine_select(out=mask[:, c:c + P], in_=mask[:, c:c + P],
                                                       compare_op=ALU.is_ge, fill=NEG, base=0, pattern=[[-1, P]],
                                                       channel_multiplier=1))
            chained(nc.gpsimd.memset(ones_bf[:], 1.0))
            chained(nc.gpsimd.memset(ident_rep[:], 0.0))
            for g in range(3):
                rep = ident_rep[32 * g:32 * g + 32]
                chained(nc.gpsimd.affine_select(out=rep, in_=rep, compare_op=ALU.not_equal, fill=1.0,
                                                base=0, pattern=[[-1, NEXP]], channel_multiplier=1))
            constant("gate_sel", nc.gpsimd.tensor_copy(gate_sel[:],
                                                       ident_rep[:, 0:3].unsqueeze(2).to_broadcast([96, 3, P])))
            rstd_of(2, FOX_D, 16, QK_EPS)
            rstd_of(3, FOX_D, 16, QK_EPS)

            for n, (src, dst, c) in enumerate(bias_chunks):
                if n == 1:
                    rstd_of(4, MEM_D, 8, QK_EPS)
                if n == 3:
                    rstd_of(5, MEM_D, 8, QK_EPS)
                pool.wait_ge(brow_loaded, 16 * 3 * (n + 1))
                part = dst[:, c * W:(c + 1) * W]
                chained(nc.gpsimd.tensor_copy(part, b_raw[:]))
                chained(nc.gpsimd.tensor_tensor(b_raw[:], b_raw[:], part, ALU.subtract))
                chained(nc.gpsimd.tensor_copy(b_mid[:], b_raw[:]))
                chained(nc.gpsimd.tensor_copy(part[32:64], b_mid[32:64]))
                nc.gpsimd.tensor_tensor(part[64:96], b_raw[64:96], b_mid[64:96],
                                        ALU.subtract).then_inc(brow_used, 1)
                pool.wait_ge(brow_used, n + 1)
            chained(nc.gpsimd.memset(tri_strict[:], 1.0))
            chained(nc.gpsimd.memset(block_tri[:], 0.0))
            constant("tri_strict", nc.gpsimd.affine_select(out=tri_strict[:], in_=tri_strict[:], compare_op=ALU.is_ge, fill=0.0,
                                             base=-1, pattern=[[1, P]], channel_multiplier=-1))
            for g in range(3):
                s = slice(32 * g, 32 * g + 32)
                constant(f"block_tri{g}", nc.gpsimd.affine_select(out=block_tri[s, s], in_=ones_bf[s, 0:32], compare_op=ALU.is_ge,
                                                 fill=0.0, base=-1, pattern=[[1, 32]], channel_multiplier=-1))
            constant("iota", nc.gpsimd.iota(iota[:], pattern=[[1, SLOTS]], base=0, channel_multiplier=0,
                                    allow_small_or_imprecise_dtypes=True))
            constant("iota_e", nc.gpsimd.iota(iota_e[:], pattern=[[0, 2]], base=0, channel_multiplier=1,
                                    allow_small_or_imprecise_dtypes=True))
            constant("ones_f", nc.gpsimd.memset(ones_f[:], 1.0))

            pool.wait_ge(merged_done, 4)
            chained(nc.gpsimd.memset(zeros_bf[:], 0.0))
            chained(nc.gpsimd.memset(pos_tab[:], -1.0))
            chained(nc.gpsimd.memset(comb_tab[:], 0.0))
            chained(nc.gpsimd.memset(exp_sel[:], 0.0))
            constant("tables", nc.gpsimd.tensor_copy(exp_sel[:, 0:NEXP], ident_rep[:]))
            pool.wait_ge(x1_squared, 4)
            halves = ss[:, 6, 0:2 * NT].rearrange("p (t h) -> p t h", h=2)
            chained(nc.gpsimd.tensor_tensor(ms[:, 6, 0:NT], halves[:, :, 0], halves[:, :, 1], ALU.add))
            chained(nc.gpsimd.tensor_scalar(ms[:, 6, 0:NT], ms[:, 6, 0:NT], 1.0 / D, NORM_EPS, ALU.mult, ALU.add))
            nc.gpsimd.tensor_tensor(rstd[:, 6, 0:NT], ms[:, 6, 0:NT], minus_half[:, 0:NT], ALU.pow
                                    ).then_inc(rstd_ready, 1)
            pool.wait_ge(parts_act, 1)
            nc.gpsimd.tensor_tensor(x1s[:, 0], x1s[:, 0], m_parts[:, 0, 0], ALU.subtract).then_inc(parts_pool, 1)
            pool.wait_ge(parts_pool, 1)
            pool.wait_ge(parts_act, 3)
            nc.gpsimd.tensor_tensor(m_parts[:, 2, 0], x1s[:, 0], m_parts[:, 1, 0], ALU.subtract
                                    ).then_inc(parts_pool, 1)

        @block.scalar
        def _(act):
            act.dma_start(cols[:], cols_d).then_inc(params_loaded, 16)
            act.dma_start(spread[:], spread_d).then_inc(params_loaded, 16)
            act.dma_start(wf[:], wf_d).then_inc(params_loaded, 16)

            def bias_rows(n):
                src, _, c = bias_chunks[n]
                rows = src.shape[0]
                if n == 0:
                    act.wait_ge(act_step, 1)
                else:
                    act.wait_ge(brow_used, n)
                for g in range(3):
                    act.dma_start(b_raw[32 * g:32 * g + rows], src[:, c * W:(c + 1) * W]).then_inc(brow_loaded, 16)

            def split_hi(p, halves=(0, 1)):
                for h in halves:
                    s = 2 * p + h
                    if p == 0 and h == 0:
                        act.wait_ge(raw_half_loaded, 16)
                    elif p == 0 or h == 0:
                        act.wait_ge(raw_loaded[p % 4], 16 * (p // 4 + 1))
                    if s >= 4:
                        act.wait_ge(half_used, s - 3)
                    nc.scalar.activation(w_hi[:, s % 4], raw[:, p % 4, 2 * h:2 * h + 2], ACT.Copy).then_inc(hi_done, 1)

            scratch = [tile[:].rearrange("p t n -> p (t n)") for tile in (gate, prob)]
            for t in range(NT):
                act.wait_ge(x_loaded[t], 16)
                nc.scalar.activation(xs[:, t], x1[:, t], ACT.Square, accum_out=ss[:, 0, t:t + 1]
                                     ).then_inc(ss_ready[0], 1)

            def finish_job(j, kind, arg):
                bank = aux[j % 4]
                free = aux_free[j % 4]
                if kind in ("hT", "mT"):
                    hi, g = (hT_hi, C_G1) if kind == "hT" else (mT_hi, C_GM)
                    act.wait_ge(aux_ready, j + 1)
                    for i in range(2):
                        k = 2 * arg + i
                        ins = nc.scalar.activation(hi[:, k], bank[:, i * SEQ:(i + 1) * SEQ], ACT.Copy,
                                                   scale=cols[:, g + k:g + k + 1])
                    ins.then_inc(part_hi, 1)
                elif kind in ("qT", "kT"):
                    dst, scale = (q_rows, qcols[0:FOX_D, 0:1]) if kind == "qT" else \
                                 (k_rows, cols[0:FOX_D, C_FK:C_FK + 1])
                    act.wait_ge(const_built, built("xa_gain"))
                    act.wait_ge(aux_ready, j + 1)
                    nc.scalar.activation(dst[0:FOX_D, 2 * arg:2 * arg + 2], bank[0:FOX_D, :].rearrange(
                        "p (h s) -> p h s", h=2), ACT.Copy, scale=scale).then_inc(free, 1)
                elif kind in ("mkT", "xqT"):
                    dst, scale = (mkT, cols[:, C_XK:C_XK + 1]) if kind == "mkT" else (xqT, qcols[:, 1:2])
                    act.wait_ge(aux_ready, j + 1)
                    nc.scalar.activation(dst[:, 2 * arg:2 * arg + 2], bank[:, :].rearrange("p (h s) -> p h s", h=2),
                                         ACT.Copy, scale=scale).then_inc(free, 1)
                elif kind == "logit_f":
                    act.wait_ge(forget_neg, 1)
                    nc.scalar.activation(f_tmp[:, 1], f_tmp[:, 1], ACT.Exp).then_inc(act_step, 1)
                    act.wait_ge(act_step, 2)
                    nc.scalar.activation(f_tmp[:, 1], f_tmp[:, 1], ACT.Ln, bias=1.0).then_inc(forget_log, 1)
                elif kind == "cum":
                    act.wait_ge(const_built, built("k_ones"))
                    act.wait_ge(aux_ready, j + 1)
                    s = slice(R_NEG, R_NEG + FOX_H)
                    nc.scalar.activation(k_rows[s], bank[s, 0:SEQ].unsqueeze(1).to_broadcast([FOX_H, FOX_H, SEQ]),
                                         ACT.Copy).then_inc(k_cum_ready, 1)
                elif kind in ("fox_s", "mem_s"):
                    n = SMAX_NO[kind[:3], arg]
                    act.wait_ge(max_ready, n + 1)
                    if n >= 2:
                        old = SMAX[n - 2]
                        act.wait_ge(aux_ready, JOB[old[0] + "_pT", old[1]] + 1)
                    edges = (0, P, 3 * P) if kind == "fox_s" else (0, SEQ, 2 * SEQ)
                    for t in range(NT):
                        c = slice(edges[t], edges[t + 1])
                        nc.scalar.activation(prob[:, n % 2, c], score[:, n % 2, c], ACT.Exp,
                                             bias=nmax[:, n % 2, t:t + 1],
                                             accum_out=den[:, n % 2, t:t + 1]).then_inc(exp_ready, 1)
                elif kind in ("fox_pT", "mem_pT"):
                    n = SMAX_NO[kind[:3], arg]
                    width = 3 * P if kind == "fox_pT" else W
                    act.wait_ge(aux_ready, j + 1)
                    if n >= 2:
                        old = SMAX[n - 2]
                        y = ("fox_y", old[1] // 2) if old[0] == "fox" else ("mem_y", old[1])
                        act.wait_ge(aux_ready, JOB[y] + 1)
                    nc.scalar.activation(pT[:, n % 2, 0:width], bank[:, 0:width], ACT.Copy).then_inc(free, 1)
                elif kind == "fox_y":
                    act.wait_ge(aux_ready, j + 1)
                    nc.scalar.activation(yT_hi[0][:, arg], bank[:, 0:SEQ], ACT.Copy).then_inc(part_hi, 1)
                elif kind == "mem_y":
                    act.wait_ge(aux_ready, j + 1)
                    nc.scalar.activation(yT_hi[2][:, arg], bank[:, 0:SEQ], ACT.Copy).then_inc(part_hi, 1)
                elif kind == "zT":
                    act.wait_ge(aux_ready, j + 1)
                    nc.scalar.activation(hT_hi[:, 2 * arg:2 * arg + 2], bank[:].rearrange("p (k s) -> p k s", k=2),
                                         ACT.Copy).then_inc(part_hi, 1)

            def finish_block(b):
                n = BLOCK_NO[b]
                banks = acc[2 * (n % 2):2 * (n % 2) + 2]
                kind = b[0]
                if kind in ("q", "k", "mk", "xq"):
                    block_done(act, b)
                    m = {"q": 2, "k": 3, "mk": 4, "xq": 5}[kind]
                    if m > 2:
                        act.wait_ge(ss_ready[m - 1], 1)
                    for t in range(NT):
                        nc.scalar.activation(gate[:, t], banks[t][:], ACT.Square).then_inc(squares, 1)
                elif kind in ("v", "mv"):
                    block_done(act, b)
                    dst = v_tok if kind == "v" else mv_tok
                    for t in range(NT):
                        ins = nc.scalar.activation(dst[:, t], banks[t][:], ACT.Copy)
                    ins.then_inc(block_free[n % 2], 1)
                elif kind == "cu":
                    block_done(act, b)
                    for i in range(2):
                        ins = nc.scalar.activation(conv_cu[:, 2 * i:2 * i + 2],
                                                   banks[i][:].rearrange("p (c s) -> p c s", c=2), ACT.Copy)
                    ins.then_inc(block_free[n % 2], 1)
                elif kind == "cb":
                    act.wait_ge(conv_y, 1)
                    nc.scalar.activation(yT_hi[1][:], conv_out[:], ACT.Copy).then_inc(conv_hi, 1)
                elif kind == "gate":
                    block_done(act, b)
                    g = (n - BLOCK_NO[("gate", 1, 0)]) // 2
                    if g == 0:
                        act.wait_ge(ss_ready[5], 1)
                    elif g <= 2:
                        block_read(act, BLOCKS[n - 1])
                    else:
                        act.wait_ge(merged_done, g - 2)
                    for t in range(NT):
                        ins = nc.scalar.activation(gate[:, t], banks[t][:], ACT.Sigmoid)
                    ins.then_inc(block_free[n % 2], 1)

            bias_steps = [3, 8, 10, 13, 15, 17, 19, 21]
            for step in range(0, NP):
                if step == 0:
                    for h in range(2):
                        split_hi(0, (h,))
                        if h == 0:
                            act.wait_ge(params_loaded, 16 * 3)
                        for j, kind, arg in jobs_at(-1)[2 * h:2 * h + 2]:
                            finish_job(j, kind, arg)
                    nc.scalar.activation(wf_hi[:], wf[:], ACT.Copy).then_inc(wf_hi_done, 1)
                    for t in range(NT):
                        act.wait_ge(mem_loaded[t], 16)
                        ins = nc.scalar.activation(scratch[t], mem_sb[:, t], ACT.Square, accum_out=ss[:, 1, t:t + 1])
                    ins.then_inc(ss_ready[1], 1)
                    nc.scalar.activation(b_raw[:], ident[0:96, 0:1].to_broadcast([96, W]), ACT.Copy,
                                         scale=0.0).then_inc(act_step, 1)
                if step + 1 < NP:
                    split_hi(step + 1)
                if step > 0:
                    for j, kind, arg in jobs_at(step - 1):
                        finish_job(j, kind, arg)
                for b in BLOCKS:
                    if LAST_PIECE[b] == step - 1:
                        finish_block(b)
                if step == bias_steps[-1] + 8:
                    act.wait_ge(brow_used, len(bias_chunks))
                    act.dma_start(wr[:], wr_d).then_inc(wr_loaded, 16)
                if step in bias_steps:
                    bias_rows(bias_steps.index(step))

            for h in range(2):
                for t in range(NT):
                    act.wait_ge(x1_ready, 2 * h + t + 1)
                    nc.scalar.activation(acc[2 * (1 - h) + t][:], x1[:, t, h * W:(h + 1) * W], ACT.Square,
                                         accum_out=ss[:, 6, 2 * t + h:2 * t + h + 1]).then_inc(x1_squared, 1)
                g = 2 * h
                act.wait_ge(x1T_ready, g + 1)
                for k in (2 * g, 2 * g + 1):
                    ins = nc.scalar.activation(h2T[:, k], aux[g][:, (k % 2) * SEQ:(k % 2 + 1) * SEQ], ACT.Copy,
                                               scale=cols[:, C_G2 + k:C_G2 + k + 1])
                ins.then_inc(h2T_act, 1)
            for t in range(NT):
                act.wait_ge(x1s_ready, t + 1)
                nc.scalar.activation(m_parts[:, 0, t], x1s[:, t], ACT.Copy).then_inc(parts_act, 1)
            for t in range(NT):
                if t == 0:
                    act.wait_ge(parts_pool, 1)
                else:
                    act.wait_ge(parts_dve, 1)
                nc.scalar.activation(m_parts[:, 1, t], x1s[:, t], ACT.Copy).then_inc(parts_act, 1)
            act.wait_ge(top_ready, 1)
            for t in range(NT):
                nc.scalar.activation(top_e[:, t], top_v[:, t, 0:TOPK], ACT.Exp, bias=ntop[:, t:t + 1],
                                     accum_out=top_den[:, t, 0:1]).then_inc(soft_ready, 1)

            nc.scalar.activation(aT[:, 0], ident[:], ACT.Copy).then_inc(aT_ready, 1)
            nc.scalar.activation(y_sb[:, 0:P], ident[:], ACT.Copy).then_inc(y_ready, 1)

            def item(n):
                act.wait_ge(glu_ready, n)
                nc.scalar.activation(sig[:], glu[:], ACT.Sigmoid, scale=ALPHA).then_inc(sig_ready, 1)
                act.wait_ge(aT_done, n)
                nc.scalar.activation(aT[:].rearrange("p k s -> p (k s)"), bank_t[:], ACT.Copy).then_inc(aT_ready, 1)
                act.wait_ge(pick_wT_done, n)
                act.wait_ge(scattered, 4 * n)
                nc.scalar.activation(pick_wT[:].rearrange("p t s -> p (t s)"), bank_t[:, 0:NT * P],
                                     ACT.Copy).then_inc(pick_wT_ready, 1)
                act.wait_ge(y_done, n)
                nc.scalar.activation(y_sb[:], bank_cy[:], ACT.Copy).then_inc(y_ready, 1)

            with act.Fori(1, NEXP + 1) as n:
                item(n)
            act.wait_ge(meta_ready, 1)
            more = act.value_load(meta[0:1, EXTRA_COLS:EXTRA_COLS + 1], min_val=0, max_val=EXTRA)
            with act.If(more > 0):
                with act.Fori(NEXP + 1, NEXP + 1 + more) as n:
                    item(n)

        @block.vector
        def _(dve):
            steps = [0]

            def chained(ins):
                steps[0] += 1
                ins.then_inc(dve_step, 1)
                dve.wait_ge(dve_step, steps[0])

            def plain_f32(ap):
                return ap.bitcast(F32)

            def split_lo(p, halves=(0, 1)):
                for h in halves:
                    s = 2 * p + h
                    dve.wait_ge(hi_done, s + 1)
                    nc.vector.tensor_tensor(w_lo[:, s % 4], raw[:, p % 4, 2 * h:2 * h + 2],
                                            plain_f32(w_hi[:, s % 4]), ALU.subtract).then_inc(lo_done, 1)


            def finish_job(j, kind, arg):
                bank = aux[j % 4]
                free = aux_free[j % 4]
                if kind in ("hT", "mT"):
                    hi, lo, g = (hT_hi, hT_lo, C_G1) if kind == "hT" else (mT_hi, mT_lo, C_GM)
                    dve.wait_ge(part_hi, SPLIT_NO[j] + 1)
                    for i in range(2):
                        k = 2 * arg + i
                        ins = nc.vector.scalar_tensor_tensor(lo[:, k], bank[:, i * SEQ:(i + 1) * SEQ],
                                                             cols[:, g + k:g + k + 1], plain_f32(hi[:, k]),
                                                             ALU.mult, ALU.subtract)
                    ins.then_inc(free, 1)
                elif kind == "logit_f":
                    dve.wait_ge(aux_ready, j + 1)
                    dve.wait_ge(params_loaded, 16 * 3)
                    nc.vector.tensor_scalar(f_tmp[:, 0], bank[0:FOX_H, 0:SEQ], cols[0:FOX_H, C_BF:C_BF + 1], None,
                                            ALU.add).then_inc(free, 1)
                    dve.wait_ge(free, j // 4 + 1)
                    nc.vector.scalar_tensor_tensor(f_tmp[:, 1], f_tmp[:, 0], -1.0, f_tmp[:, 0],
                                                   ALU.mult, ALU.min).then_inc(forget_neg, 1)
                    dve.wait_ge(forget_log, 1)
                    nc.vector.scalar_tensor_tensor(f_tmp[:, 2], f_tmp[:, 0], 0.0, f_tmp[:, 1],
                                                   ALU.min, ALU.subtract).then_inc(forget_ready, 1)
                elif kind == "forgetT":
                    dve.wait_ge(const_built, built("f_cols"))
                    dve.wait_ge(aux_ready, j + 1)
                    logs = bank[:, 0:NT * FOX_H].rearrange("p (t h) -> p t h", t=NT)
                    nc.vector.tensor_copy(f_cols[:, :, R_POS:R_END], logs)
                    nc.vector.tensor_scalar(f_cols[:, :, R_NEG:R_NEG + FOX_H], logs, -1.0, None,
                                            ALU.mult).then_inc(free, 1)
                elif kind == "cum":
                    dve.wait_ge(const_built, built("q_hot"))
                    dve.wait_ge(k_cum_ready, 1)
                    s = slice(R_POS, R_END)
                    nc.vector.tensor_tensor(
                        q_rows[s], bank[s, 0:SEQ].unsqueeze(1).to_broadcast([FOX_H, FOX_H, SEQ]),
                        head_hot[s].unsqueeze(2).to_broadcast([FOX_H, FOX_H, SEQ]), ALU.mult).then_inc(free, 1)
                elif kind in ("fox_s", "mem_s"):
                    n = SMAX_NO[kind[:3], arg]
                    edges = (0, P, 3 * P) if kind == "fox_s" else (0, SEQ, 2 * SEQ)
                    if n >= 2:
                        dve.wait_ge(exp_ready, 2 * (n - 2) + 2)
                    dve.wait_ge(aux_ready, j + 1)
                    if kind == "fox_s":
                        dve.wait_ge(const_built, built("mask1"))
                        nc.vector.tensor_tensor(score[:, n % 2, 0:3 * P], bank[:, 0:3 * P], mask[:],
                                                ALU.add).then_inc(free, 1)
                    else:
                        nc.vector.tensor_copy(score[:, n % 2], bank[:]).then_inc(free, 1)
                    dve.wait_ge(free, j // 4 + 1)
                    for t in range(NT):
                        ins = nc.vector.tensor_reduce(nmax[:, n % 2, t:t + 1], score[:, n % 2, edges[t]:edges[t + 1]],
                                                      AX, ALU.max, negate=True)
                    ins.then_inc(max_ready, 1)
                elif kind in ("fox_y", "mem_y"):
                    dve.wait_ge(part_hi, SPLIT_NO[j] + 1)
                    b = 0 if kind == "fox_y" else 2
                    nc.vector.tensor_tensor(yT_lo[b][:, arg], bank[:, 0:SEQ], plain_f32(yT_hi[b][:, arg]),
                                            ALU.subtract).then_inc(free, 1)
                elif kind == "zT":
                    dve.wait_ge(part_hi, SPLIT_NO[j] + 1)
                    k = slice(2 * arg, 2 * arg + 2)
                    nc.vector.tensor_tensor(hT_lo[:, k], bank[:].rearrange("p (k s) -> p k s", k=2),
                                            plain_f32(hT_hi[:, k]), ALU.subtract).then_inc(free, 1)

            def normalise_probs(kind, arg):
                n = SMAX_NO[kind[:3], arg]
                edges = (0, P, 3 * P) if kind == "fox_s" else (0, SEQ, 2 * SEQ)
                dve.wait_ge(exp_ready, 2 * n + 2)
                chained(nc.vector.reciprocal(rden[:, n % 2], den[:, n % 2]))
                for t in range(NT):
                    c = slice(edges[t], edges[t + 1])
                    ins = nc.vector.tensor_scalar(prob[:, n % 2, c], prob[:, n % 2, c], rden[:, n % 2, t:t + 1],
                                                  None, ALU.mult)
                ins.then_inc(prob_ready, 1)

            norm_blocks = {"q": (2, 0), "k": (3, 1), "mk": (4, 0), "xq": (5, 1)}

            def block_squares(b):
                n, _ = norm_blocks[b[0]]
                heads = FOX_H if n < 4 else MEM_H
                for t in range(NT):
                    dve.wait_ge(squares, 2 * (n - 2) + t + 1)
                    ins = nc.vector.tensor_reduce(ss[:, n, t * heads:(t + 1) * heads],
                                                  gate[:, t].rearrange("p (h d) -> p h d", h=heads), AX, ALU.add)
                ins.then_inc(ss_ready[n], 1)

            def block_scale(b):
                n, where = norm_blocks[b[0]]
                no = BLOCK_NO[b]
                banks = acc[2 * (no % 2):2 * (no % 2) + 2]
                heads = FOX_H if n < 4 else MEM_H
                width = W // heads
                dve.wait_ge(rstd_ready, n + 1)
                if n == 2:
                    dve.wait_ge(xs_ready, 4)
                if n >= 4:
                    dve.wait_ge(aux_ready, JOB[{4: "qT", 5: "kT"}[n], 3] + 1)
                for t in range(NT):
                    ins = nc.vector.tensor_tensor(
                        tok[:, where, t].rearrange("p (h d) -> p h d", h=heads),
                        banks[t][:].rearrange("p (h d) -> p h d", h=heads),
                        rstd[:, n, t * heads:(t + 1) * heads].unsqueeze(2).to_broadcast([P, heads, width]), ALU.mult)
                ins.then_inc(block_free[no % 2], 1)

            def finish_block(b):
                n = BLOCK_NO[b]
                banks = acc[2 * (n % 2):2 * (n % 2) + 2]
                kind = b[0]
                if kind == "cc":
                    block_read(dve, ("cu",))
                    nc.vector.memset(conv_u[:, :, 0:2], 0.0).then_inc(dve_step, 1)
                    steps[0] += 1
                    block_done(dve, b)
                    for i in range(2):
                        ins = nc.vector.tensor_tensor(conv_u[:, 2 * i:2 * i + 2, 2:2 + SEQ],
                                                      banks[i][:].rearrange("p (c s) -> p c s", c=2),
                                                      conv_cu[:, 2 * i:2 * i + 2], ALU.mult)
                    ins.then_inc(block_free[n % 2], 1)
                    block_read(dve, b)
                    dve.wait_ge(dve_step, steps[0])
                    for c in range(KB):
                        tap = cols[:, C_CONV + c:C_CONV + c + 1]
                        nc.vector.tensor_scalar(conv_out[:, c], conv_u[:, c, 0:SEQ], tap, None,
                                                ALU.mult).then_inc(dve_step, 1)
                        steps[0] += 1
                    for j in (1, 2):
                        dve.wait_ge(dve_step, steps[0])
                        for c in range(KB):
                            tap = cols[:, C_CONV + j * KB + c:C_CONV + j * KB + c + 1]
                            nc.vector.scalar_tensor_tensor(conv_out[:, c], conv_u[:, c, j:j + SEQ], tap,
                                                           conv_out[:, c], ALU.mult, ALU.add).then_inc(dve_step, 1)
                            steps[0] += 1
                elif kind == "cb":
                    dve.wait_ge(dve_step, steps[0])
                    block_done(dve, b)
                    for i in range(2):
                        s = slice(2 * i, 2 * i + 2)
                        ins = nc.vector.tensor_tensor(conv_out[:, s], banks[i][:].rearrange("p (c s) -> p c s", c=2),
                                                      conv_out[:, s], ALU.mult)
                    ins.then_inc(conv_y, 1)
                    dve.wait_ge(conv_hi, 1)
                    nc.vector.tensor_tensor(yT_lo[1][:], conv_out[:], plain_f32(yT_hi[1][:]),
                                            ALU.subtract).then_inc(block_free[n % 2], 1)
                elif kind == "proj":
                    g = (n - BLOCK_NO[("proj", 1, 0)]) // 2
                    half = slice(b[2] * W, (b[2] + 1) * W)
                    block_read(dve, BLOCKS[n - 1])
                    block_done(dve, b)
                    if g < 2:
                        for t in range(NT):
                            ins = nc.vector.tensor_tensor(merged[:, t, half], banks[t][:], gate[:, t], ALU.mult)
                        ins.then_inc(block_free[n % 2], 1)
                    else:
                        for t in range(NT):
                            ins = nc.vector.tensor_tensor(gate[:, t], banks[t][:], gate[:, t], ALU.mult)
                        ins.then_inc(block_free[n % 2], 1)
                        block_read(dve, b)
                        for t in range(NT):
                            ins = nc.vector.tensor_tensor(merged[:, t, half], merged[:, t, half], gate[:, t], ALU.add)
                        ins.then_inc(merged_done, 1)
                elif kind == "out":
                    half = slice(b[1] * W, (b[1] + 1) * W)
                    for t in range(NT):
                        if b[1] == 1 and t == 0:
                            dve.wait_ge(last_tile0, 1)
                        else:
                            block_done(dve, b)
                        nc.vector.tensor_tensor(x1[:, t, half], banks[t][:], x1[:, t, half],
                                                ALU.add).then_inc(x1_ready, 1)

            for t in range(NT):
                dve.wait_ge(rstd_ready if t else rstd_tile0, 1)
                nc.vector.tensor_scalar(xs[:, t], x1[:, t], rstd[:, 0, t:t + 1], None, ALU.mult).then_inc(xs_ready, 1)
            for h in range(2):
                split_lo(0, (h,))
                for j, kind, arg in jobs_at(-1)[2 * h:2 * h + 2]:
                    finish_job(j, kind, arg)
            dve.wait_ge(wf_hi_done, 1)
            nc.vector.tensor_tensor(wf_lo[:], wf[:], plain_f32(wf_hi[:]), ALU.subtract).then_inc(wf_lo_done, 1)
            for step in range(0, NP):
                here = jobs_at(step - 1)
                for j, kind, arg in here:
                    if kind in ("fox_s", "mem_s"):
                        finish_job(j, kind, arg)
                done = [b for b in BLOCKS if LAST_PIECE[b] == step - 1]
                if step + 1 < NP:
                    split_lo(step + 1)
                for b in done:
                    if b[0] in norm_blocks:
                        block_squares(b)
                for j, kind, arg in here:
                    if kind in ("fox_s", "mem_s"):
                        normalise_probs(kind, arg)
                    elif kind != "hT":
                        finish_job(j, kind, arg)
                for b in done:
                    if b[0] in norm_blocks:
                        block_scale(b)
                    else:
                        finish_block(b)
                if step == 0:
                    dve.wait_ge(rstd_ready, 2)
                    dve.wait_ge(aux_ready, JOB["hT", 3] + 1)
                    for t in range(NT):
                        nc.vector.tensor_scalar(xs[:, t], mem_sb[:, t], rstd[:, 1, t:t + 1], None,
                                                ALU.mult).then_inc(xs_ready, 1)

            def move_x1T(g):
                dve.wait_ge(x1T_ready, g + 1)
                for k in (2 * g, 2 * g + 1):
                    ins = nc.vector.tensor_scalar(h2T[:, k], aux[g][:, (k % 2) * SEQ:(k % 2 + 1) * SEQ],
                                                  cols[:, C_G2 + k:C_G2 + k + 1], None, ALU.mult)
                ins.then_inc(h2T_dve, 1)

            def scale_x1(t):
                nc.vector.tensor_scalar(x1s[:, t], x1[:, t], rstd[:, 6, t:t + 1], None, ALU.mult).then_inc(x1s_ready, 1)

            move_x1T(1)
            finish_block(("out", 1))
            move_x1T(3)
            dve.wait_ge(rstd_ready, 7)
            scale_x1(0)
            scale_x1(1)
            dve.wait_ge(parts_act, 2)
            nc.vector.tensor_tensor(x1s[:, 1], x1s[:, 1], m_parts[:, 0, 1], ALU.subtract).then_inc(parts_dve, 1)
            dve.wait_ge(logits_ready, 1)
            for t in range(NT):
                ins = nc.vector.scalar_tensor_tensor(logits[:, t], acc[2][:, t * NEXP:(t + 1) * NEXP],
                                                     rstd[:, 6, t:t + 1], spread[:], ALU.mult, ALU.add)
            chained(ins)
            for t in range(NT):
                ins = nc.vector.max(top_v[:, t], logits[:, t])
            chained(ins)
            for t in range(NT):
                ins = nc.vector.max_index(top_i[:, t], top_v[:, t], logits[:, t])
            chained(ins)
            chained(nc.vector.tensor_copy(top_f[:], top_i[:]))
            dve.wait_ge(const_built, built("ones_f"))
            wide4 = [P, NT, TOPK, NEXP]
            chained(nc.vector.tensor_tensor(hot4[:], iota[:, 0:NEXP].unsqueeze(1).unsqueeze(1).to_broadcast(wide4),
                                            top_f[:, :, 0:TOPK].unsqueeze(3).to_broadcast(wide4), ALU.is_equal))
            chained(nc.vector.tensor_reduce(chosen[:], hot4[:].rearrange("p t k e -> p t e k"), AX, ALU.add))
            for c in (slice(0, 1), slice(1, 3)):
                nc.vector.tensor_copy(chosen3[:, :, c], chosen[:].unsqueeze(2).to_broadcast(
                    [P, NT, c.stop - c.start, NEXP])).then_inc(chosen_ready, 1)
            nc.vector.tensor_scalar(ntop[:], top_v[:, :, 0], -1.0, None, ALU.mult).then_inc(top_ready, 1)
            dve.wait_ge(const_built, built("tables"))
            dve.wait_ge(slots_ready, 1)
            slots = acc[3][:, 0:NT * NEXP].rearrange("p (t e) -> p t e", t=NT)
            chained(nc.vector.scalar_tensor_tensor(pos_tab[:, :, 0:NEXP], slots, 1.0, chosen[:], ALU.add, ALU.mult))
            nc.vector.tensor_scalar(pos_tab[:, :, 0:NEXP], pos_tab[:, :, 0:NEXP], -1.0, None,
                                    ALU.add).then_inc(table_ready, 1)
            dve.wait_ge(table_ready, 1)

            def build_pick(col):
                for t in range(NT):
                    ins = nc.vector.tensor_scalar(pick[:, t], iota[:], pos_tab[:, t, col], None, ALU.is_equal)
                ins.then_inc(pick_ready, 1)

            def build_pick_w(col):
                for t in range(NT):
                    ins = nc.vector.tensor_scalar(pick_w[:, t], iota[:].unsqueeze(1).to_broadcast([P, 2, SLOTS]),
                                                  pos_tab[:, t, col], comb_tab[:, t, col], ALU.is_equal, ALU.mult)
                ins.then_inc(pick_w_ready, 1)

            def build_bias_sel(col):
                nc.vector.tensor_scalar(bias_sel[:], ones_bf[0:96, 0:SLOTS], exp_sel[:, col], None,
                                        ALU.mult).then_inc(bias_sel_ready, 1)

            def move_gathered():
                nc.vector.tensor_tensor(xgT[:], bank_cy[:].rearrange("p (k s) -> p k s", k=KD),
                                        cols[:, C_G2:C_G2 + KD].unsqueeze(2).to_broadcast([P, KD, SLOTS]),
                                        ALU.mult).then_inc(xg_ready, 1)

            build_pick(slice(0, 1))
            build_bias_sel(slice(0, 1))
            dve.wait_ge(slots_ready, 2)
            nc.vector.tensor_copy(count[:, 0:1], bank_glu[0:96, 0:1]).then_inc(extra_ready, 1)
            dve.wait_ge(parts_act, 4)
            nc.vector.tensor_tensor(m_parts[:, 2, 1], x1s[:, 1], m_parts[:, 1, 1], ALU.subtract
                                    ).then_inc(parts_dve, 1)
            nc.vector.memset(glu[:, 0:1], 0.0).then_inc(up_read, 1)
            dve.wait_ge(gathered, 1)
            move_gathered()
            build_pick(slice(1, 2))
            dve.wait_ge(soft_ready, 2)
            chained(nc.vector.reciprocal(top_den[:, :, 1:2], top_den[:, :, 0:1]))
            chained(nc.vector.tensor_tensor(top_e[:], top_e[:], top_den[:, :, 1:2].to_broadcast([P, NT, TOPK]),
                                            ALU.mult))
            chained(nc.vector.tensor_tensor(hot4w[:], hot4[:], top_e[:].unsqueeze(3).to_broadcast(wide4), ALU.mult))
            nc.vector.tensor_reduce(comb_tab[:, :, 0:NEXP], hot4w[:].rearrange("p t k e -> p t e k"),
                                    AX, ALU.add).then_inc(table_ready, 1)
            dve.wait_ge(table_ready, 2)
            build_pick_w(slice(0, 1))
            dve.wait_ge(extra_ready, 1)
            chained(nc.vector.tensor_scalar(count[:, 1:2], count[:, 0:1], float(SLOTS), None, ALU.is_gt))
            chained(nc.vector.scalar_tensor_tensor(count[:, 2:3], count[:, 0:1], 2.0 * SLOTS, count[:, 1:2],
                                                   ALU.is_gt, ALU.add))
            chained(nc.vector.scalar_tensor_tensor(extra[:, 0:1], count[:, 0:1], 3.0 * SLOTS, count[:, 2:3],
                                                   ALU.is_gt, ALU.add))
            nc.vector.tensor_copy(extra_bf[:], extra[:, 0:1].to_broadcast([96, 2])).then_inc(extra_ready, 1)

            dve.wait_ge(first_ready, 1)
            nc.vector.tensor_copy(first[:, 0:1], bank_t[0:96, 0:1]).then_inc(list_read, 1)
            dve.wait_ge(list_read, 1)
            chained(nc.vector.tensor_scalar(xt[:, 0], iota[0:96, 0:EXTRA_COLS], first[:, 0:1], None, ALU.subtract))
            chained(nc.vector.tensor_scalar(xt[:, 1], xt[:, 0], 0.0, None, ALU.is_ge))
            chained(nc.vector.scalar_tensor_tensor(exp_sel[:, NEXP:NEXP + EXTRA_COLS], xt[:, 0], extra[:, 0:1],
                                                   xt[:, 1], ALU.is_lt, ALU.mult))
            chained(nc.vector.scalar_tensor_tensor(xt[:, 2], xt[:, 0], 1.0, exp_sel[:, NEXP:NEXP + EXTRA_COLS],
                                                   ALU.add, ALU.mult))
            chained(nc.vector.tensor_scalar(xt[:, 2], xt[:, 2], -float(SLOTS), None, ALU.mult))
            dve.wait_ge(list_ready, 1)
            nc.vector.tensor_copy(posT[:], bank_t[0:32, :].rearrange("p (a t s) -> p a t s", a=2, t=NT)
                                  ).then_inc(xtab_ready, 1)
            dve.wait_ge(list_ready, 2)
            nc.vector.tensor_copy(pos_tab[:, :, NEXP:NEXP + EXTRA_COLS],
                                  bank_t[:, 0:NT * EXTRA_COLS].rearrange("p (t j) -> p t j", t=NT))
            nc.vector.tensor_copy(comb_tab[:, :, NEXP:NEXP + EXTRA_COLS],
                                  bank_t[:, SEQ:SEQ + NT * EXTRA_COLS].rearrange("p (t j) -> p t j", t=NT))
            nc.vector.tensor_copy(meta[0:1, :], bank_t[0:1, 128:128 + EXTRA_COLS + 1]).then_inc(meta_ready, 1)
            dve.wait_ge(meta_ready, 1)

            def item(n):
                dve.wait_ge(up_done, n)
                nc.vector.tensor_scalar(glu[:], bank_glu[:], LIMIT, None, ALU.min).then_inc(glu_ready, 1)
                nc.vector.tensor_scalar(lin[:], bank_lin[:], LIMIT, -LIMIT, ALU.min, ALU.max).then_inc(up_read, 1)
                dve.wait_ge(glu_ready, n)
                dve.wait_ge(up_read, n + 1)
                nc.vector.scalar_tensor_tensor(glin[:], lin[:], 1.0, glu[:], ALU.add, ALU.mult
                                               ).then_inc(glin_ready, 1)
                dve.wait_ge(glin_ready, n)
                dve.wait_ge(sig_ready, n)
                nc.vector.tensor_tensor(a_tok[:], glin[:], sig[:], ALU.mult).then_inc(a_ready, 1)
                dve.wait_ge(gathered, n + 1)
                move_gathered()
                build_pick(bass.ds(n + 1, 1))
                dve.wait_ge(pick_wT_done, n)
                build_pick_w(bass.ds(n, 1))
                dve.wait_ge(y_done, n)
                build_bias_sel(bass.ds(n, 1))

            with dve.Fori(1, NEXP + 1) as n:
                item(n)
            more = dve.value_load(meta[0:1, EXTRA_COLS:EXTRA_COLS + 1], min_val=0, max_val=EXTRA)
            with dve.If(more > 0):
                with dve.Fori(NEXP + 1, NEXP + 1 + more) as n:
                    item(n)
            for t in range(NT):
                for h in range(2):
                    dve.wait_ge(scattered, 4 * more + (4 * NEXP + 2 * t + h + 1))
                    s = slice(h * W, (h + 1) * W)
                    nc.vector.tensor_tensor(x1[:, t, s], acc[2 * t + h][:], x1[:, t, s], ALU.add).then_inc(out_ready, 1)

        @block.tensor
        def _(pe):
            def bank_of(j):
                if j >= 4:
                    pe.wait_ge(aux_free[j % 4], j // 4)
                return aux[j % 4]

            def job_read(kind, arg):
                j = JOB[kind, arg]
                pe.wait_ge(aux_free[j % 4], j // 4 + 1)

            def do_job(j, kind, arg):
                if kind == "mT":
                    pe.wait_ge(xs_ready, 4)
                    bank = bank_of(j)
                    for i in range(2):
                        for t in range(NT):
                            k = 2 * arg + i
                            ins = nc.tensor.transpose(bank[:, i * SEQ + t * P:i * SEQ + (t + 1) * P],
                                                      xs[:, t, k * P:(k + 1) * P], ident[:])
                elif kind == "logit_f":
                    bank = bank_of(j)
                    pe.wait_ge(wf_lo_done, 1)
                    for g in range(4):
                        job_read("hT", g)
                    for k in range(KD):
                        for c, (a, w) in enumerate(((hT_hi, wf_hi), (hT_lo, wf_hi), (hT_hi, wf_lo))):
                            ins = nc.tensor.matmul(bank[0:FOX_H, 0:SEQ], w[:, k], a[:, k],
                                                   start=(k == 0 and c == 0), stop=(k == KD - 1 and c == 2))
                elif kind == "forgetT":
                    bank = bank_of(j)
                    pe.wait_ge(forget_ready, 1)
                    for t in range(NT):
                        ins = nc.tensor.transpose(bank[:, t * FOX_H:(t + 1) * FOX_H], f_tmp[:, 2, t * P:(t + 1) * P],
                                                  ident[0:FOX_H, 0:FOX_H])
                elif kind == "cum":
                    bank = bank_of(j)
                    job_read("forgetT", 0)
                    nc.tensor.matmul(bank[0:R_END, 0:SEQ], f_cols[:, 0], tri_ones[:], start=True, stop=False,
                                     skip_group_check=True)
                    ins = nc.tensor.matmul(bank[0:R_END, P:SEQ], f_cols[:, 1], tri_ones[:, 0:P], start=False,
                                           stop=True, skip_group_check=True)
                elif kind in ("qT", "kT"):
                    bank = bank_of(j)
                    block_read(pe, (kind[0],))
                    for i in range(2):
                        h = 2 * arg + i
                        for t in range(NT):
                            ins = nc.tensor.transpose(bank[0:FOX_D, i * SEQ + t * P:i * SEQ + (t + 1) * P],
                                                      tok[:, 0 if kind == "qT" else 1, t, h * FOX_D:(h + 1) * FOX_D],
                                                      ident[:])
                elif kind in ("mkT", "xqT"):
                    bank = bank_of(j)
                    block_read(pe, (kind[:2],))
                    for i in range(2):
                        h = 2 * arg + i
                        for t in range(NT):
                            ins = nc.tensor.transpose(bank[:, i * SEQ + t * P:i * SEQ + (t + 1) * P],
                                                      tok[:, 0 if kind == "mkT" else 1, t, h * P:(h + 1) * P], ident[:])
                elif kind == "fox_s":
                    bank = bank_of(j)
                    if arg == 0:
                        job_read("qT", 3)
                        pe.wait_ge(const_built, built("q_hot"))
                        job_read("cum", 0)
                    if arg % 2 == 0:
                        job_read("kT", arg // 2)
                    nc.tensor.matmul(bank[:, 0:P], q_rows[0:R_END, arg, 0:P], k_rows[0:R_END, arg, 0:P],
                                     start=True, stop=True)
                    ins = nc.tensor.matmul(bank[:, P:3 * P], q_rows[0:R_END, arg, P:SEQ], k_rows[0:R_END, arg],
                                           start=True, stop=True)
                elif kind == "mem_s":
                    bank = bank_of(j)
                    if arg % 2 == 0:
                        job_read("xqT", arg // 2)
                        job_read("mkT", arg // 2)
                    for t in range(NT):
                        ins = nc.tensor.matmul(bank[:, t * SEQ:(t + 1) * SEQ], xqT[:, arg, t * P:(t + 1) * P],
                                               mkT[:, arg], start=True, stop=True)
                elif kind in ("fox_pT", "mem_pT"):
                    bank = bank_of(j)
                    n = SMAX_NO[kind[:3], arg]
                    pe.wait_ge(prob_ready, n + 1)
                    order = [0, 1, 2] if kind == "fox_pT" else [0, 2, 1, 3]
                    for i, c in enumerate(order):
                        ins = nc.tensor.transpose(bank[:, i * P:(i + 1) * P], prob[:, n % 2, c * P:(c + 1) * P],
                                                  ident[:])
                elif kind == "fox_y":
                    bank = bank_of(j)
                    if arg == 0:
                        block_read(pe, ("v",))
                    for tile in range(NT):
                        for h in (2 * arg, 2 * arg + 1):
                            if tile == 0:
                                job_read("fox_pT", h)
                            n = SMAX_NO["fox", h]
                            rows = slice(FOX_D * (h % 2), FOX_D * (h % 2) + FOX_D)
                            queries, p = ((0, slice(0, SEQ)), (P, slice(SEQ, 3 * P)))[tile]
                            ins = nc.tensor.matmul(bank[rows, queries:SEQ], v_tok[:, tile, h * FOX_D:(h + 1) * FOX_D],
                                                   pT[:, n % 2, p], start=(tile == 0), stop=(tile == 1),
                                                   skip_group_check=True)
                elif kind == "mem_y":
                    bank = bank_of(j)
                    if arg == 0:
                        block_read(pe, ("mv",))
                    job_read("mem_pT", arg)
                    n = SMAX_NO["mem", arg]
                    for t in range(NT):
                        ins = nc.tensor.matmul(bank[:, 0:SEQ], mv_tok[:, t, arg * P:(arg + 1) * P],
                                               pT[:, n % 2, t * SEQ:(t + 1) * SEQ], start=(t == 0), stop=(t == 1))
                elif kind == "zT":
                    bank = bank_of(j)
                    pe.wait_ge(merged_done, 3 if arg < 2 else 4)
                    for i in range(2):
                        for t in range(NT):
                            k = 2 * arg + i
                            ins = nc.tensor.transpose(bank[:, i * SEQ + t * P:i * SEQ + (t + 1) * P],
                                                      merged[:, t, k * P:(k + 1) * P], ident[:])
                ins.then_inc(aux_ready, 1)

            def piece(p):
                b, half = PIECES[p]
                kind = b[0]
                n = BLOCK_NO[b]
                banks = acc[2 * (n % 2):2 * (n % 2) + 2]
                last = p == LAST_PIECE[b]
                if half == 0 and n >= 2:
                    pe.wait_ge(block_free[n % 2], n // 2)
                if b == ("mk",) and half == 0:
                    job_read("mT", 3)
                if kind == "proj" and b[2] == 0:
                    if b[1] == 0:
                        for pair in range(FOX_H // 2):
                            job_read("fox_y", pair)
                    elif b[1] == 1:
                        block_read(pe, ("cb",))
                    else:
                        for h in range(MEM_H):
                            job_read("mem_y", h)
                if kind == "out" and b[1] == 0:
                    job_read("zT", 2 * half)
                    job_read("zT", 2 * half + 1)
                if kind == "proj":
                    a_hi, a_lo = yT_hi[b[1]], yT_lo[b[1]]
                elif kind in ("mk", "mv"):
                    a_hi, a_lo = mT_hi, mT_lo
                else:
                    a_hi, a_lo = hT_hi, hT_lo
                if kind == "gate" and half == 0:
                    if n == BLOCK_NO[("gate", 1, 0)]:
                        pe.wait_ge(const_built, built("gate_sel"))
                        pe.wait_ge(brow_used, 2)
                    for t in range(NT):
                        nc.tensor.matmul(banks[t][:], gate_sel[:, b[1]], bias_gate[:, b[2] * W:(b[2] + 1) * W],
                                         start=True, stop=False)
                for h in range(2):
                    s = 2 * p + h
                    pe.wait_ge(lo_done, s + 1)
                    if p < 2:
                        job_read("hT", s)
                    if p == NP - 1 and h == 1:
                        for t in range(NT):
                            ts = slice(t * P, (t + 1) * P)
                            for i in range(2):
                                k = half * KB + 2 * h + i
                                wh, wl = w_hi[:, s % 4, i], w_lo[:, s % 4, i]
                                for m, (a_, w_) in enumerate(((hT_hi, wh), (hT_hi, wl), (hT_lo, wh))):
                                    ins = nc.tensor.matmul(banks[t][:], a_[:, k, ts], w_, start=False,
                                                           stop=i == 1 and m == 2)
                            ins.then_inc(half_used if t else last_tile0, 1)
                        continue
                    for i in range(2):
                        k = half * KB + 2 * h + i
                        opening = half == 0 and h == 0 and i == 0
                        closing = last and h == 1 and i == 1
                        wh, wl = w_hi[:, s % 4, i], w_lo[:, s % 4, i]
                        if kind in ("cu", "cc", "cb"):
                            for c in range(KB):
                                dst = banks[c // 2][:, (c % 2) * SEQ:(c % 2 + 1) * SEQ]
                                cs = slice(c * P, (c + 1) * P)
                                for m, (w_, a_) in enumerate(((wh, a_hi), (wh, a_lo), (wl, a_hi))):
                                    ins = nc.tensor.matmul(dst, w_[:, cs], a_[:, k],
                                                           start=opening and m == 0 and c % 2 == 0,
                                                           stop=closing and m == 2, skip_group_check=True)
                        else:
                            for t in range(NT):
                                ts = slice(t * P, (t + 1) * P)
                                for m, (a_, w_) in enumerate(((a_hi, wh), (a_hi, wl), (a_lo, wh))):
                                    ins = nc.tensor.matmul(banks[t][:], a_[:, k, ts], w_,
                                                           start=opening and m == 0 and kind != "gate",
                                                           stop=closing and m == 2)
                    ins.then_inc(half_used, 1)
                    if p == NP - 1:
                        transpose_x1(0)

            def transpose_x1(h):
                pe.wait_ge(x1_ready, 2 * h + 2)
                for g in (2 * h, 2 * h + 1):
                    pe.wait_ge(aux_free[g], len([j for j in range(len(JOBS)) if j % 4 == g]))
                    for i in range(2):
                        for t in range(NT):
                            k = 2 * g + i
                            ins = nc.tensor.transpose(aux[g][:, i * SEQ + t * P:i * SEQ + (t + 1) * P],
                                                      x1[:, t, k * P:(k + 1) * P], ident[:])
                    ins.then_inc(x1T_ready, 1)

            pe.wait_ge(const_built, built("ident"))
            for _ in range(WARM_UP):
                nc.tensor.matmul(acc[0][:, 0:P], ident[:], ident[:], start=True, stop=True)
            for t in range(NT):
                pe.wait_ge(xs_ready, t + 1)
                for g in range(4):
                    for k in (2 * g, 2 * g + 1):
                        ins = nc.tensor.transpose(aux[g][:, (k % 2) * SEQ + t * P:(k % 2) * SEQ + (t + 1) * P],
                                                  xs[:, t, k * P:(k + 1) * P], ident[:])
                    if t == NT - 1:
                        ins.then_inc(aux_ready, 1)
            for p in range(NP):
                piece(p)
                for j, kind, arg in jobs_at(p):
                    do_job(j, kind, arg)

            def logit_products(t, h):
                for k in range(4 * h, 4 * h + 4):
                    ins = nc.tensor.matmul(acc[2][:, t * NEXP:(t + 1) * NEXP], h2T[:, k, t * P:(t + 1) * P], wr[:, k],
                                           start=(k == 0 and t == 0), stop=(k == KD - 1), skip_group_check=True)
                return ins

            pe.wait_ge(x1_squared, 2)
            pe.wait_ge(h2T_act, 1)
            pe.wait_ge(h2T_dve, 1)
            pe.wait_ge(wr_loaded, 16)
            logit_products(0, 0)
            transpose_x1(1)
            logit_products(1, 0)
            pe.wait_ge(h2T_act, 2)
            pe.wait_ge(h2T_dve, 2)
            for t in range(NT):
                ins = logit_products(t, 1)
            ins.then_inc(logits_ready, 1)
            pe.wait_ge(x1_squared, 4)
            pe.wait_ge(const_built, built("tables"))
            for _ in range(KEEP_UP):
                nc.tensor.matmul(acc[0][:], zeros_bf[:, 0:P], zeros_bf[:], start=True, stop=True)
            for b in range(2):
                nc.tensor.matmul(acc[b][:], zeros_bf[:, 0:P], zeros_bf[:], start=True, stop=True).then_inc(scattered, 1)
            pe.wait_ge(chosen_ready, 1)
            hot = [chosen3[:, t, 0] for t in range(NT)]
            nc.tensor.matmul(acc[3][:, 0:NEXP], tri_strict[:], hot[0], start=True, stop=True)
            nc.tensor.matmul(acc[3][:, NEXP:2 * NEXP], ones_bf[:], hot[0], start=True, stop=False)
            nc.tensor.matmul(acc[3][:, NEXP:2 * NEXP], tri_strict[:], hot[1], start=False, stop=True
                             ).then_inc(slots_ready, 1)
            pe.wait_ge(chosen_ready, 2)
            for t in range(NT):
                ins = nc.tensor.matmul(bank_glu[0:96, 0:2],
                                       chosen3[:, t].rearrange("p a e -> p (a e)"), ones_bf[:, 0:2],
                                       start=(t == 0), stop=(t == 1))
            ins.then_inc(slots_ready, 1)
            nc.tensor.matmul(acc[2][:], zeros_bf[:, 0:P], zeros_bf[:], start=True, stop=True).then_inc(scattered, 1)

            def gather(first_item=False):
                for t in range(NT):
                    for m in range(3):
                        if first_item and t == 1 and m == 2:
                            pe.wait_ge(parts_dve, 2)
                        for k in range(KD):
                            ins = nc.tensor.matmul(bank_cy[:, k * SLOTS:(k + 1) * SLOTS],
                                                   m_parts[:, m, t, k * P:(k + 1) * P], pick[:, t],
                                                   start=(t == 0 and m == 0 and k == 0),
                                                   stop=(t == NT - 1 and m == 2), skip_group_check=True)
                ins.then_inc(gathered, 1)

            pe.wait_ge(pick_ready, 1)
            pe.wait_ge(parts_act, 4)
            pe.wait_ge(parts_pool, 2)
            gather(first_item=True)
            pe.wait_ge(table_ready, 1)
            pe.wait_ge(extra_ready, 1)
            nc.tensor.matmul(acc[3][:], zeros_bf[:, 0:P], zeros_bf[:], start=True, stop=True).then_inc(scattered, 1)

            def list_first():
                pe.wait_ge(extra_ready, 2)
                nc.tensor.matmul(bank_t[0:96, 0:2], block_tri[:], extra_bf[:], start=True, stop=True
                                 ).then_inc(first_ready, 1)

            def list_transposes():
                pe.wait_ge(list_read, 1)
                pe.wait_ge(table_ready, 2)
                for a, tab in enumerate((pos_tab, comb_tab)):
                    for t in range(NT):
                        c = (a * NT + t) * P
                        ins = nc.tensor.transpose(bank_t[0:32, c:c + P], tab[:, t, 0:NEXP], ident[:])
                ins.then_inc(list_ready, 1)

            def list_products():
                pe.wait_ge(xtab_ready, 1)
                hot_x = exp_sel[0:32, NEXP:NEXP + EXTRA_COLS]
                for t in range(NT):
                    c = t * EXTRA_COLS
                    nc.tensor.matmul(bank_t[:, c:c + EXTRA_COLS], posT[:, 0, t], hot_x, start=True, stop=False)
                    nc.tensor.matmul(bank_t[:, c:c + EXTRA_COLS], ones_f[:], xt[0:32, 2], start=False, stop=True)
                    nc.tensor.matmul(bank_t[:, SEQ + c:SEQ + c + EXTRA_COLS], posT[:, 1, t], hot_x,
                                     start=True, stop=True)
                nc.tensor.matmul(bank_t[0:1, 128:128 + EXTRA_COLS], iota_e[:, 0:1], hot_x, start=True, stop=True)
                nc.tensor.matmul(bank_t[0:1, 128 + EXTRA_COLS:128 + EXTRA_COLS + 1], ones_f[:, 0:1],
                                 extra[0:32, 0:1], start=True, stop=True).then_inc(list_ready, 1)

            def scatter(items, banks):
                pe.wait_ge(y_ready, items)
                pe.wait_ge(pick_wT_ready, items - 1)
                for b in banks:
                    t, half = b // 2, b % 2
                    s = slice(64 * half, 64 * half + 64)
                    nc.tensor.matmul(acc[b][:], pick_wT[s, t], y_sb[s, :],
                                     start=False, stop=True, skip_group_check=True).then_inc(scattered, 1)

            def item(n, places, between={}):
                first_item = bool(between)
                pe.wait_ge(xg_ready, n)
                pe.wait_ge(up_read, n)
                for k in range(KD):
                    pe.wait_ge(up_loaded[k], 16 * n)
                    for bank, c0 in ((bank_glu, 0), (bank_lin, FF)):
                        for half in range(2):
                            ins = nc.tensor.matmul(bank[64 * half:64 * half + 64, :], xgT[:, k],
                                                   places[k][:, c0 + half * W:c0 + (half + 1) * W],
                                                   start=(k == 0), stop=(k == KD - 1), skip_group_check=True)
                    ins.then_inc(up_used[k] if k < KD - 1 else up_done, 1)
                    if k == 0:
                        pe.wait_ge(bias_sel_ready, n)
                        for bank, c0 in ((bank_glu, 0), (bank_lin, FF)):
                            for half in range(2):
                                nc.tensor.matmul(bank[64 * half:64 * half + 64, :], bias_sel[:],
                                                 bias_up[:, c0 + half * W:c0 + (half + 1) * W],
                                                 start=False, stop=False, skip_group_check=True)
                    if k in between:
                        between[k]()
                    if k == (KD - 1 if first_item else KD - 2):
                        pe.wait_ge(pick_ready, n + 1)
                        pe.wait_ge(y_ready, n)
                        gather()
                if not first_item:
                    scatter(n, range(3))
                pe.wait_ge(a_ready, n)
                if first_item:
                    pe.wait_ge(meta_ready, 1)
                else:
                    pe.wait_ge(pick_wT_ready, n - 1)
                for j in range(KB):
                    ins = nc.tensor.transpose(bank_t[:, j * P:(j + 1) * P], a_tok[:, j * P:(j + 1) * P], ident[:])
                ins.then_inc(aT_done, 1)
                if not first_item:
                    scatter(n, (3,))
                pe.wait_ge(pick_w_ready, n)
                pe.wait_ge(aT_ready, n + 1)
                for t in range(NT):
                    ins = nc.tensor.transpose(bank_t[:, t * P:(t + 1) * P],
                                              pick_w[:, t].rearrange("p a s -> p (a s)"), ident[:])
                ins.then_inc(pick_wT_done, 1)
                pe.wait_ge(xg_ready, n + 1)
                for half in range(2):
                    nc.tensor.matmul(bank_cy[64 * half:64 * half + 64, :], bias_sel[:],
                                     bias_down[:, half * W:(half + 1) * W], start=True, stop=False,
                                     skip_group_check=True)
                starts = [start for start, _ in DOWN]
                for m in range(KD):
                    if m in starts:
                        pe.wait_ge(down_loaded[starts.index(m)], 16 * n)
                    j, ff_half = m % KB, m // KB
                    for half in range(2):
                        ins = nc.tensor.matmul(bank_cy[64 * half:64 * half + 64, :],
                                               aT[:, j, 64 * ff_half:64 * ff_half + 64],
                                               w_down_ring[:, m, half * W:(half + 1) * W],
                                               start=False, stop=(m == KD - 1), skip_group_check=True)
                    if m == KD - 1:
                        ins.then_inc(y_done, 1)
                    elif m + 1 in starts:
                        ins.then_inc(down_used[starts.index(m + 1) - 1], 1)
            item(1, w_up_ring, {1: list_first, 3: list_transposes, 5: list_products})

            with pe.Fori(2, AHEAD, 2) as i:
                item(i, w_up_next)
                item(i + 1, w_up_ring)
            item(AHEAD, w_up_next)
            with pe.Fori(AHEAD + 1, NEXP + 1) as n:
                item(n, w_up_ring)
            more = pe.value_load(meta[0:1, EXTRA_COLS:EXTRA_COLS + 1], min_val=0, max_val=EXTRA)
            with pe.If(more > 0):
                with pe.Fori(NEXP + 1, NEXP + 1 + more) as n:
                    item(n, w_up_ring)
            scatter(more + (NEXP + 1), range(4))


def kernel(**inputs):
    import numpy as np
    import concourse.bacc as bacc
    from concourse.bass_utils import run_bass_kernel_spmd

    a = {name: np.ascontiguousarray(value) for name, value in inputs.items()}
    cols = np.zeros((P, NCOLS), np.float32)
    for c, name in ((C_G1, "norm1_g"), (C_GM, "mem_norm_g"), (C_G2, "norm2_g")):
        cols[:, c:c + KD] = a[name][0].reshape(KD, P).T
    for j in range(3):
        cols[:, C_CONV + j * KB:C_CONV + (j + 1) * KB] = a["conv_w"][0, j].reshape(KB, P).T
    cols[:, C_XQ], cols[:, C_XK] = a["xa_q_g"][0], a["xa_k_g"][0]
    cols[:FOX_H, C_BF] = a["b_forget"][0]
    cols[:FOX_D, C_FQ], cols[:FOX_D, C_FK] = a["fox_q_g"][0], a["fox_k_g"][0]
    spread = np.ascontiguousarray(np.broadcast_to(a["b_router"][0][None, :], (P, NEXP)))

    def by_row(w):
        return np.ascontiguousarray(w.reshape(KD, P, -1).transpose(1, 0, 2))

    arrays = {
        "x": a["x"][0], "mem": a["mem"][0], "w_in": a["w_in"][0], "w_kv": a["w_mem_kv"][0],
        "w_branch": a["w_branch"][0], "w_out": a["w_out"][0], "w_up": a["w_up"][0], "w_down": a["w_down"][0],
        "cols": cols, "spread": spread, "wf": by_row(a["w_in"][0][:, 3 * W:3 * W + FOX_H]),
        "wr": by_row(a["w_router"][0]), "b_gate": a["b_gate"][0], "b_up": a["b_up"][0], "b_down": a["b_down"][0],
    }
    nc = bacc.Bacc("TRN2", target_bir_lowering=False, num_devices=1)
    args = [nc.dram_tensor(f"{name}_dram", v.shape, mybir.dt.from_np(v.dtype), kind="ExternalInput").ap()
            for name, v in arrays.items()]
    args.append(nc.dram_tensor("out_dram", (SEQ, D), F32, kind="ExternalOutput").ap())
    hybrid_block(nc, *args)
    got = run_bass_kernel_spmd(nc, [{f"{name}_dram": v for name, v in arrays.items()}], core_ids=[0])
    return got.results[0]["out_dram"].reshape(1, SEQ, D)
```
